# Optimizing a Trainium2 kernel written in Bass

```python
import jax, jax.numpy as jnp
from jax import lax
import numpy as np

D_MODEL = 1024
BATCH = 1
SEQ = 256
DEPTH = 1

MEM_LEN = 256
EPS = 1e-5
NEG = -1e30

RET_HEADS = 4
RET_DK = 64
RET_DV = 128
RET_CHUNK = 128
MOBA_HEADS = 8
MOBA_HD = 64
MOBA_BLOCK = 256
MOBA_TOPK = 3
MOBA_QCHUNK = 32
MEM_HEADS = 4
MEM_HD = 128
N_BRANCH = 3
N_EXPERTS = 32
TOP_K = 4
D_FF = D_MODEL
SWIGLU_LIMIT = 7.0
SWIGLU_ALPHA = 1.702
MOE_BLOCK = 256

RET_Q = RET_HEADS * RET_DK
RET_V = RET_HEADS * RET_DV
MOBA_W = MOBA_HEADS * MOBA_HD
MEM_W = MEM_HEADS * MEM_HD
IN_SPLITS = (RET_Q, RET_Q, RET_V, RET_V, MOBA_W, MOBA_W, MOBA_W, MEM_W, N_BRANCH * D_MODEL)
D_IN = sum(IN_SPLITS)
SPLIT_POINTS = tuple(int(v) for v in np.cumsum(IN_SPLITS)[:-1])

kernel_name = "hybrid_retention_moba_memory_moe"

def rms_norm(x, g):
    xf = x.astype(jnp.float32)
    y = xf * lax.rsqrt(jnp.mean(xf * xf, axis=-1, keepdims=True) + EPS)
    return (y * g.astype(jnp.float32)).astype(x.dtype)

def retention(q, k, v):
    B, S, H, dk = q.shape
    dv = v.shape[-1]
    C = RET_CHUNK
    nc = S // C
    log_g = jnp.log1p(-jnp.exp2(-5.0 - jnp.arange(H, dtype=jnp.float32)))
    i = jnp.arange(C, dtype=jnp.float32)
    diff = i[:, None] - i[None, :]
    decay_in = jnp.where(diff >= 0, jnp.exp(jnp.maximum(diff, 0.0)[None] * log_g[:, None, None]), 0.0).astype(q.dtype)
    decay_k = jnp.exp((C - 1 - i)[:, None] * log_g[None, :]).astype(q.dtype)
    decay_q = jnp.exp((i + 1)[:, None] * log_g[None, :]).astype(q.dtype)
    decay_chunk = jnp.exp(C * log_g).astype(v.dtype)
    qc = q.reshape(B, nc, C, H, dk)
    kc = k.reshape(B, nc, C, H, dk)
    vc = v.reshape(B, nc, C, H, dv)
    scores = jnp.einsum("bnihd,bnjhd->bnhij", qc, kc) * decay_in
    intra = jnp.einsum("bnhij,bnjhe->bnihe", scores, vc)
    upd = jnp.einsum("bnjhd,bnjhe->nbhde", kc * decay_k[:, :, None], vc)

    def step(state, u):
        return decay_chunk[None, :, None, None] * state + u, state

    _, prev = lax.scan(step, jnp.zeros((B, H, dk, dv), v.dtype), upd)
    cross = jnp.einsum("bnihd,nbhde->bnihe", qc * decay_q[:, :, None], prev)
    return (intra + cross).reshape(B, S, H, dv)

def moba_attention(q, k, v):
    B, H, S, d = q.shape
    BS = MOBA_BLOCK
    QC = MOBA_QCHUNK
    nb = -(-S // BS)
    n_sel = min(MOBA_TOPK, nb)
    pad = ((0, 0), (0, 0), (0, nb * BS - S), (0, 0))
    kb = jnp.pad(k, pad).reshape(B, H, nb, BS, d)
    vb = jnp.pad(v, pad).reshape(B, H, nb, BS, d)
    k_mean = jnp.mean(kb.astype(jnp.float32), axis=3)
    q_blk = jnp.arange(S) // BS
    gate = jnp.einsum("bhsd,bhnd->bhsn", q.astype(jnp.float32), k_mean)
    past = jnp.arange(nb)[None, :] < q_blk[:, None]
    gate = jnp.where(past, gate, -jnp.inf)
    _, idx = lax.top_k(gate, n_sel)
    valid = idx < q_blk[:, None]
    slopes = jnp.exp2(-8.0 * (jnp.arange(H, dtype=jnp.float32) + 1.0) / H)
    scale = d ** -0.5
    nq = S // QC
    q_ch = q.reshape(B, H, nq, QC, d).transpose(2, 0, 1, 3, 4)
    idx_ch = idx.reshape(B, H, nq, QC, n_sel).transpose(2, 0, 1, 3, 4)
    valid_ch = valid.reshape(B, H, nq, QC, n_sel).transpose(2, 0, 1, 3, 4)
    starts = jnp.arange(nq, dtype=jnp.int32) * QC
    bi = jnp.arange(B)[:, None, None, None]
    hi = jnp.arange(H)[None, :, None, None]
    kpos = jnp.arange(BS)

    def chunk(args):
        qc, idc, vld, start = args
        t = start + jnp.arange(QC)
        bid = start // BS
        k_own = lax.dynamic_index_in_dim(kb, bid, axis=2, keepdims=False)
        v_own = lax.dynamic_index_in_dim(vb, bid, axis=2, keepdims=False)
        dist_own = (t[:, None] - (bid * BS + kpos)[None, :]).astype(jnp.float32)
        sc_own = jnp.einsum("bhqd,bhkd->bhqk", qc, k_own).astype(jnp.float32) * scale - slopes[:, None, None] * dist_own
        sc_own = jnp.where(dist_own >= 0, sc_own, NEG)
        k_sel = kb[bi, hi, idc]
        v_sel = vb[bi, hi, idc]
        dist_sel = (t[None, None, :, None, None] - (idc[..., None] * BS + kpos)).astype(jnp.float32)
        sc_sel = jnp.einsum("bhqd,bhqjkd->bhqjk", qc, k_sel).astype(jnp.float32) * scale - slopes[None, :, None, None, None] * dist_sel
        sc_sel = jnp.where(vld[..., None], sc_sel, NEG)
        sc = jnp.concatenate([sc_own, sc_sel.reshape(B, H, QC, n_sel * BS)], axis=-1)
        p = jax.nn.softmax(sc, axis=-1).astype(v.dtype)
        p_own = p[..., :BS]
        p_sel = p[..., BS:].reshape(B, H, QC, n_sel, BS)
        return jnp.einsum("bhqk,bhkd->bhqd", p_own, v_own) + jnp.einsum("bhqjk,bhqjkd->bhqd", p_sel, v_sel)

    out = lax.map(chunk, (q_ch, idx_ch, valid_ch, starts))
    return out.transpose(1, 0, 3, 2, 4).reshape(B, S, H * d)

def hybrid_mixer(x, mem, g_mix, w_in, b_gate, g_ret_out, g_moba_q, g_moba_k, g_mem, w_mem_kv, g_mem_q, g_mem_k, w_br_ret, w_br_moba, w_br_mem, w_out):
    B, S, D = x.shape
    h = rms_norm(x, g_mix)
    rq, rk, rv, rg, mq, mk, mv, cq, gl = jnp.split(h @ w_in, SPLIT_POINTS, axis=-1)
    o_ret = retention(rq.reshape(B, S, RET_HEADS, RET_DK), rk.reshape(B, S, RET_HEADS, RET_DK) * (RET_DK ** -0.5), rv.reshape(B, S, RET_HEADS, RET_DV))
    o_ret = (rms_norm(o_ret, g_ret_out) * jax.nn.silu(rg.reshape(B, S, RET_HEADS, RET_DV))).reshape(B, S, RET_V)
    qm = rms_norm(mq.reshape(B, S, MOBA_HEADS, MOBA_HD), g_moba_q).transpose(0, 2, 1, 3)
    km = rms_norm(mk.reshape(B, S, MOBA_HEADS, MOBA_HD), g_moba_k).transpose(0, 2, 1, 3)
    vm = mv.reshape(B, S, MOBA_HEADS, MOBA_HD).transpose(0, 2, 1, 3)
    o_moba = moba_attention(qm, km, vm)
    M = mem.shape[1]
    mk_, mv_ = jnp.split(rms_norm(mem, g_mem) @ w_mem_kv, 2, axis=-1)
    qc = rms_norm(cq.reshape(B, S, MEM_HEADS, MEM_HD), g_mem_q)
    kc = rms_norm(mk_.reshape(B, M, MEM_HEADS, MEM_HD), g_mem_k)
    vc = mv_.reshape(B, M, MEM_HEADS, MEM_HD)
    sc = jnp.einsum("bshd,bmhd->bhsm", qc, kc).astype(jnp.float32) * (MEM_HD ** -0.5)
    p = jax.nn.softmax(sc, axis=-1).astype(vc.dtype)
    o_mem = jnp.einsum("bhsm,bmhd->bshd", p, vc).reshape(B, S, MEM_W)
    gates = jax.nn.sigmoid((gl + b_gate).astype(jnp.float32)).astype(x.dtype).reshape(B, S, N_BRANCH, D)
    y = gates[:, :, 0] * (o_ret @ w_br_ret) + gates[:, :, 1] * (o_moba @ w_br_moba) + gates[:, :, 2] * (o_mem @ w_br_mem)
    return x + y @ w_out

def moe_ffn(x, g_ffn, w_router, b_router, w_mlp1, b_mlp1, w_mlp2, b_mlp2):
    B, S, D = x.shape
    N = B * S
    xt = rms_norm(x, g_ffn).reshape(N, D)
    logits = (xt @ w_router + b_router).astype(jnp.float32)
    top_v, top_e = lax.top_k(logits, TOP_K)
    wts = jax.nn.softmax(top_v, axis=-1).astype(x.dtype)
    P = N * TOP_K
    T = MOE_BLOCK
    e_flat = top_e.reshape(P)
    tok_flat = jnp.arange(P, dtype=jnp.int32) // TOP_K
    w_flat = wts.reshape(P)
    order = jnp.argsort(e_flat)
    e_sorted = e_flat[order]
    tok_sorted = tok_flat[order]
    w_sorted = w_flat[order]
    counts = jnp.bincount(e_flat, length=N_EXPERTS)
    starts = jnp.cumsum(counts) - counts
    padded = ((counts + T - 1) // T) * T
    pad_ends = jnp.cumsum(padded)
    pad_starts = pad_ends - padded
    dest = pad_starts[e_sorted] + (jnp.arange(P) - starts[e_sorted])
    NB = -(-P // T) + N_EXPERTS
    R = NB * T
    slot_tok = jnp.full((R,), N, dtype=jnp.int32).at[dest].set(tok_sorted)
    slot_w = jnp.zeros((R,), x.dtype).at[dest].set(w_sorted)
    block_e = jnp.minimum(jnp.searchsorted(pad_ends, jnp.arange(NB) * T, side="right"), N_EXPERTS - 1)
    x_pad = jnp.concatenate([xt, jnp.zeros((1, D), xt.dtype)], axis=0)
    xb = x_pad[slot_tok].reshape(NB, T, D)

    def expert_block(args):
        xblk, e = args
        hdn = xblk @ w_mlp1[e] + b_mlp1[e]
        x_glu = jnp.minimum(hdn[:, ::2], SWIGLU_LIMIT)
        x_lin = jnp.clip(hdn[:, 1::2], -SWIGLU_LIMIT, SWIGLU_LIMIT)
        act = x_glu * jax.nn.sigmoid(SWIGLU_ALPHA * x_glu) * (x_lin + 1.0)
        return act @ w_mlp2[e] + b_mlp2[e]

    yb = lax.map(expert_block, (xb, block_e)).reshape(R, D) * slot_w[:, None]
    y = jnp.zeros((N + 1, D), x.dtype).at[slot_tok].add(yb)[:N]
    return x + y.reshape(B, S, D)

def setup_inputs(seed: int = 0) -> dict:
    key = jax.random.key(seed)
    ks = jax.random.split(key, 24)
    f32 = jnp.float32

    def nrm(k, shape, fan_in):
        return jax.random.normal(k, shape, f32) * (fan_in ** -0.5)

    def gain(k, shape):
        return 1.0 + 0.02 * jax.random.normal(k, shape, f32)

    L = DEPTH
    return {
        "x": jax.random.normal(ks[0], (BATCH, SEQ, D_MODEL), f32),
        "mem": jax.random.normal(ks[1], (BATCH, MEM_LEN, D_MODEL), f32),
        "g_mix": gain(ks[2], (L, D_MODEL)),
        "w_in": nrm(ks[3], (L, D_MODEL, D_IN), D_MODEL),
        "b_gate": 0.01 * jax.random.normal(ks[4], (L, N_BRANCH * D_MODEL), f32),
        "g_ret_out": gain(ks[5], (L, RET_DV)),
        "g_moba_q": gain(ks[6], (L, MOBA_HD)),
        "g_moba_k": gain(ks[7], (L, MOBA_HD)),
        "g_mem": gain(ks[8], (L, D_MODEL)),
        "w_mem_kv": nrm(ks[9], (L, D_MODEL, 2 * MEM_W), D_MODEL),
        "g_mem_q": gain(ks[10], (L, MEM_HD)),
        "g_mem_k": gain(ks[11], (L, MEM_HD)),
        "w_br_ret": nrm(ks[12], (L, RET_V, D_MODEL), RET_V),
        "w_br_moba": nrm(ks[13], (L, MOBA_W, D_MODEL), MOBA_W),
        "w_br_mem": nrm(ks[14], (L, MEM_W, D_MODEL), MEM_W),
        "w_out": nrm(ks[15], (L, D_MODEL, D_MODEL), D_MODEL),
        "g_ffn": gain(ks[16], (L, D_MODEL)),
        "w_router": nrm(ks[17], (L, D_MODEL, N_EXPERTS), D_MODEL),
        "b_router": 0.01 * jax.random.normal(ks[18], (L, N_EXPERTS), f32),
        "w_mlp1": nrm(ks[19], (L, N_EXPERTS, D_MODEL, 2 * D_FF), D_MODEL),
        "b_mlp1": 0.01 * jax.random.normal(ks[20], (L, N_EXPERTS, 2 * D_FF), f32),
        "w_mlp2": nrm(ks[21], (L, N_EXPERTS, D_FF, D_MODEL), D_FF),
        "b_mlp2": 0.01 * jax.random.normal(ks[22], (L, N_EXPERTS, D_MODEL), f32),
    }

def reference(x, mem, g_mix, w_in, b_gate, g_ret_out, g_moba_q, g_moba_k, g_mem, w_mem_kv, g_mem_q, g_mem_k, w_br_ret, w_br_moba, w_br_mem, w_out, g_ffn, w_router, b_router, w_mlp1, b_mlp1, w_mlp2, b_mlp2):
    for l in range(DEPTH):
        x = hybrid_mixer(x, mem, g_mix[l], w_in[l], b_gate[l], g_ret_out[l], g_moba_q[l], g_moba_k[l], g_mem[l], w_mem_kv[l], g_mem_q[l], g_mem_k[l], w_br_ret[l], w_br_moba[l], w_br_mem[l], w_out[l])
        x = moe_ffn(x, g_ffn[l], w_router[l], b_router[l], w_mlp1[l], b_mlp1[l], w_mlp2[l], b_mlp2[l])
    return x


_drawn_inputs = setup_inputs


def setup_inputs(seed=0):
    import zlib

    import numpy as np

    out = dict(_drawn_inputs(seed))
    spreads = {}
    factors = {'b_gate': 3.87,
     'g_moba_q': 11.473,
     'g_moba_k': 2.851,
     'g_mem': 4.56,
     'g_mem_q': 2.995,
     'g_mem_k': 2.812,
     'b_mlp1': 21.599,
     'b_mlp2': 24.789,
     'g_ret_out': 5.028,
     'b_router': 3.814,
     'g_ffn': 2.829}
    for name, (base, spread) in spreads.items():
        noise = np.random.default_rng([zlib.crc32(name.encode()), seed]).standard_normal(out[name].shape)
        drawn = base * np.exp(spread * noise) if base else spread * noise
        out[name] = __import__('jax').numpy.asarray(drawn.astype(out[name].dtype))
    for name, factor in factors.items():
        out[name] = (out[name] * factor).astype(out[name].dtype)
    return out
```

```python
import concourse.bass as bass
from concourse import mybir
from contextlib import ExitStack

F32 = mybir.dt.float32
F32R = mybir.dt.float32r
I32 = mybir.dt.int32
U32 = mybir.dt.uint32
ALU = mybir.AluOpType
ACT = mybir.ActivationFunctionType
AX = mybir.AxisListType

P = 128
S = 256
TT = S // P
D = 1024
KC = D // P
EPS = 1e-5
RET_H, RET_DK, RET_DV = 4, 64, 128
MOBA_H, MOBA_HD = 8, 64
MEM_H, MEM_HD = 4, 128
NE = 32
TOPK = 4
FF2 = 2 * D
LIMIT, ALPHA = 7.0, 1.702
SL = 64
MISC = 4 * P + 128
MAX_ITEMS = NE + (S * TOPK) // SL
G_COLS = 512

GROUPS = [("rqk", KC), ("mq", KC), ("mk", KC), ("cq", KC), ("ck", KC), ("rv", KC), ("mv", KC), ("cv", KC), ("rg", KC)]
GROUPS += [(f"gate{i}", KC) for i in range(6)]
BRANCH_ORDER = [(n, br) for n in range(2) for br in ("moba", "mem", "ret")]
GROUPS += [(f"br_{br}{n}", 4) for n, br in BRANCH_ORDER]
GROUPS += [(f"out{n}", KC) for n in range(2)]
GI = {name: i for i, (name, _) in enumerate(GROUPS)}
W_IN_COL = {"rqk": 0, "rv": 512, "rg": 1024, "mq": 1536, "mk": 2048, "mv": 2560, "cq": 3072,
            **{f"gate{i}": 3584 + 512 * i for i in range(6)}}
UNITS = [(g, hk) for g, (_, kc) in enumerate(GROUPS) for hk in range(kc // 4)]
N_MIX = len(UNITS)
UNITS_DONE = [sum(1 for (gg, _) in UNITS if gg <= g) for g in range(len(GROUPS))]

RING = 6
W1U, W2U = 8, 4
IU = W1U + W2U
NATIVE = {1, 4, 9}
HL = 3
SPLIT = [u for u in range(IU) if u not in NATIVE]
assert len(SPLIT) % HL == 0 and IU % RING == 0
W2_SPLIT = [u for u in SPLIT if u >= W1U]
W2_NATIVE = [u for u in NATIVE if u >= W1U]

Q_GROUPS = ["rqk", "mq", "mk", "cq", "ck"]
HEADS = [("moba", h) for h in range(MOBA_H)] + [("mem", h) for h in range(MEM_H)]
NH = len(HEADS)
SLOTS = ["mv", "cv", "rg"] + [f"gate{i}" for i in range(6)]


def schedule():
    steps = [("task", "hT", 0, t, kk) for t in range(TT) for kk in range(2)]
    steps += [("group", "rqk")]
    steps += [("task", "hT", 1, t, kk) for t in range(TT) for kk in range(2)]
    steps += [("group", "mq")] + [("task", "qT", "rqk", t) for t in range(TT)]
    steps += [("group", "mk")] + [("task", "qT", "mq", t) for t in range(TT)] + [("task", "ret_s", 0), ("task", "ret_s", 1)]
    steps += [("group", "cq")] + [("task", "qT", "mk", t) for t in range(TT)]
    steps += [("group", "ck")] + [("task", "qT", "cq", t) for t in range(TT)]
    steps += [("group", "rv")] + [("task", "qT", "ck", t) for t in range(TT)]
    steps += [("task", "ret_o", 0), ("task", "ret_s", 2), ("task", "ret_s", 3)]
    for s, g in enumerate(SLOTS):
        steps += [("group", g)]
        if g == "mv":
            steps += [("task", "ret_o", 1)]
        for a in (2 * s - 4, 2 * s - 3):
            if 0 <= a < NH:
                steps += [("task", "pv", a)]
        for a in (2 * s - 2, 2 * s - 1):
            if 0 <= a < NH:
                steps += [("task", "pT", a)]
        for a in (2 * s, 2 * s + 1):
            if a < NH:
                steps += [("task", "sc", a)]
        if g == "gate3":
            steps += [("task", "oT", "moba", t) for t in range(TT)]
        if g == "gate4":
            steps += [("task", "oT", "ret", t) for t in range(TT)]
        if g == "gate5":
            steps += [("task", "oT", "mem", t) for t in range(TT)]
    for i, (n, br) in enumerate(BRANCH_ORDER):
        steps += [("group", f"br_{br}{n}")]
        if i == 4:
            steps += [("task", "yT", 0, t) for t in range(TT)]
    steps += [("task", "yT", 1, t) for t in range(TT)]
    steps += [("group", "out0"), ("group", "out1")]
    steps += [("task", "xT", t, kk) for t in range(TT) for kk in range(2)]
    steps += [("task", "logits")]
    steps += [("task", "pos"), ("task", "cnt"), ("task", "tabT"), ("task", "off"), ("task", "tab")]
    steps += [("task", "b2", t, n) for t in range(TT) for n in range(2)]
    return steps


NORMS = ["x", "mem", "mq", "mk", "cq", "ck", "ret0", "ret1", "x2"]
SQUARES = [2, 2, 1, 1, 1, 1, 1, 1, 2]
SUMS = [0, 0, 1, 1, 1, 1, 1, 1, 0]
ROUTE = ["max0", "max1", "mi0", "mi1", "nv", "if", "oh0", "oh1", "m0", "m1", "rse", "w4", "ow0", "ow1", "g0", "g1",
         "posm", "g3", "n", "off", "offr", "s1", "s2", "s3", "t1", "t2", "u1", "u2", "u3", "si", "sz",
         "posi", "gi", "bsel"]
RI = {n: i + 1 for i, n in enumerate(ROUTE)}
STEPS = schedule()
TASKS = {s[1:]: n for n, s in enumerate([s for s in STEPS if s[0] == "task"])}
N_TASKS = len(TASKS)


def host_constants():
    import numpy as np
    i = np.arange(P, dtype=np.float64)[:, None]
    t = np.arange(S, dtype=np.float64)[None, :]
    diff = t - i
    decay = np.zeros((P, RET_H, 384))
    for h in range(RET_H):
        lg = np.log1p(-np.exp2(-5.0 - h))
        d = np.where(diff >= 0, np.exp(np.maximum(diff, 0) * lg), 0.0) * RET_DK ** -0.5
        decay[:, h, 0:S] = d
        decay[:, h, S:384] = d[:, 0:P]
    alibi = np.zeros((P, TT, S))
    for tt in range(TT):
        dist = (i + P * tt) - t
        alibi[:, tt, :] = np.where(dist >= 0, -dist, -1e33)
    misc = np.zeros((P, MISC))
    misc[:, 0:P] = np.eye(P)
    misc[:, P:2 * P] = (i < i.T)
    misc[:, 2 * P:3 * P] = 1.0
    misc[:, 3 * P:4 * P] = np.arange(P)[None, :] % SL
    misc[:, 4 * P:4 * P + 32] = np.arange(32)[None, :]
    misc[:, 4 * P + 32] = i[:, 0]
    misc[:, 4 * P + 33:4 * P + 36] = [SL, 2 * SL, 3 * SL]
    misc[:, 4 * P + 36] = EPS
    misc[0:NE, 4 * P + 64:4 * P + 128] = np.concatenate([np.eye(NE), np.eye(NE)], 1)
    f = np.float32
    return decay.reshape(P, -1).astype(f), alibi.reshape(P, -1).astype(f), misc.astype(f)


def build(nc, a, out):
    ctx = ExitStack()
    with ctx:
        def sem(name):
            return ctx.enter_context(nc.semaphore(name))

        def sb(name, shape, dt=F32, scope=ctx):
            return scope.enter_context(nc.sbuf_tensor(name, shape, dt))

        raw = [sb(f"raw{i}", [P, 2048]) for i in range(RING)]
        X = sb("X", [P, TT, D])
        hT = sb("hT", [P, KC, S])
        hx = sb("hx", [P, TT, D])
        mT = sb("mT", [P, KC, S])
        misc = sb("misc", [P, MISC])
        ident, before, ones, slotn = (misc[:, i * P:(i + 1) * P] for i in range(4))
        iota32 = misc[:, 4 * P:4 * P + 32]
        iotap = misc[:, 4 * P + 32:4 * P + 33]
        thresholds = misc[:, 4 * P + 33:4 * P + 36]
        eps = misc[:, 4 * P + 36:4 * P + 37]
        twice = misc[0:NE, 4 * P + 64:4 * P + 128]
        gffn = sb("gffn", [P, D])
        wr = sb("wr", [P, KC, NE])
        brt = sb("brt", [P, NE])
        gains = sb("gains", [P, 2 * KC + 5])
        gcol = gains[:, 0:2 * KC]
        qgain = gains[:, 2 * KC:]
        stat = sb("stat", [P, 3, 16 * len(NORMS)])
        smx = sb("smx", [P, 4, 2 * NH])
        lg = sb("lg", [P, TT, NE])
        v8 = sb("v8", [P, TT, 8])
        i8 = sb("i8", [P, TT, 8], U32)
        i8f = sb("i8f", [P, TT, 8])
        nv = sb("nv", [P, TT])
        e4 = sb("e4", [P, TT, 4])
        se = sb("se", [P, 2 * TT])
        oh = sb("oh", [P, TT, 4, NE])
        ohw = sb("ohw", [P, TT, 4, NE])
        MG = sb("MG", [P, 2, TT, NE])
        posm = sb("posm", [P, TT, NE])
        rt = sb("rt", [NE, 96])
        selw = sb("selw", [NE, 2, MAX_ITEMS])
        tabT = sb("tabT", [NE, 2, S])
        posi = sb("posi", [P, TT, MAX_ITEMS])
        gi = sb("gi", [P, TT, MAX_ITEMS])
        bsel = sb("bsel", [64, MAX_ITEMS])
        items = sb("items", [1, MAX_ITEMS + 2], I32)

        mix = ExitStack()
        mem = sb("mem", [P, TT, D], scope=mix)
        V = {g: sb(f"V_{g}", [P, TT, 512], scope=mix) for g in ("rv", "mv", "cv", "rg")}
        gates = sb("gates", [P, TT, 3 * D], scope=mix)
        bg = sb("bg", [P, 3 * D], scope=mix)
        tq = [sb(f"tq{i}", [P, TT, 512], scope=mix) for i in range(2)]
        qT = {g: sb(f"qT_{g}", [P, 4, S], scope=mix) for g in Q_GROUPS}
        PT = [sb(f"PT{i}", [P, 512], scope=mix) for i in range(4)]
        o = {br: sb(f"o_{br}", [P, TT, 512], scope=mix) for br in ("ret", "moba", "mem")}
        alibi = sb("alibi", [P, TT * S], scope=mix)
        mix.close()
        probs = [hx[:, i // 2, (i % 2) * 512:(i % 2) * 512 + 512] for i in range(4)]
        decay = gates[:, 1, 3 * D - RET_H * 384:3 * D]
        retS = [PT[i][:, 0:384] for i in range(2)]
        sq = gates[:, 0, 0:D]
        rgs = mem[:, 1, :].rearrange("p (t n) -> p t n", t=TT)
        tmp = V["rv"]
        oT = {"ret": tq[0][:, :, :].rearrange("p a (b s) -> p (a b) s", s=S),
              "moba": tq[1][:, :, :].rearrange("p a (b s) -> p (a b) s", s=S),
              "mem": mem[:, 0, :].rearrange("p (c s) -> p c s", s=S)}
        y = hx
        b2s = V["mv"][0:NE, :, :].rearrange("p t n -> p (t n)")

        hi = [sb(f"hi{i}", [P, 2048], F32R) for i in range(HL)]
        lo = [sb(f"lo{i}", [P, 2048], F32R) for i in range(HL)]
        xth = sb("xth", [P, TT, D], F32R)
        xtl = sb("xtl", [P, TT, D], F32R)
        XG = sb("XG", [P, KC, 2 * SL], F32R)
        AT = sb("AT", [P, KC, 2, SL], F32R)
        YH = sb("YH", [P, D], F32R)
        YL = sb("YL", [P, D], F32R)
        SG = sb("SG", [P, TT, 2 * SL], F32R)
        SS = sb("SS", [P, TT, 2 * SL], F32R)
        ST = sb("ST", [P, S], F32R)
        b1s = sb("b1s", [P, FF2], F32R)
        BL = sb("BL", [P, 2 * SL], F32R)
        slotw = sb("slotw", [P, 1])
        b1raw = hT[0:64, :, :].rearrange("p k s -> p (k s)")
        HB = mT[:, 0:4, :].rearrange("p k s -> p (k s)")
        HS = mT[:, 4:8, :].rearrange("p k s -> p (k s)")
        hview = hT[:, :, :].rearrange("p k s -> p (k s)")
        glu, lin, sig, act_t = (hview[:, i * 512:(i + 1) * 512] for i in range(4))

        PS = ctx.enter_context(nc.psum_tensor("PS", [P, 4096], F32))
        banks = [PS[:, i * 512:(i + 1) * 512] for i in range(8)]
        pair = [PS[:, i * 1024:(i + 1) * 1024].rearrange("p (t n) -> p t n", t=TT) for i in range(2)]

        def bank(key):
            return banks[4 + TASKS[key] % 4]

        raw_in = [sem(f"raw_in{i}") for i in range(RING)]
        x_in, mem_in, const_in, bcast_in, b1_in, b2_in = (sem(n) for n in ("x_in", "mem_in", "const_in", "bcast_in", "b1_in", "b2_in"))
        unit_used = sem("unit_used")
        task_done = sem("task_done")
        pair_free = [sem(f"pair_free{i}") for i in range(2)]
        bank_read = [sem(f"bank_read{i}") for i in range(4)]
        sq_done, sd_done = sem("sq_done"), sem("sd_done")
        rs_done = sem("rs_done")
        ss_done = sem("ss_done")
        hx_done = sem("hx_done")
        max_done = sem("max_done")
        exp_done = sem("exp_done")
        rcp_done = sem("rcp_done")
        sig_done = sem("sig_done")
        y_done = sem("y_done")
        silu_done = sem("silu_done")
        xt_done = sem("xt_done")
        xh_done, xl_done = sem("xh_done"), sem("xl_done")
        rout = sem("rout")
        rexp = sem("rexp")
        b1h, b1l = sem("b1h"), sem("b1l")
        zeroed = sem("zeroed")
        hi_done, lo_done = sem("hi_done"), sem("lo_done")
        hl_used = sem("hl_used")
        nat_used = sem("nat_used")
        sg_done = sem("sg_done")
        ss_mat = sem("ss_mat")
        st_pe, st_act, slw = sem("st_pe"), sem("st_act"), sem("slw")
        ga_pe, xgh, xgl = sem("ga_pe"), sem("xgh"), sem("xgl")
        hb_act = sem("hb_act")
        swi = sem("swi")
        sgm = sem("sgm")
        tr_pe, ath, atl = sem("tr_pe"), sem("ath"), sem("atl")
        yh, yl = sem("yh"), sem("yl")
        sc_pe, sc_add = sem("sc_pe"), sem("sc_add")
        out_dma = sem("out_dma")

        N_CONST, N_BCAST = 4, 4

        def sigmoid_gate(act, i):
            act.wait_ge(pair_sem(f"gate{i}"), GI[f"gate{i}"] // 2 + 1)
            act.activation(gates[:, :, 512 * i:512 * i + 512], gates[:, :, 512 * i:512 * i + 512], ACT.Sigmoid).then_inc(sig_done, 1)

        def raw_at(j, u):
            if isinstance(j, int) and j == 0:
                return (N_MIX + u) % RING, (N_MIX + u) // RING + 1
            n = N_MIX + W1U - IU + u
            return n % RING, j * (IU // RING) + (n // RING + 1)

        def split_count(j, u):
            upto = sum(1 for x in SPLIT if x <= u)
            return upto if isinstance(j, int) and j == 0 else j * len(SPLIT) + (upto - len(W2_SPLIT))

        def native_count(j, u):
            upto = sum(1 for x in NATIVE if x <= u)
            return upto if isinstance(j, int) and j == 0 else j * len(NATIVE) + (upto - len(W2_NATIVE))

        def hl_slot(j, u):
            k = SPLIT.index(u)
            return k % HL if isinstance(j, int) and j == 0 else (k - len(W2_SPLIT)) % HL

        def unit_done(eng, j, u):
            if u in NATIVE:
                eng.wait_ge(nat_used, native_count(j, u))
            else:
                eng.wait_ge(hl_used, split_count(j, u))

        def in_sbuf(eng, key):
            n = TASKS[key]
            eng.wait_ge(bank_read[n % 4], n // 4 + 1)

        def read_sem(key):
            return bank_read[TASKS[key] % 4]

        def pair_sem(g):
            return pair_free[GI[g] % 2]

        def number_of_items(eng):
            in_sbuf(eng, ("off",))
            return eng.value_load(items[0:1, MAX_ITEMS:MAX_ITEMS + 1], min_val=0, max_val=MAX_ITEMS - NE - 1) + NE

        block = ctx.enter_context(nc.Block())

        @block.sync
        def _(sp):
            sp.dma_start(X[:, :, :], a["x"].rearrange("o (t p) d -> p (o t) d", p=P)).then_inc(x_in, 16)

            def mixer_source(g, hk):
                name = GROUPS[g][0]
                if name in W_IN_COL:
                    w, c = a["w_in"][0], W_IN_COL[name]
                elif name in ("ck", "cv"):
                    w, c = a["w_mem_kv"][0], 512 * (name == "cv")
                elif name.startswith("br_"):
                    w, c = a[{"ret": "w_br_ret", "moba": "w_br_moba", "mem": "w_br_mem"}[name[3:-1]]][0], 512 * int(name[-1])
                else:
                    w, c = a["w_out"][0], 512 * int(name[-1])
                return w[512 * hk:512 * hk + 512, c:c + 512].rearrange("(k p) n -> p k n", p=P)

            for m, (g, hk) in enumerate(UNITS):
                if m >= RING:
                    sp.wait_ge(unit_used, m - RING + 1)
                sp.dma_start(raw[m % RING][:, :].rearrange("p (k n) -> p k n", k=4),
                             mixer_source(g, hk)).then_inc(raw_in[m % RING], 16)
                if m == 2:
                    sp.dma_start(mem[:, :, :], a["mem"].rearrange("o (t p) d -> p (o t) d", p=P)).then_inc(mem_in, 16)

            def slot_free(j, u):
                if isinstance(j, int) and j == 0 and u < RING:
                    sp.wait_ge(unit_used, N_MIX - RING + u + 1)
                    return
                if isinstance(j, int) and j == 1 and u < RING:
                    pj, pu = 0, W1U - RING + u
                elif u >= RING:
                    pj, pu = j, u - RING
                else:
                    pj, pu = j - 1, u + IU - RING
                if pu in NATIVE:
                    sp.wait_ge(nat_used, native_count(pj, pu))
                else:
                    sp.wait_ge(hi_done, split_count(pj, pu))
                    sp.wait_ge(lo_done, split_count(pj, pu))

            w1, w2 = a["w_mlp1"][0], a["w_mlp2"][0]

            def load_w1(j, e):
                for u in range(W1U):
                    slot_free(j, u)
                    slot, _ = raw_at(j, u)
                    sp.dma_start(raw[slot][:, :], w1[e, u * P:(u + 1) * P, :].rearrange("e p n -> p (e n)"))\
                        .then_inc(raw_in[slot], 16)

            def load_w2(j, e, first):
                for v in range(W2U):
                    slot_free(j, first + v)
                    slot, _ = raw_at(j, first + v)
                    sp.dma_start(raw[slot][:, :].rearrange("p (k n) -> p k n", k=2),
                                 w2[e, 2 * v * P:(2 * v + 2) * P, :].rearrange("e (k p) n -> p (e k) n", p=P))\
                        .then_inc(raw_in[slot], 16)

            load_w1(0, slice(0, 1))
            in_sbuf(sp, ("tab",))
            n_items = number_of_items(sp)

            def expert(j):
                return bass.ds(sp.value_load(items[0:1, bass.ds(j, 1)], min_val=0, max_val=NE - 1), 1)

            load_w1(1, slice(1, 2))
            load_w2(1, slice(0, 1), W1U)
            with sp.Fori(2, n_items) as j:
                load_w1(j, expert(j))
                load_w2(j, expert(j - 1), W1U)
            load_w2(n_items, expert(n_items - 1), 0)
            sp.wait_ge(sc_add, n_items * 4)
            sp.dma_start(out.rearrange("o (t p) d -> p (o t) d", p=P), X[:, :, :]).then_inc(out_dma, 16)
            sp.wait_ge(out_dma, 16)

        @block.gpsimd
        def _(pool):
            pool.dma_start(bg[:, :], a["b_gate"][0:1, :].to_broadcast([P, 3 * D])).then_inc(bcast_in, 16)
            pool.dma_start(gffn[:, :], a["g_ffn"][0:1, :].to_broadcast([P, D])).then_inc(bcast_in, 16)
            pool.dma_start(brt[:, :], a["b_router"][0:1, :].to_broadcast([P, NE])).then_inc(bcast_in, 16)
            pool.dma_start(wr[:, :, :], a["w_router"][0].rearrange("(k p) e -> p k e", p=P)).then_inc(bcast_in, 16)
            pool.wait_ge(pair_sem("gate5"), GI["gate5"] // 2 + 1)
            pool.dma_start(b2s, a["b_mlp2"][0]).then_inc(b2_in, 16)
            in_sbuf(pool, ("logits",))
            pool.memset(b1s[64:P, :].bitcast(F32), 0.0).then_inc(zeroed, 1)
            pool.wait_ge(zeroed, 1)
            pool.memset(BL[:, :].bitcast(F32), 0.0).then_inc(zeroed, 1)

        @block.scalar
        def _(act):
            act.dma_start(misc[:, :], a["misc"]).then_inc(const_in, 16)
            act.dma_start(gains[:, :], a["gains"]).then_inc(const_in, 16)
            act.dma_start(decay, a["decay"]).then_inc(const_in, 16)
            act.dma_start(alibi[:, :], a["alibi"]).then_inc(const_in, 16)

            def roots(name, count, n):
                i = NORMS.index(name)
                act.wait_ge(sq_done, sum(SQUARES[:i + 1]))
                if SUMS[i]:
                    act.wait_ge(ss_done, sum(SUMS[:i + 1]))
                act.activation(stat[:, 1, 16 * i:16 * i + count], stat[:, 0, 16 * i:16 * i + count], ACT.Sqrt,
                               bias=eps, scale=1.0 / n).then_inc(sd_done, 1)

            def row_squares(name, src):
                i = NORMS.index(name)
                for t in range(TT):
                    if sum(SQUARES[:i]) + t:
                        act.wait_ge(sq_done, sum(SQUARES[:i]) + t)
                    act.activation(sq, src[:, t, :], ACT.Square,
                                   accum_out=stat[:, 0, 16 * i + t:16 * i + t + 1]).then_inc(sq_done, 1)
                roots(name, TT, D)

            act.wait_ge(x_in, 16)
            act.wait_ge(const_in, 16 * N_CONST)
            row_squares("x", X)
            act.wait_ge(mem_in, 16)
            row_squares("mem", mem)

            for step in STEPS:
                if step[0] == "group":
                    g = step[1]
                    P2 = pair[GI[g] % 2]
                    if g in ("mq", "mk", "cq", "ck"):
                        act.wait_ge(unit_used, UNITS_DONE[GI[g]])
                        act.wait_ge(sq_done, sum(SQUARES[:NORMS.index(g)]))
                        act.activation(sq.rearrange("p (t n) -> p t n", t=TT), P2, ACT.Square).then_inc(sq_done, 1)
                        heads = TT * (MOBA_H if g[0] == "m" else MEM_H)
                        roots(g, heads, MOBA_HD if g[0] == "m" else MEM_HD)
                    elif g in V:
                        act.wait_ge(unit_used, UNITS_DONE[GI[g]])
                        act.activation(V[g][:, :, :], P2, ACT.Copy).then_inc(pair_sem(g), 1)
                    elif g == "gate3":
                        act.wait_ge(pair_sem("rg"), GI["rg"] // 2 + 1)
                        act.activation(rgs, V["rg"][:, :, :], ACT.Sigmoid).then_inc(sig_done, 1)
                        for i in range(4):
                            sigmoid_gate(act, i)
                    elif g in ("gate4", "gate5"):
                        sigmoid_gate(act, int(g[-1]))
                else:
                    key = step[1:]
                    kind, b = key[0], bank(key)
                    if kind == "ret_o":
                        hp = key[1]
                        act.wait_ge(task_done, TASKS[key] + 1)
                        act.wait_ge(sq_done, sum(SQUARES[:NORMS.index(f"ret{hp}")]))
                        act.activation(sq[:, 0:512], b, ACT.Square).then_inc(sq_done, 1)
                        roots(f"ret{hp}", 2 * TT, RET_DV)
                    elif kind == "sc":
                        h = key[1]
                        act.wait_ge(max_done, 2 * h + 2)
                        pr = probs[h % 4]
                        if HEADS[h][0] == "mem" and h >= 4:
                            act.wait_ge(task_done, TASKS[("pT", h - 4)] + 1)
                        for it in range(TT):
                            cols = slice(it * S, (it + 1) * S)
                            act.activation(pr[:, cols], (pr if HEADS[h][0] == "moba" else b)[:, cols], ACT.Exp,
                                           bias=smx[:, 1, 2 * h + it:2 * h + it + 1],
                                           accum_out=smx[:, 2, 2 * h + it:2 * h + it + 1]).then_inc(exp_done, 1)
                    elif kind == "pT":
                        h = key[1]
                        n = 384 if HEADS[h][0] == "moba" else 512
                        act.wait_ge(task_done, TASKS[key] + 1)
                        if h >= 4:
                            act.wait_ge(task_done, TASKS[("pv", h - 4)] + 1)
                        act.activation(PT[h % 4][:, 0:n], b[:, 0:n], ACT.Copy).then_inc(read_sem(key), 1)
                    elif kind == "oT" and key[1] != "ret":
                        act.wait_ge(task_done, TASKS[key] + 1)
                        act.activation(oT[key[1]][:, :, key[2] * P:(key[2] + 1) * P], b.rearrange("p (c s) -> p c s", s=P),
                                       ACT.Copy).then_inc(read_sem(key), 1)
                    elif kind == "yT":
                        n, t = key[1:]
                        act.wait_ge(task_done, TASKS[key] + 1)
                        act.activation(mT[:, 4 * n:4 * n + 4, t * P:(t + 1) * P], b.rearrange("p (c s) -> p c s", s=P),
                                       ACT.Copy).then_inc(read_sem(key), 1)
                    elif kind == "xT":
                        t, kk = key[1:]
                        if (t, kk) == (0, 0):
                            for i in range(TT):
                                act.wait_ge(xt_done, i + 1)
                                act.activation(xth[:, i, :], hx[:, i, :], ACT.Copy).then_inc(xh_done, 1)
                        act.wait_ge(task_done, TASKS[key] + 1)
                        act.activation(hT[:, 4 * kk:4 * kk + 4, t * P:(t + 1) * P], b.rearrange("p (c s) -> p c s", s=P),
                                       ACT.Copy).then_inc(read_sem(key), 1)
                    elif kind == "logits":
                        act.wait_ge(task_done, TASKS[key] + 1)
                        for half in range(2):
                            act.dma_start(b1raw[32 * half:32 * half + 32, :], a["b_mlp1"][0]).then_inc(b1_in, 16)
                        act.wait_ge(rout, RI["nv"])
                        for t in range(TT):
                            act.activation(e4[:, t, :], v8[:, t, 0:4], ACT.Exp, bias=nv[:, t:t + 1],
                                           accum_out=se[:, t:t + 1]).then_inc(rexp, 1)
                        act.wait_ge(b1_in, 32)
                        act.activation(b1s[0:64, :], b1raw, ACT.Copy).then_inc(b1h, 1)
                if step == ("group", "out1"):
                    for g in ("out0", "out1"):
                        act.wait_ge(pair_sem(g), GI[g] // 2 + 1)
                    row_squares("x2", X)

            def high(j, u):
                if u in NATIVE:
                    return
                slot, uses = raw_at(j, u)
                act.wait_ge(raw_in[slot], uses * 16)
                if not (isinstance(j, int) and split_count(j, u) <= HL):
                    act.wait_ge(hl_used, split_count(j, u) - HL)
                act.activation(hi[hl_slot(j, u)][:, :], raw[slot][:, :], ACT.Copy).then_inc(hi_done, 1)

            def gathered(i):
                act.wait_ge(ga_pe, i * 2 + 1)
                act.activation(XG[:, :, 0:SL], banks[6].rearrange("p (k s) -> p k s", s=SL), ACT.Copy).then_inc(xgh, 1)

            def output_high(i):
                act.activation(YH[:, :], PS[:, 2048:3072], ACT.Copy).then_inc(yh, 1)

            def scatter_matrix(i):
                act.activation(ST[:, :], banks[7][:, 0:S], ACT.Copy).then_inc(st_act, 1)

            def body(j):
                later = not isinstance(j, int)
                for u in range(W1U):
                    high(j, u)
                    if u == 0 and (later or j >= 1):
                        act.wait_ge(tr_pe, j)
                        act.activation(AT[:, :, 0, :].rearrange("p (h c) s -> p h c s", h=2),
                                       banks[6].rearrange("p (c h s) -> p h c s", h=2, s=SL), ACT.Copy).then_inc(ath, 1)
                    if u == 1 and later:
                        unit_done(act, j - 1, IU - 1)
                        output_high(j - 2)
                    if u == 3:
                        act.wait_ge(st_pe, j + 1)
                        if later:
                            scatter_matrix(j - 2)
                        if later or j >= 1:
                            act.wait_ge(swi, 6 * j)
                        act.activation(slotw[:, :], banks[7][:, S:S + 1], ACT.Copy).then_inc(slw, 1)
                if later or j >= 1:
                    for u in range(W1U, IU):
                        high(j, u)
                unit_done(act, j, W1U - 1)
                act.activation(HB[0:64, :], PS[64:P, 0:1024], ACT.Copy).then_inc(hb_act, 1)
                act.activation(HB[64:P, :], PS[0:64, 1024:2048], ACT.Copy).then_inc(hb_act, 1)
                gathered(j + 1)
                act.wait_ge(swi, 6 * j + 3)
                act.activation(sig, glu, ACT.Sigmoid, scale=ALPHA).then_inc(sgm, 1)

            in_sbuf(act, ("tab",))
            for q in range(4):
                in_sbuf(act, ("b2", q // 2, q % 2))
            n_items = number_of_items(act)
            gathered(0)
            body(0)
            body(1)
            with act.Fori(2, n_items) as j:
                body(j)
            j = n_items
            act.wait_ge(tr_pe, j)
            act.activation(AT[:, :, 0, :].rearrange("p (h c) s -> p h c s", h=2),
                           banks[6].rearrange("p (c h s) -> p h c s", h=2, s=SL), ACT.Copy).then_inc(ath, 1)
            unit_done(act, j - 1, IU - 1)
            output_high(j - 2)
            act.wait_ge(st_pe, j + 1)
            scatter_matrix(j - 2)
            act.wait_ge(nat_used, native_count(j - 1, IU - 1) + W2U)
            act.wait_ge(sc_pe, 4 * (j - 1))
            output_high(j - 1)
            act.wait_ge(st_pe, j + 2)
            scatter_matrix(j - 1)

        @block.vector
        def _(dve):
            def linked(ins, s, value):
                ins.then_inc(s, 1)
                dve.wait_ge(s, value)

            def reciprocal_roots(name, count):
                i = NORMS.index(name)
                dve.wait_ge(sd_done, i + 1)
                linked(dve.reciprocal(stat[:, 2, 16 * i:16 * i + count], stat[:, 1, 16 * i:16 * i + count]), rs_done, i + 1)
                return stat[:, 2, 16 * i:16 * i + count]

            def row_norm(i, src, dst):
                r = reciprocal_roots(NORMS[i], TT)
                for t in range(TT):
                    dve.tensor_scalar(dst[:, t, :], src[:, t, :], r[:, t:t + 1], None, ALU.mult).then_inc(hx_done, 1)

            row_norm(0, X, hx)
            dve.wait_ge(bcast_in, 16 * N_BCAST)
            dve.wait_ge(const_in, 16 * N_CONST)
            for step in STEPS:
                if step[0] == "group":
                    g = step[1]
                    P2 = pair[GI[g] % 2]
                    free = pair_sem(g)
                    if g == "rqk":
                        row_norm(1, mem, mem)
                        dve.wait_ge(unit_used, UNITS_DONE[GI[g]])
                        dve.tensor_copy(tq[0][:, :, :], P2).then_inc(free, 1)
                    elif g in ("mq", "mk", "cq", "ck"):
                        i, hd = NORMS.index(g), (MOBA_HD if g[0] == "m" else MEM_HD)
                        heads = 512 // hd
                        dve.wait_ge(sq_done, sum(SQUARES[:i + 1]))
                        dve.tensor_reduce(stat[:, 0, 16 * i:16 * i + TT * heads], sq.rearrange("p (g d) -> p g d", d=hd),
                                          AX.X, ALU.add).then_inc(ss_done, 1)
                        r = reciprocal_roots(g, TT * heads)
                        q = Q_GROUPS.index(g)
                        if q >= 2:
                            dve.wait_ge(task_done, TASKS[("qT", Q_GROUPS[q - 2], 1)] + 1)
                        dve.tensor_tensor(tq[q % 2][:, :, :].rearrange("p t (h d) -> p (t h) d", d=hd),
                                          P2.rearrange("p t (h d) -> p (t h) d", d=hd),
                                          r.rearrange("p (g o) -> p g o", o=1).to_broadcast([P, TT * heads, hd]),
                                          ALU.mult).then_inc(free, 1)
                    elif g.startswith("gate"):
                        i = int(g[-1])
                        dve.wait_ge(unit_used, UNITS_DONE[GI[g]])
                        for t in range(TT):
                            ins = dve.tensor_tensor(gates[:, t, 512 * i:512 * i + 512], P2[:, t, :], bg[:, 512 * i:512 * i + 512], ALU.add)
                            if t:
                                ins.then_inc(free, 1)
                        if g == "gate4":
                            dve.wait_ge(sig_done, 1)
                            linked(dve.tensor_tensor(V["rg"][:, :, :], V["rg"][:, :, :], rgs, ALU.mult), silu_done, 1)
                            dve.tensor_tensor(o["ret"][:, :, :], o["ret"][:, :, :], V["rg"][:, :, :], ALU.mult).then_inc(silu_done, 1)
                    elif g.startswith("br_"):
                        n, br = int(g[-1]), g[3:-1]
                        gate = 2 * {"ret": 0, "moba": 1, "mem": 2}[br] + n
                        col = 512 * gate
                        half = slice(512 * n, 512 * n + 512)
                        dve.wait_ge(unit_used, UNITS_DONE[GI[g]])
                        dve.wait_ge(sig_done, gate + 2)
                        if br == BRANCH_ORDER[0][1]:
                            dve.tensor_tensor(y[:, :, half], P2, gates[:, :, col:col + 512], ALU.mult).then_inc(free, 1)
                        else:
                            linked(dve.tensor_tensor(tmp[:, :, :], P2, gates[:, :, col:col + 512], ALU.mult), free, GI[g] // 2 + 1)
                            k = 2 * n + (br == "ret") + 1
                            if k % 2:
                                first = f"br_{BRANCH_ORDER[0][1]}{n}"
                                dve.wait_ge(pair_sem(first), GI[first] // 2 + 1)
                            linked(dve.tensor_tensor(y[:, :, half], y[:, :, half], tmp[:, :, :], ALU.add), y_done, k)
                    elif g.startswith("out"):
                        n = int(g[-1])
                        half = slice(512 * n, 512 * n + 512)
                        dve.wait_ge(unit_used, UNITS_DONE[GI[g]])
                        dve.tensor_tensor(X[:, :, half], X[:, :, half], P2, ALU.add).then_inc(free, 1)
                    continue
                key = step[1:]
                kind, b = key[0], bank(key)
                done = read_sem(key)
                blocks = b.rearrange("p (c s) -> p c s", s=P)
                if kind == "hT":
                    src, t, kk = key[1:]
                    dve.wait_ge(task_done, TASKS[key] + 1)
                    c = src * KC + 4 * kk
                    dve.tensor_tensor((hT, mT)[src][:, 4 * kk:4 * kk + 4, t * P:(t + 1) * P], blocks,
                                      gcol[:, c:c + 4].rearrange("p (c o) -> p c o", o=1).to_broadcast([P, 4, P]),
                                      ALU.mult).then_inc(done, 1)
                elif kind == "qT":
                    g, t = key[1:]
                    dst = qT[g][:, :, t * P:(t + 1) * P]
                    dve.wait_ge(task_done, TASKS[key] + 1)
                    if g == "rqk":
                        dve.tensor_copy(dst, blocks).then_inc(done, 1)
                    else:
                        c = ("mq", "mk", "cq", "ck").index(g)
                        scale = {"mq": MOBA_HD ** -0.5, "cq": MEM_HD ** -0.5}.get(g, 1.0)
                        dve.tensor_scalar(dst, blocks, qgain[:, c:c + 1], scale, ALU.mult, ALU.mult).then_inc(done, 1)
                elif kind == "ret_s":
                    h = key[1]
                    dve.wait_ge(task_done, TASKS[key] + 1)
                    if h >= 2:
                        dve.wait_ge(task_done, TASKS[("ret_o", h // 2 - 1)] + 1)
                    dve.tensor_tensor(retS[h % 2], b[:, 0:384], decay[:, 384 * h:384 * h + 384], ALU.mult).then_inc(done, 1)
                elif kind == "ret_o":
                    hp = key[1]
                    i = NORMS.index(f"ret{hp}")
                    dve.wait_ge(sq_done, sum(SQUARES[:i + 1]))
                    dve.tensor_reduce(stat[:, 0, 16 * i:16 * i + 4], sq[:, 0:512].rearrange("p (g d) -> p g d", d=RET_DV),
                                      AX.X, ALU.add).then_inc(ss_done, 1)
                    r = reciprocal_roots(f"ret{hp}", 4)
                    dve.tensor_tensor(o["ret"][:, :, 256 * hp:256 * hp + 256].rearrange("p t (h d) -> p t h d", d=RET_DV),
                                      b.rearrange("p (t h d) -> p t h d", t=TT, d=RET_DV),
                                      r.rearrange("p (t h o) -> p t h o", t=TT, o=1).to_broadcast([P, TT, 2, RET_DV]),
                                      ALU.mult).then_inc(done, 1)
                elif kind == "sc":
                    h = key[1]
                    hh, moba = HEADS[h][1], HEADS[h][0] == "moba"
                    cols = slice(2 * h, 2 * h + 2)
                    dve.wait_ge(task_done, TASKS[key] + 1)
                    src = b
                    if moba:
                        if h >= 4:
                            dve.wait_ge(task_done, TASKS[("pT", h - 4)] + 1)
                        src = probs[h % 4]
                        dve.scalar_tensor_tensor(src, alibi[:, :], 2.0 ** (-8.0 * (hh + 1) / MOBA_H), b, ALU.mult, ALU.add)\
                            .then_inc(done, 1)
                        in_sbuf(dve, key)
                    linked(dve.tensor_reduce(smx[:, 0, cols], src.rearrange("p (t s) -> p t s", s=S), AX.X, ALU.max),
                           max_done, 2 * h + 1)
                    dve.tensor_scalar(smx[:, 1, cols], smx[:, 0, cols], -1.0, None, ALU.mult).then_inc(max_done, 1)
                    dve.wait_ge(exp_done, 2 * h + 2)
                    dve.reciprocal(smx[:, 3, cols], smx[:, 2, cols]).then_inc(rcp_done if moba else done, 1)
                elif kind == "pv":
                    h = key[1]
                    br, hh = HEADS[h]
                    hd = MOBA_HD if br == "moba" else MEM_HD
                    dve.wait_ge(task_done, TASKS[key] + 1)
                    if br == "moba":
                        dve.wait_ge(rcp_done, h + 1)
                    else:
                        in_sbuf(dve, ("sc", h))
                    dve.tensor_tensor(o[br][:, :, hh * hd:(hh + 1) * hd],
                                      b[:, 0:TT * hd].rearrange("p (t d) -> p t d", d=hd),
                                      smx[:, 3, 2 * h:2 * h + 2].rearrange("p (t o) -> p t o", o=1).to_broadcast([P, TT, hd]),
                                      ALU.mult).then_inc(done, 1)
                elif kind == "oT" and key[1] == "ret":
                    t = key[2]
                    dve.wait_ge(task_done, TASKS[key] + 1)
                    dve.tensor_scalar(oT["ret"][:, :, t * P:(t + 1) * P], blocks, qgain[:, 4:5], None, ALU.mult).then_inc(done, 1)
                elif kind == "xT" and key[1:] == (0, 0):
                    r = reciprocal_roots("x2", TT)
                    for t in range(TT):
                        dve.scalar_tensor_tensor(hx[:, t, :], X[:, t, :], r[:, t:t + 1], gffn[:, :], ALU.mult, ALU.mult)\
                            .then_inc(xt_done, 1)
                    for t in range(TT):
                        dve.wait_ge(xh_done, t + 1)
                        dve.tensor_tensor(xtl[:, t, :], hx[:, t, :], xth[:, t, :].bitcast(F32), ALU.subtract).then_inc(xl_done, 1)
                elif kind == "logits":
                    dve.wait_ge(task_done, TASKS[key] + 1)
                    for t in range(TT):
                        ins = dve.tensor_tensor(lg[:, t, :], b[:, t * NE:(t + 1) * NE], brt[:, :], ALU.add)
                    ins.then_inc(done, 1)
                    in_sbuf(dve, key)
                    for t in range(TT):
                        dve.max(v8[:, t, :], lg[:, t, :]).then_inc(rout, 1)
                    dve.wait_ge(rout, RI["max1"])
                    for t in range(TT):
                        dve.max_index(i8[:, t, :], v8[:, t, :], lg[:, t, :]).then_inc(rout, 1)
                    dve.tensor_scalar(nv[:, :], v8[:, :, 0], -1.0, None, ALU.mult).then_inc(rout, 1)
                    dve.wait_ge(rout, RI["mi1"])
                    linked(dve.tensor_copy(i8f[:, :, :], i8[:, :, :]), rout, RI["if"])
                    for t in range(TT):
                        dve.tensor_tensor(oh[:, t, :, :], iota32.rearrange("p (o e) -> p o e", o=1).to_broadcast([P, 4, NE]),
                                          i8f[:, t, 0:4].rearrange("p (k o) -> p k o", o=1).to_broadcast([P, 4, NE]),
                                          ALU.is_equal).then_inc(rout, 1)
                    dve.wait_ge(rout, RI["oh1"])
                    for t in range(TT):
                        dve.tensor_reduce(MG[:, 0, t, :], oh[:, t, :, :].rearrange("p k e -> p e k"), AX.X, ALU.add).then_inc(rout, 1)
                    dve.wait_ge(rexp, TT)
                    linked(dve.reciprocal(se[:, TT:2 * TT], se[:, 0:TT]), rout, RI["rse"])
                    linked(dve.tensor_tensor(e4[:, :, :], e4[:, :, :],
                                             se[:, TT:2 * TT].rearrange("p (t o) -> p t o", o=1).to_broadcast([P, TT, 4]), ALU.mult),
                           rout, RI["w4"])
                    for t in range(TT):
                        dve.tensor_tensor(ohw[:, t, :, :], oh[:, t, :, :],
                                          e4[:, t, :].rearrange("p (k o) -> p k o", o=1).to_broadcast([P, 4, NE]),
                                          ALU.mult).then_inc(rout, 1)
                    dve.wait_ge(rout, RI["ow1"])
                    for t in range(TT):
                        dve.tensor_reduce(MG[:, 1, t, :], ohw[:, t, :, :].rearrange("p k e -> p e k"), AX.X, ALU.add).then_inc(rout, 1)
                    dve.wait_ge(rout, RI["g1"])
                elif kind == "pos":
                    dve.wait_ge(task_done, TASKS[key] + 1)
                    dve.scalar_tensor_tensor(posm[:, :, :], b[:, 0:TT * NE].rearrange("p (t e) -> p t e", t=TT), 1.0,
                                             MG[:, 0, :, :], ALU.add, ALU.mult).then_inc(done, 1)
                    in_sbuf(dve, key)
                    dve.tensor_scalar(posm[:, :, :], posm[:, :, :], -1.0, None, ALU.add).then_inc(rout, 1)
                elif kind == "cnt":
                    dve.wait_ge(task_done, TASKS[key] + 1)
                    dve.tensor_copy(rt[:, 0:1], b[0:NE, 0:1]).then_inc(done, 1)
                    in_sbuf(dve, key)
                    dve.wait_ge(rout, RI["posm"])
                    linked(dve.tensor_scalar(rt[:, 1:4], thresholds[0:NE, :], rt[:, 0:1], None, ALU.is_lt), rout, RI["g3"])
                    linked(dve.tensor_reduce(rt[:, 4:5], rt[:, 1:4], AX.X, ALU.add), rout, RI["n"])
                elif kind == "tabT":
                    dve.wait_ge(task_done, TASKS[key] + 1)
                    dve.tensor_copy(tabT[:, :, :], b[0:NE, :].rearrange("p (a s) -> p a s", a=2)).then_inc(done, 1)
                elif kind == "off":
                    dve.wait_ge(task_done, TASKS[key] + 1)
                    linked(dve.tensor_copy(rt[:, 5:6], b[0:NE, 0:1]), rout, RI["off"])
                    dve.tensor_copy(items[0:1, MAX_ITEMS:MAX_ITEMS + 1], b[0:1, 2:3]).then_inc(done, 1)
                    linked(dve.tensor_scalar(rt[:, 6:9], iota32[0:NE, 0:3], rt[:, 5:6], None, ALU.add), rout, RI["offr"])
                    sel = [rt[:, 16 + 16 * r:32 + 16 * r] for r in range(3)]
                    for r in range(3):
                        dve.tensor_scalar(sel[r], iota32[0:NE, 0:16], rt[:, 6 + r:7 + r], rt[:, 1 + r:2 + r], ALU.is_equal, ALU.mult)\
                            .then_inc(rout, 1)
                    dve.wait_ge(rout, RI["s3"])
                    linked(dve.tensor_tensor(selw[:, 0, NE:], sel[0], sel[1], ALU.add), rout, RI["t1"])
                    linked(dve.tensor_tensor(selw[:, 0, NE:], selw[:, 0, NE:], sel[2], ALU.add), rout, RI["t2"])
                    linked(dve.scalar_tensor_tensor(selw[:, 1, NE:], sel[1], 2.0, sel[0], ALU.mult, ALU.add), rout, RI["u1"])
                    linked(dve.scalar_tensor_tensor(selw[:, 1, NE:], sel[2], 3.0, selw[:, 1, NE:], ALU.mult, ALU.add), rout, RI["u2"])
                    dve.tensor_scalar(selw[:, 1, NE:], selw[:, 1, NE:], -float(SL), None, ALU.mult).then_inc(rout, 1)
                    dve.tensor_copy(selw[:, 0, 0:NE], ident[0:NE, 0:NE]).then_inc(rout, 1)
                    dve.memset(selw[:, 1, 0:NE], 0.0).then_inc(rout, 1)
                elif kind == "tab":
                    dve.wait_ge(task_done, TASKS[key] + 1)
                    m = MAX_ITEMS
                    dve.tensor_copy(posi[:, :, :], b[:, 0:2 * m].rearrange("p (t j) -> p t j", t=TT)).then_inc(rout, 1)
                    dve.tensor_copy(gi[:, :, :], b[:, 2 * m:4 * m].rearrange("p (t j) -> p t j", t=TT)).then_inc(rout, 1)
                    dve.tensor_copy(bsel[:, :], b[0:64, 4 * m:5 * m]).then_inc(rout, 1)
                    dve.tensor_copy(items[0:1, 0:m], b[0:1, 5 * m:6 * m]).then_inc(done, 1)
                elif kind == "b2":
                    t, n = key[1:]
                    dve.wait_ge(task_done, TASKS[key] + 1)
                    dve.tensor_tensor(X[:, t, 512 * n:512 * n + 512], X[:, t, 512 * n:512 * n + 512], b, ALU.add).then_inc(done, 1)

            dve.wait_ge(b1h, 1)
            dve.tensor_tensor(b1s[32:64, :], b1raw[32:64, :], b1s[32:64, :].bitcast(F32), ALU.subtract).then_inc(b1l, 1)

            def low(j, u):
                if u in NATIVE:
                    return
                slot, _ = raw_at(j, u)
                dve.wait_ge(hi_done, split_count(j, u))
                dve.tensor_tensor(lo[hl_slot(j, u)][:, :], raw[slot][:, :], hi[hl_slot(j, u)][:, :].bitcast(F32), ALU.subtract)\
                    .then_inc(lo_done, 1)

            def gather_matrix(i):
                for t in range(TT):
                    dve.tensor_scalar(SG[:, t, :], slotn, posi[:, t, bass.ds(i, 1)], None, ALU.is_equal).then_inc(sg_done, 1)
                dve.tensor_scalar(BL[0:64, 0:SL], ones[0:64, 0:SL], bsel[:, bass.ds(i, 1)], None, ALU.mult).then_inc(sg_done, 1)

            def scatter_matrix(i):
                for t in range(TT):
                    dve.tensor_scalar(SS[:, t, :], slotn, posi[:, t, bass.ds(i, 1)], None, ALU.is_equal).then_inc(ss_mat, 1)

            def gathered(i):
                dve.wait_ge(ga_pe, i * 2 + 2)
                dve.tensor_copy(XG[:, :, SL:2 * SL], banks[7].rearrange("p (k s) -> p k s", s=SL)).then_inc(xgl, 1)

            def activations_low(j):
                dve.wait_ge(ath, j)
                dve.tensor_tensor(AT[:, :, 1, :].rearrange("p (h c) s -> p h c s", h=2),
                                  banks[6].rearrange("p (c h s) -> p h c s", h=2, s=SL),
                                  AT[:, :, 0, :].bitcast(F32).rearrange("p (h c) s -> p h c s", h=2), ALU.subtract).then_inc(atl, 1)

            def output_low(i):
                dve.wait_ge(yh, i + 1)
                dve.tensor_tensor(YL[:, :], PS[:, 2048:3072], YH[:, :].bitcast(F32), ALU.subtract).then_inc(yl, 1)

            def add(i, q):
                t, n = q // 2, q % 2
                dve.wait_ge(sc_pe, 4 * i + (q + 1))
                dve.tensor_tensor(X[:, t, 512 * n:512 * n + 512], X[:, t, 512 * n:512 * n + 512], banks[6 + q % 2], ALU.add)\
                    .then_inc(sc_add, 1)

            def body(j):
                later = not isinstance(j, int)
                for u in range(W1U):
                    low(j, u)
                    if u == 0 and (later or j >= 1):
                        activations_low(j)
                    if u == 1 and later:
                        output_low(j - 2)
                        dve.wait_ge(st_pe, j)
                        scatter_matrix(j - 2)
                    if later and u in (5, 7):
                        for q in ((0, 1) if u == 5 else (2, 3)):
                            add(j - 2, q)
                dve.wait_ge(st_pe, j + 1)
                gather_matrix(j + 1)
                if later or j >= 1:
                    for u in range(W1U, IU):
                        low(j, u)
                dve.wait_ge(hb_act, 2 * j + 1)
                dve.tensor_tensor(HS[0:64, :], PS[0:64, 0:1024], HB[0:64, :], ALU.add).then_inc(swi, 1)
                dve.wait_ge(hb_act, 2 * j + 2)
                dve.tensor_tensor(HS[64:P, :], PS[64:P, 1024:2048], HB[64:P, :], ALU.add).then_inc(swi, 1)
                dve.wait_ge(swi, 6 * j + 2)
                dve.tensor_scalar(glu, HS[:, 0:1024:2], LIMIT, None, ALU.min).then_inc(swi, 1)
                dve.tensor_scalar(lin, HS[:, 1:1024:2], LIMIT, -LIMIT, ALU.min, ALU.max).then_inc(swi, 1)
                gathered(j + 1)
                dve.wait_ge(swi, 6 * j + 4)
                dve.scalar_tensor_tensor(lin, lin, 1.0, glu, ALU.add, ALU.mult).then_inc(swi, 1)
                dve.wait_ge(swi, 6 * j + 5)
                dve.wait_ge(sgm, j + 1)
                dve.wait_ge(slw, j + 1)
                dve.scalar_tensor_tensor(act_t, lin, slotw[:, 0:1], sig, ALU.mult, ALU.mult).then_inc(swi, 1)

            in_sbuf(dve, ("tab",))
            for q in range(4):
                in_sbuf(dve, ("b2", q // 2, q % 2))
            dve.wait_ge(rout, RI["bsel"])
            dve.wait_ge(zeroed, 2)
            n_items = number_of_items(dve)
            gather_matrix(0)
            gathered(0)
            body(0)
            body(1)
            with dve.Fori(2, n_items) as j:
                body(j)
            j = n_items
            activations_low(j)
            output_low(j - 2)
            dve.wait_ge(st_pe, j)
            scatter_matrix(j - 2)
            for q in range(4):
                add(j - 2, q)
            dve.wait_ge(st_pe, j + 1)
            scatter_matrix(j - 1)
            output_low(j - 1)
            for q in range(4):
                add(j - 1, q)

        @block.tensor
        def _(pe):
            unit = 0
            for step in STEPS:
                if step[0] == "group":
                    g = step[1]
                    gi_, kc = GI[g], dict(GROUPS)[g]
                    if g == "rqk":
                        src = hT
                        for t in range(TT):
                            for kk in range(2):
                                in_sbuf(pe, ("hT", 0, t, kk))
                    if g == "ck":
                        for t in range(TT):
                            for kk in range(2):
                                in_sbuf(pe, ("hT", 1, t, kk))
                    if g.startswith("br_"):
                        for t in range(TT):
                            in_sbuf(pe, ("oT", g[3:-1], t))
                    if g == "out0":
                        for n in range(2):
                            for t in range(TT):
                                in_sbuf(pe, ("yT", n, t))
                    src = mT if g in ("ck", "cv") or g.startswith("out") else oT[g[3:-1]] if g.startswith("br_") else hT
                    if gi_ >= 2:
                        pe.wait_ge(pair_free[gi_ % 2], gi_ // 2)
                    for hk in range(kc // 4):
                        pe.wait_ge(raw_in[unit % RING], 16 * (unit // RING + 1))
                        w = raw[unit % RING][:, :].rearrange("p (k n) -> p k n", k=4)
                        for t in range(TT):
                            for kk in range(4):
                                k = 4 * hk + kk
                                mm = pe.matmul(pair[gi_ % 2][:, t, :], src[:, k, t * P:(t + 1) * P], w[:, kk, :],
                                               start=(k == 0), stop=(k == kc - 1))
                        mm.then_inc(unit_used, 1)
                        unit += 1
                    continue
                key = step[1:]
                kind, b, n = key[0], bank(key), TASKS[key]
                if n >= 4:
                    pe.wait_ge(bank_read[n % 4], n // 4)

                def transposes(src, rows=P, blocks=4):
                    for c in range(blocks):
                        mm = pe.transpose(b[0:P, c * P:(c + 1) * P], src(c), ident)
                    return mm

                if kind == "hT":
                    s, t, kk = key[1:]
                    pe.wait_ge(const_in, 16 * N_CONST)
                    pe.wait_ge(hx_done, 2 * s + t + 1)
                    mm = transposes(lambda c: (hx, mem)[s][:, t, (4 * kk + c) * P:(4 * kk + c + 1) * P])
                elif kind == "qT":
                    g, t = key[1:]
                    pe.wait_ge(pair_sem(g), GI[g] // 2 + 1)
                    mm = transposes(lambda c: tq[Q_GROUPS.index(g) % 2][:, t, c * P:(c + 1) * P])
                elif kind == "ret_s":
                    h = key[1]
                    po, c = 64 * (h % 2), h // 2
                    q, k = qT["rqk"][po:po + 64, c, :], qT["rqk"][po:po + 64, 2 + c, :]
                    for t in range(TT):
                        in_sbuf(pe, ("qT", "rqk", t))
                    pe.matmul(b[:, 0:S], k[:, 0:P], q, start=True, stop=True)
                    mm = pe.matmul(b[:, S:384], k[:, P:S], q[:, P:S], start=True, stop=True)
                elif kind == "ret_o":
                    hp = key[1]
                    pe.wait_ge(pair_sem("rv"), GI["rv"] // 2 + 1)
                    for hh in range(2):
                        h = 2 * hp + hh
                        in_sbuf(pe, ("ret_s", h))
                        v = V["rv"][:, :, h * RET_DV:(h + 1) * RET_DV]
                        sc = retS[h % 2]
                        pe.matmul(b[:, hh * P:(hh + 1) * P], sc[:, 0:P], v[:, 0, :], start=True, stop=True)
                        ob = b[:, S + hh * P:S + (hh + 1) * P]
                        pe.matmul(ob, sc[:, P:S], v[:, 0, :], start=True, stop=False)
                        mm = pe.matmul(ob, sc[:, S:384], v[:, 1, :], start=False, stop=True)
                elif kind == "sc":
                    br, h = HEADS[key[1]]
                    gq, gk = ("mq", "mk") if br == "moba" else ("cq", "ck")
                    for t in range(TT):
                        in_sbuf(pe, ("qT", gq, t))
                        in_sbuf(pe, ("qT", gk, t))
                    rows, c = (slice(64 * (h % 2), 64 * (h % 2) + 64), h // 2) if br == "moba" else (slice(0, P), h)
                    for it in range(TT):
                        mm = pe.matmul(b[:, it * S:(it + 1) * S], qT[gq][rows, c, it * P:(it + 1) * P], qT[gk][rows, c, :],
                                       start=True, stop=True)
                elif kind == "pT":
                    h = key[1]
                    pe.wait_ge(exp_done, 2 * h + 2)
                    order = [(0, 0), (1, 0), (1, 1)] if HEADS[h][0] == "moba" else [(0, 0), (0, 1), (1, 0), (1, 1)]
                    mm = transposes(lambda c: probs[h % 4][:, order[c][0] * S + order[c][1] * P:order[c][0] * S + (order[c][1] + 1) * P],
                                    blocks=len(order))
                elif kind == "pv":
                    h = key[1]
                    br, hh = HEADS[h]
                    hd, vg = (MOBA_HD, "mv") if br == "moba" else (MEM_HD, "cv")
                    in_sbuf(pe, ("pT", h))
                    pe.wait_ge(pair_sem(vg), GI[vg] // 2 + 1)
                    order = [(0, 0), (1, 0), (1, 1)] if br == "moba" else [(0, 0), (0, 1), (1, 0), (1, 1)]
                    for c, (it, jt) in enumerate(order):
                        last = c + 1 == len(order) or order[c + 1][0] != it
                        mm = pe.matmul(b[:, it * hd:(it + 1) * hd], PT[h % 4][:, c * P:(c + 1) * P], V[vg][:, jt, hh * hd:(hh + 1) * hd],
                                       start=(jt == 0), stop=last)
                elif kind == "oT":
                    br, t = key[1:]
                    if br == "ret":
                        pe.wait_ge(silu_done, 2)
                    else:
                        for h in range(NH):
                            if HEADS[h][0] == br:
                                in_sbuf(pe, ("pv", h))
                    mm = transposes(lambda c: o[br][:, t, c * P:(c + 1) * P])
                elif kind == "yT":
                    nn, t = key[1:]
                    pe.wait_ge(y_done, 2 * nn + 2)
                    mm = transposes(lambda c: y[:, t, nn * 512 + c * P:nn * 512 + (c + 1) * P])
                elif kind == "xT":
                    t, kk = key[1:]
                    pe.wait_ge(xt_done, t + 1)
                    mm = transposes(lambda c: hx[:, t, (4 * kk + c) * P:(4 * kk + c + 1) * P])
                elif kind == "logits":
                    for t in range(TT):
                        for kk in range(2):
                            in_sbuf(pe, ("xT", t, kk))
                    pe.wait_ge(bcast_in, 16 * N_BCAST)
                    for t in range(TT):
                        for k in range(KC):
                            mm = pe.matmul(b[:, t * NE:(t + 1) * NE], hT[:, k, t * P:(t + 1) * P], wr[:, k, :],
                                           start=(k == 0), stop=(k == KC - 1))
                elif kind == "pos":
                    pe.wait_ge(rout, RI["m1"])
                    pe.matmul(b[:, 0:NE], before, MG[:, 0, 0, :], start=True, stop=True)
                    pe.matmul(b[:, NE:2 * NE], ones, MG[:, 0, 0, :], start=True, stop=False)
                    mm = pe.matmul(b[:, NE:2 * NE], before, MG[:, 0, 1, :], start=False, stop=True)
                elif kind == "cnt":
                    for t in range(TT):
                        mm = pe.matmul(b[0:NE, 0:1], MG[:, 0, t, :], ones[:, 0:1], start=(t == 0), stop=(t == 1))
                elif kind == "tabT":
                    pe.wait_ge(rout, RI["posm"])
                    for t in range(TT):
                        pe.transpose(b[0:NE, t * P:(t + 1) * P], posm[:, t, :], ident)
                        mm = pe.transpose(b[0:NE, S + t * P:S + (t + 1) * P], MG[:, 1, t, :], ident)
                elif kind == "off":
                    pe.wait_ge(rout, RI["n"])
                    pe.matmul(b[0:NE, 0:1], before[0:NE, 0:NE], rt[:, 4:5], start=True, stop=True)
                    mm = pe.matmul(b[0:1, 2:3], ones[0:NE, 0:1], rt[:, 4:5], start=True, stop=True)
                elif kind == "tab":
                    pe.wait_ge(rout, RI["sz"])
                    in_sbuf(pe, ("tabT",))
                    m = MAX_ITEMS
                    for t in range(TT):
                        rows = slice(t * P, (t + 1) * P)
                        pe.matmul(b[:, t * m:(t + 1) * m], tabT[:, 0, rows], selw[:, 0, :], start=True, stop=False)
                        pe.matmul(b[:, t * m:(t + 1) * m], ones[0:NE, :], selw[:, 1, :], start=False, stop=True)
                        pe.matmul(b[:, (2 + t) * m:(3 + t) * m], tabT[:, 1, rows], selw[:, 0, :], start=True, stop=True)
                    pe.matmul(b[0:64, 4 * m:5 * m], twice, selw[:, 0, :], start=True, stop=True)
                    mm = pe.matmul(b[0:1, 5 * m:6 * m], iotap[0:NE, :], selw[:, 0, :], start=True, stop=True)
                elif kind == "b2":
                    t, nn = key[1:]
                    pe.wait_ge(b2_in, 16)
                    mm = pe.matmul(b, tabT[:, 1, t * P:(t + 1) * P], b2s[:, nn * 512:nn * 512 + 512], start=True, stop=True)
                mm.then_inc(task_done, 1)

            def gather(i):
                pe.wait_ge(sg_done, 3 * (i + 1))
                for part, xt in enumerate((xth, xtl)):
                    for k in range(KC):
                        for t in range(TT):
                            mm = pe.matmul(banks[6 + part][:, k * SL:(k + 1) * SL], xt[:, t, k * P:(k + 1) * P], SG[:, t, 0:SL],
                                           start=(t == 0), stop=(t == 1))
                    mm.then_inc(ga_pe, 1)

            def products(j, u, first, chunks, lhs, width, out0, last_chunk, use_native):
                slot, uses = raw_at(j, u)
                if use_native:
                    pe.wait_ge(raw_in[slot], uses * 16)
                    parts = [raw[slot][:, :]]
                else:
                    pe.wait_ge(hi_done, split_count(j, u))
                    pe.wait_ge(lo_done, split_count(j, u))
                    parts = [hi[hl_slot(j, u)][:, :], lo[hl_slot(j, u)][:, :]]
                for c in range(chunks):
                    for p, w in enumerate(parts):
                        for n in range(width // 512):
                            mm = pe.matmul(PS[:, out0 + n * 512:out0 + (n + 1) * 512],
                                           lhs(c).bitcast(F32) if use_native else lhs(c),
                                           w[:, c * width + n * 512:c * width + (n + 1) * 512],
                                           start=(first and c == 0 and p == 0),
                                           stop=(last_chunk and c == chunks - 1 and p == len(parts) - 1))
                mm.then_inc(nat_used if use_native else hl_used, 1)

            def up(j, u):
                products(j, u, False, 1, lambda c: XG[:, u, :], FF2, 0, u == W1U - 1, u in NATIVE)

            def down(j, u, v, use_native):
                products(j, u, v == 0, 2, lambda c: AT[:, 2 * v + c, :, :].rearrange("p a s -> p (a s)"), D, 2048, v == W2U - 1, use_native)

            def scatter_transposes(i):
                pe.wait_ge(ss_mat, 2 * (i + 1))
                for t in range(TT):
                    mm = pe.transpose(banks[7][:, t * P:(t + 1) * P], SS[:, t, :].bitcast(F32), ident)
                return mm

            def scatter(i, q):
                t, n = q // 2, q % 2
                for p, part in enumerate((YH, YL)):
                    mm = pe.matmul(banks[6 + q % 2], ST[:, t * P:(t + 1) * P], part[:, n * 512:(n + 1) * 512], start=(p == 0), stop=(p == 1))
                mm.then_inc(sc_pe, 1)

            def body(j):
                later = not isinstance(j, int)
                pe.wait_ge(xgh, j + 1)
                pe.wait_ge(xgl, j + 1)
                if later or j >= 1:
                    pe.wait_ge(swi, 6 * j - 4)
                for n in range(4):
                    pe.matmul(banks[n], BL[:, :], b1s[:, n * 512:(n + 1) * 512], start=True, stop=False)
                for u in range(W1U):
                    up(j, u)
                    if u == 2:
                        if later:
                            scatter_transposes(j - 2)
                        for t in range(TT):
                            mm = pe.matmul(banks[7][:, S:S + 1], SG[:, t, :].bitcast(F32), gi[:, t, bass.ds(j, 1)],
                                           start=(t == 0), stop=(t == 1))
                        mm.then_inc(st_pe, 1)
                    if later and u == 4:
                        pe.wait_ge(atl, j)
                        pe.wait_ge(yh, j - 1)
                        pe.wait_ge(yl, j - 1)
                        pe.wait_ge(st_act, j - 1)
                        scatter(j - 2, 0)
                        pe.wait_ge(slw, j + 1)
                        scatter(j - 2, 1)
                    if later and u == 6:
                        for q in (2, 3):
                            pe.wait_ge(sc_add, 4 * (j - 2) + (q - 1))
                            scatter(j - 2, q)
                if later:
                    pe.wait_ge(sc_add, 4 * (j - 1))
                else:
                    pe.wait_ge(slw, j + 1)
                    if j == 1:
                        pe.wait_ge(atl, j)
                gather(j + 1)
                if later or j >= 1:
                    pe.wait_ge(ath, j)
                    pe.wait_ge(atl, j)
                    if later:
                        pe.wait_ge(yl, j - 1)
                    for v in range(W2U):
                        down(j, W1U + v, v, W1U + v in NATIVE)
                pe.wait_ge(swi, 6 * (j + 1))
                pe.wait_ge(xgh, j + 2)
                for c in range(4):
                    mm = pe.transpose(banks[6][:, c * P:(c + 1) * P], act_t[:, c * P:(c + 1) * P], ident)
                mm.then_inc(tr_pe, 1)

            for g in ("out0", "out1"):
                pe.wait_ge(pair_sem(g), GI[g] // 2 + 1)
            for q in range(4):
                in_sbuf(pe, ("b2", q // 2, q % 2))
            pe.wait_ge(xh_done, TT)
            pe.wait_ge(xl_done, TT)
            n_items = number_of_items(pe)
            gather(0)
            pe.wait_ge(b1h, 1)
            pe.wait_ge(b1l, 1)
            pe.wait_ge(zeroed, 2)
            body(0)
            body(1)
            with pe.Fori(2, n_items) as j:
                body(j)
            j = n_items
            pe.wait_ge(xgl, j + 1)
            scatter_transposes(j - 2).then_inc(st_pe, 1)
            pe.wait_ge(ath, j)
            pe.wait_ge(atl, j)
            pe.wait_ge(yl, j - 1)
            for v in range(W2U):
                down(j, v, v, True)
            pe.wait_ge(yh, j - 1)
            pe.wait_ge(st_act, j - 1)
            for q in range(4):
                if q >= 2:
                    pe.wait_ge(sc_add, 4 * (j - 2) + (q - 1))
                scatter(j - 2, q)
            pe.wait_ge(sc_add, 4 * (j - 1))
            scatter_transposes(j - 1).then_inc(st_pe, 1)
            pe.wait_ge(yh, j)
            pe.wait_ge(yl, j)
            pe.wait_ge(st_act, j)
            for q in range(4):
                if q >= 2:
                    pe.wait_ge(sc_add, 4 * (j - 1) + (q - 1))
                scatter(j - 1, q)


NAMES = ["x", "mem", "g_mix", "w_in", "b_gate", "g_ret_out", "g_moba_q", "g_moba_k", "g_mem", "w_mem_kv", "g_mem_q", "g_mem_k",
         "w_br_ret", "w_br_moba", "w_br_mem", "w_out", "g_ffn", "w_router", "b_router", "w_mlp1", "b_mlp1", "w_mlp2", "b_mlp2"]


def kernel(x, mem, g_mix, w_in, b_gate, g_ret_out, g_moba_q, g_moba_k, g_mem, w_mem_kv, g_mem_q, g_mem_k, w_br_ret, w_br_moba,
           w_br_mem, w_out, g_ffn, w_router, b_router, w_mlp1, b_mlp1, w_mlp2, b_mlp2):
    import numpy as np
    import concourse.bacc as bacc
    from concourse.bass_utils import run_bass_kernel_spmd

    given = dict(zip(NAMES, (x, mem, g_mix, w_in, b_gate, g_ret_out, g_moba_q, g_moba_k, g_mem, w_mem_kv, g_mem_q, g_mem_k,
                             w_br_ret, w_br_moba, w_br_mem, w_out, g_ffn, w_router, b_router, w_mlp1, b_mlp1, w_mlp2, b_mlp2)))
    arrays = {n: np.ascontiguousarray(v) for n, v in given.items()}
    cols = [arrays[n][0].reshape(KC, P).T for n in ("g_mix", "g_mem")]
    cols += [np.tile(arrays[n][0], P // arrays[n].shape[1])[:, None] for n in ("g_moba_q", "g_moba_k", "g_mem_q", "g_mem_k", "g_ret_out")]
    arrays["gains"] = np.ascontiguousarray(np.concatenate(cols, 1))
    for n in ("g_mix", "g_mem", "g_moba_q", "g_moba_k", "g_mem_q", "g_mem_k", "g_ret_out"):
        del arrays[n]
    arrays["decay"], arrays["alibi"], arrays["misc"] = host_constants()
    nc = bacc.Bacc("TRN2", target_bir_lowering=False, num_devices=1)
    aps = {n: nc.dram_tensor(f"in_{n}", v.shape, mybir.dt.from_np(v.dtype), kind="ExternalInput").ap() for n, v in arrays.items()}
    out = nc.dram_tensor("out", (1, S, D), F32, kind="ExternalOutput").ap()
    build(nc, aps, out)
    r = run_bass_kernel_spmd(nc, [{f"in_{n}": v for n, v in arrays.items()}], core_ids=[0])
    return r.results[0]["out"]
```

```python
import concourse.bass as bass
from concourse import mybir
from contextlib import ExitStack

F32 = mybir.dt.float32
F32R = mybir.dt.float32r
I32 = mybir.dt.int32
U32 = mybir.dt.uint32
ALU = mybir.AluOpType
ACT = mybir.ActivationFunctionType
AX = mybir.AxisListType

P = 128
S = 256
TT = S // P
D = 1024
KC = D // P
EPS = 1e-5
RET_H, RET_DK, RET_DV = 4, 64, 128
MOBA_H, MOBA_HD = 8, 64
MEM_H, MEM_HD = 4, 128
NE = 32
TOPK = 4
FF2 = 2 * D
LIMIT, ALPHA = 7.0, 1.702
SL = 64
MISC = 4 * P + 128
MAX_ITEMS = NE + (S * TOPK) // SL
G_COLS = 512

GROUPS = [("rqk", KC), ("mq", KC), ("mk", KC), ("cq", KC), ("ck", KC), ("rv", KC), ("mv", KC), ("cv", KC), ("rg", KC)]
GROUPS += [(f"gate{i}", KC) for i in range(6)]
BRANCH_ORDER = [(n, br) for n in range(2) for br in ("moba", "mem", "ret")]
GROUPS += [(f"br_{br}{n}", 4) for n, br in BRANCH_ORDER]
GROUPS += [(f"out{n}", KC) for n in range(2)]
GI = {name: i for i, (name, _) in enumerate(GROUPS)}
W_IN_COL = {"rqk": 0, "rv": 512, "rg": 1024, "mq": 1536, "mk": 2048, "mv": 2560, "cq": 3072,
            **{f"gate{i}": 3584 + 512 * i for i in range(6)}}
UNITS = [(g, hk) for g, (_, kc) in enumerate(GROUPS) for hk in range(kc // 4)]
N_MIX = len(UNITS)
UNITS_DONE = [sum(1 for (gg, _) in UNITS if gg <= g) for g in range(len(GROUPS))]

RING = 6
W1U, W2U = 8, 4
IU = W1U + W2U
NATIVE = {1, 4, 9}
NATIVE_0 = {3, 6}
HL = 3
SPLIT = [u for u in range(IU) if u not in NATIVE]
SPLIT_0 = [u for u in range(W1U) if u not in NATIVE_0]
W2_SPLIT = [u for u in SPLIT if u >= W1U]
W2_NATIVE = [u for u in NATIVE if u >= W1U]
assert len(SPLIT) % HL == 0 and IU % RING == 0 and len(SPLIT_0) == len(SPLIT) - len(W2_SPLIT) and SPLIT_0[:HL] == list(range(HL))

Q_GROUPS = ["rqk", "mq", "mk", "cq", "ck"]
HEADS = [("moba", h) for h in range(MOBA_H)] + [("mem", h) for h in range(MEM_H)]
NH = len(HEADS)
SLOTS = ["mv", "cv", "rg"] + [f"gate{i}" for i in range(6)]


def schedule():
    steps = [("task", "hT", 0, t, kk) for t in range(TT) for kk in range(2)]
    steps += [("group", "rqk")]
    steps += [("task", "hT", 1, t, kk) for t in range(TT) for kk in range(2)]
    steps += [("group", "mq")] + [("task", "qT", "rqk", t) for t in range(TT)]
    steps += [("group", "mk")] + [("task", "qT", "mq", t) for t in range(TT)] + [("task", "ret_s", 0), ("task", "ret_s", 1)]
    steps += [("group", "cq")] + [("task", "qT", "mk", t) for t in range(TT)]
    steps += [("group", "ck")] + [("task", "qT", "cq", t) for t in range(TT)]
    steps += [("group", "rv")] + [("task", "qT", "ck", t) for t in range(TT)]
    steps += [("task", "ret_o", 0), ("task", "ret_s", 2), ("task", "ret_s", 3)]
    for s, g in enumerate(SLOTS):
        steps += [("group", g)]
        if g == "mv":
            steps += [("task", "ret_o", 1)]
        for a in (2 * s - 4, 2 * s - 3):
            if 0 <= a < NH:
                steps += [("task", "pv", a)]
        for a in (2 * s - 2, 2 * s - 1):
            if 0 <= a < NH:
                steps += [("task", "pT", a)]
        for a in (2 * s, 2 * s + 1):
            if a < NH:
                steps += [("task", "sc", a)]
        if g == "gate3":
            steps += [("task", "oT", "moba", t) for t in range(TT)]
        if g == "gate4":
            steps += [("task", "oT", "ret", t) for t in range(TT)]
        if g == "gate5":
            steps += [("task", "oT", "mem", t) for t in range(TT)]
    for i, (n, br) in enumerate(BRANCH_ORDER):
        steps += [("group", f"br_{br}{n}")]
        if i == 4:
            steps += [("task", "yT", 0, t) for t in range(TT)]
    steps += [("task", "yT", 1, t) for t in range(TT)]
    steps += [("group", "out0")] + [("task", "xT", t, 0) for t in range(TT)]
    steps += [("group", "out1")] + [("task", "xT", t, 1) for t in range(TT)]
    steps += [("task", "pos")]
    return steps


LATE = [("cnt",), ("off",), ("tabT",), ("tab",)] + [("b2", t, n) for t in range(TT) for n in range(2)]
LATE_PE = {2: [("tab",)], 4: [LATE[4]], 5: [LATE[5]], 6: [LATE[6]], 7: [LATE[7]]}
LATE_DVE = {4: [("tab",)], 5: [LATE[4]], 7: LATE[5:8]}


NORMS = ["x", "mem", "mq", "mk", "cq", "ck", "ret0", "ret1", "x2"]
SQUARES = [2, 2, 1, 1, 1, 1, 1, 1, 4]
SUMS = [0, 0, 1, 1, 1, 1, 1, 1, 1]
ROUTE = ["lg0", "lg1", "max0", "max1", "mi0", "mi1", "nv", "if", "oh0", "oh1", "m0", "m1", "rse", "w4", "ow0", "ow1", "g0", "g1",
         "posm", "g3", "n", "off", "offr", "s1", "s2", "s3", "t1", "t2", "u1", "u2", "u3", "si", "sz",
         "posi", "gi", "bsel", "it"]
RI = {n: i + 1 for i, n in enumerate(ROUTE)}
STEPS = schedule()
TASKS = {s[1:]: n for n, s in enumerate([s for s in STEPS if s[0] == "task"])}
N_TASKS = len(TASKS)


def host_constants():
    import numpy as np
    i = np.arange(P, dtype=np.float64)[:, None]
    t = np.arange(S, dtype=np.float64)[None, :]
    diff = t - i
    decay = np.zeros((P, RET_H, 384))
    for h in range(RET_H):
        lg = np.log1p(-np.exp2(-5.0 - h))
        d = np.where(diff >= 0, np.exp(np.maximum(diff, 0) * lg), 0.0) * RET_DK ** -0.5
        decay[:, h, 0:S] = d
        decay[:, h, S:384] = d[:, 0:P]
    alibi = np.zeros((P, TT, S))
    for tt in range(TT):
        dist = (i + P * tt) - t
        alibi[:, tt, :] = np.where(dist >= 0, -dist, -1e33)
    misc = np.zeros((P, MISC))
    misc[:, 0:P] = np.eye(P)
    misc[:, P:2 * P] = (i < i.T)
    misc[:, 2 * P:3 * P] = 1.0
    misc[:, 3 * P:4 * P] = np.arange(P)[None, :] % SL
    misc[:, 4 * P:4 * P + 32] = np.arange(32)[None, :]
    misc[:, 4 * P + 32] = i[:, 0]
    misc[:, 4 * P + 33:4 * P + 36] = [SL, 2 * SL, 3 * SL]
    misc[:, 4 * P + 36] = EPS
    misc[0:NE, 4 * P + 64:4 * P + 128] = np.concatenate([np.eye(NE), np.eye(NE)], 1)
    misc[NE:2 * NE, 4 * P + 64:4 * P + 96] = np.eye(NE)
    f = np.float32
    return decay.reshape(P, -1).astype(f), alibi.reshape(P, -1).astype(f), misc.astype(f)


def build(nc, a, out):
    ctx = ExitStack()
    with ctx:
        def sem(name):
            return ctx.enter_context(nc.semaphore(name))

        def sb(name, shape, dt=F32, scope=ctx):
            return scope.enter_context(nc.sbuf_tensor(name, shape, dt))

        raw = [sb(f"raw{i}", [P, 2048]) for i in range(RING)]
        X = sb("X", [P, TT, D])
        hT = sb("hT", [P, KC, S])
        hx = sb("hx", [P, TT, D])
        mT = sb("mT", [P, KC, S])
        misc = sb("misc", [P, MISC])
        ident, before, ones, slotn = (misc[:, i * P:(i + 1) * P] for i in range(4))
        iota32 = misc[:, 4 * P:4 * P + 32]
        iotap = misc[:, 4 * P + 32:4 * P + 33]
        thresholds = misc[:, 4 * P + 33:4 * P + 36]
        eps = misc[:, 4 * P + 36:4 * P + 37]
        twice = misc[0:NE, 4 * P + 64:4 * P + 128]
        gffn = sb("gffn", [P, D])
        wr = sb("wr", [P, KC, NE])
        brt = sb("brt", [P, NE])
        gains = sb("gains", [P, 3 * KC + 5])
        gcol = gains[:, 0:2 * KC]
        fcol = gains[:, 2 * KC:3 * KC]
        qgain = gains[:, 3 * KC:]
        stat = sb("stat", [P, 3, 16 * len(NORMS)])
        smx = sb("smx", [P, 4, 2 * NH])
        spare = sb("spare", [1, 4])
        lg = sb("lg", [P, TT, NE])
        v8 = sb("v8", [P, TT, 8])
        i8 = sb("i8", [P, TT, 8], U32)
        i8f = sb("i8f", [P, TT, 8])
        nv = sb("nv", [P, TT])
        e4 = sb("e4", [P, TT, 4])
        se = sb("se", [P, 2 * TT])
        oh = sb("oh", [P, TT, 4, NE])
        ohw = sb("ohw", [P, TT, 4, NE])
        MG = sb("MG", [P, TT, NE])
        rt = sb("rt", [NE, 96])
        selw = sb("selw", [NE, 2, MAX_ITEMS])
        tabT = sb("tabT", [NE, 2, S])
        PG = sb("PG", [P, 2, TT, MAX_ITEMS])
        posi, gi = PG[:, 0, :, :], PG[:, 1, :, :]
        posm, G = posi[:, :, 0:NE], gi[:, :, 0:NE]
        bsel = sb("bsel", [64, MAX_ITEMS])
        items = sb("items", [1, MAX_ITEMS + 2], I32)

        mix = ExitStack()
        mem = sb("mem", [P, TT, D], scope=mix)
        V = {g: sb(f"V_{g}", [P, TT, 512], scope=mix) for g in ("rv", "mv", "cv", "rg")}
        gates = sb("gates", [P, TT, 3 * D], scope=mix)
        bg = sb("bg", [P, 3 * D], scope=mix)
        tq = [sb(f"tq{i}", [P, TT, 512], scope=mix) for i in range(2)]
        qT = {g: sb(f"qT_{g}", [P, 4, S], scope=mix) for g in Q_GROUPS}
        PTs = sb("PTs", [P, 2048], scope=mix)
        PT = [PTs[:, i * 512:(i + 1) * 512] for i in range(4)]
        o = {br: sb(f"o_{br}", [P, TT, 512], scope=mix) for br in ("ret", "moba", "mem")}
        alibi = sb("alibi", [P, TT * S], scope=mix)
        mix.close()
        probs = [hx[:, i // 2, (i % 2) * 512:(i % 2) * 512 + 512] for i in range(4)]
        decay = gates[:, 1, 3 * D - RET_H * 384:3 * D]
        retS = [PT[i][:, 0:384] for i in range(2)]
        sq = gates[:, 0, 0:D]
        rgs = mem[:, 1, :].rearrange("p (t n) -> p t n", t=TT)
        tmp = V["rv"]
        oT = {"ret": tq[0][:, :, :].rearrange("p a (b s) -> p (a b) s", s=S),
              "moba": tq[1][:, :, :].rearrange("p a (b s) -> p (a b) s", s=S),
              "mem": mem[:, 0, :].rearrange("p (c s) -> p c s", s=S)}
        y = hx
        b2s = o["moba"][0:NE, :, :].rearrange("p t n -> p (t n)")
        b1raw = PTs[0:64, :]

        hi = [sb(f"hi{i}", [P, 2048], F32R) for i in range(HL)]
        lo = [sb(f"lo{i}", [P, 2048], F32R) for i in range(HL)]
        xth = sb("xth", [P, TT, D], F32R)
        xtl = sb("xtl", [P, TT, D], F32R)
        XG = sb("XG", [P, KC, 2 * SL], F32R)
        b1s = sb("b1s", [P, FF2], F32R)
        AT = sb("AT", [P, KC, 2, SL], F32R)
        YH = sb("YH", [P, D], F32R)
        YL = sb("YL", [P, D], F32R)
        SG = sb("SG", [P, TT, 2 * SL], F32R)
        SS = sb("SS", [P, TT, 2 * SL], F32R)
        ST = sb("ST", [P, S], F32R)
        BL = sb("BL", [P, 2 * SL], F32R)
        slotw = sb("slotw", [P, 1])
        HB = mT[:, 0:4, :].rearrange("p k s -> p (k s)")
        HS = mT[:, 4:8, :].rearrange("p k s -> p (k s)")
        hview = hT[:, :, :].rearrange("p k s -> p (k s)")
        glu, lin, sig, act_t = (hview[:, i * 512:(i + 1) * 512] for i in range(4))

        PS = ctx.enter_context(nc.psum_tensor("PS", [P, 4096], F32))
        banks = [PS[:, i * 512:(i + 1) * 512] for i in range(8)]
        pair = [PS[:, i * 1024:(i + 1) * 1024].rearrange("p (t n) -> p t n", t=TT) for i in range(2)]

        def bank(key):
            return banks[4 + TASKS[key] % 4]

        raw_in = [sem(f"raw_in{i}") for i in range(RING)]
        x_half = [sem(f"x_half{t}") for t in range(TT)]
        mem_in, const_in, table_in, bcast_in, b1_in, b2_in = (sem(n) for n in ("mem_in", "const_in", "table_in", "bcast_in", "b1_in", "b2_in"))
        unit_used = sem("unit_used")
        task_done = sem("task_done")
        pair_free = [sem(f"pair_free{i}") for i in range(2)]
        bank_read = [sem(f"bank_read{i}") for i in range(4)]
        sq_done, sd_done = sem("sq_done"), sem("sd_done")
        rs_done = sem("rs_done")
        ss_done = sem("ss_done")
        hx_done = sem("hx_done")
        max_done = sem("max_done")
        exp_done = sem("exp_done")
        rcp_done = sem("rcp_done")
        sig_done = sem("sig_done")
        y_done = sem("y_done")
        x2_done = sem("x2_done")
        silu_done = sem("silu_done")
        xt_done = sem("xt_done")
        row0_done, logits_done = sem("row0_done"), sem("logits_done")
        late_done = sem("late_done")
        late_read = [sem(f"late_read{i}") for i in range(2)]
        warm = sem("warm")
        xh_done, xl_done = sem("xh_done"), sem("xl_done")
        rout = sem("rout")
        rexp = sem("rexp")
        b1h, b1l = sem("b1h"), sem("b1l")
        zeroed = sem("zeroed")
        hi_done, lo_done = sem("hi_done"), sem("lo_done")
        hl_used = sem("hl_used")
        nat_used = sem("nat_used")
        sg_done = sem("sg_done")
        ss_mat = sem("ss_mat")
        st_pe, st_act, slw = sem("st_pe"), sem("st_act"), sem("slw")
        ga_pe, xgh, xgl = sem("ga_pe"), sem("xgh"), sem("xgl")
        hb_act = sem("hb_act")
        swi = sem("swi")
        sgm = sem("sgm")
        tr_pe, ath, atl = sem("tr_pe"), sem("ath"), sem("atl")
        yh, yl = sem("yh"), sem("yl")
        sc_pe, sc_add = sem("sc_pe"), sem("sc_add")
        out_dma = sem("out_dma")

        N_CONST, N_TABLE, N_BCAST = 2, 2, 4

        def sigmoid_gate(act, i):
            act.wait_ge(pair_sem(f"gate{i}"), GI[f"gate{i}"] // 2 + 1)
            act.activation(gates[:, :, 512 * i:512 * i + 512], gates[:, :, 512 * i:512 * i + 512], ACT.Sigmoid).then_inc(sig_done, 1)

        def raw_at(j, u):
            if isinstance(j, int) and j == 0:
                return (N_MIX + u) % RING, (N_MIX + u) // RING + 1
            n = N_MIX + W1U - IU + u
            return n % RING, j * (IU // RING) + (n // RING + 1)

        def split_count(j, u):
            if isinstance(j, int) and j == 0:
                return sum(1 for x in SPLIT_0 if x <= u)
            return j * len(SPLIT) + (sum(1 for x in SPLIT if x <= u) - len(W2_SPLIT))

        def native_count(j, u):
            if isinstance(j, int) and j == 0:
                return sum(1 for x in NATIVE_0 if x <= u)
            return j * len(NATIVE) + (sum(1 for x in NATIVE if x <= u) - len(W2_NATIVE))

        def hl_slot(j, u):
            if isinstance(j, int) and j == 0:
                return SPLIT_0.index(u) % HL
            return (SPLIT.index(u) - len(W2_SPLIT)) % HL

        def native(j, u):
            return u in (NATIVE_0 if isinstance(j, int) and j == 0 else NATIVE)

        def unit_done(eng, j, u):
            if native(j, u):
                eng.wait_ge(nat_used, native_count(j, u))
            else:
                eng.wait_ge(hl_used, split_count(j, u))

        def in_sbuf(eng, key):
            n = TASKS[key]
            eng.wait_ge(bank_read[n % 4], n // 4 + 1)

        def late_in_sbuf(eng, key):
            n = LATE.index(key)
            eng.wait_ge(late_read[n % 2], n // 2 + 1)

        def late_bank(key):
            return banks[4 + LATE.index(key) % 2]

        def read_sem(key):
            return bank_read[TASKS[key] % 4]

        def pair_sem(g):
            return pair_free[GI[g] % 2]

        def number_of_items(eng):
            late_in_sbuf(eng, ("off",))
            return eng.value_load(items[0:1, MAX_ITEMS:MAX_ITEMS + 1], min_val=0, max_val=MAX_ITEMS - NE - 1) + NE

        block = ctx.enter_context(nc.Block())

        @block.sync
        def _(sp):
            for t in range(TT):
                sp.dma_start(X[:, t, :], a["x"][0, t * P:(t + 1) * P, :]).then_inc(x_half[t], 16)

            def mixer_source(g, hk):
                name = GROUPS[g][0]
                if name in W_IN_COL:
                    w, c = a["w_in"][0], W_IN_COL[name]
                elif name in ("ck", "cv"):
                    w, c = a["w_mem_kv"][0], 512 * (name == "cv")
                elif name.startswith("br_"):
                    w, c = a[{"ret": "w_br_ret", "moba": "w_br_moba", "mem": "w_br_mem"}[name[3:-1]]][0], 512 * int(name[-1])
                else:
                    w, c = a["w_out"][0], 512 * int(name[-1])
                return w[512 * hk:512 * hk + 512, c:c + 512].rearrange("(k p) n -> p k n", p=P)

            for m, (g, hk) in enumerate(UNITS):
                if m >= RING:
                    sp.wait_ge(unit_used, m - RING + 1)
                sp.dma_start(raw[m % RING][:, :].rearrange("p (k n) -> p k n", k=4),
                             mixer_source(g, hk)).then_inc(raw_in[m % RING], 16)
                if m == 1:
                    sp.dma_start(mem[:, :, :], a["mem"].rearrange("o (t p) d -> p (o t) d", p=P)).then_inc(mem_in, 16)

            def slot_free(j, u):
                if isinstance(j, int) and j == 0 and u < RING:
                    sp.wait_ge(unit_used, N_MIX - RING + u + 1)
                    return
                if isinstance(j, int) and j == 1 and u < RING:
                    pj, pu = 0, W1U - RING + u
                elif u >= RING:
                    pj, pu = j, u - RING
                else:
                    pj, pu = j - 1, u + IU - RING
                if native(pj, pu):
                    sp.wait_ge(nat_used, native_count(pj, pu))
                else:
                    sp.wait_ge(hi_done, split_count(pj, pu))
                    sp.wait_ge(lo_done, split_count(pj, pu))

            w1, w2 = a["w_mlp1"][0], a["w_mlp2"][0]

            def load_w1(j, e):
                for u in range(W1U):
                    slot_free(j, u)
                    slot, _ = raw_at(j, u)
                    sp.dma_start(raw[slot][:, :], w1[e, u * P:(u + 1) * P, :].rearrange("e p n -> p (e n)"))\
                        .then_inc(raw_in[slot], 16)

            def load_w2(j, e, first):
                for v in range(W2U):
                    slot_free(j, first + v)
                    slot, _ = raw_at(j, first + v)
                    sp.dma_start(raw[slot][:, :].rearrange("p (k n) -> p k n", k=2),
                                 w2[e, 2 * v * P:(2 * v + 2) * P, :].rearrange("e (k p) n -> p (e k) n", p=P))\
                        .then_inc(raw_in[slot], 16)

            load_w1(0, slice(0, 1))
            def expert(j):
                return bass.ds(sp.value_load(items[0:1, bass.ds(j, 1)], min_val=0, max_val=NE - 1), 1)

            load_w1(1, slice(1, 2))
            load_w2(1, slice(0, 1), W1U)
            late_in_sbuf(sp, ("tab",))
            n_items = number_of_items(sp)
            with sp.Fori(2, n_items) as j:
                load_w1(j, expert(j))
                load_w2(j, expert(j - 1), W1U)
            load_w2(n_items, expert(n_items - 1), 0)
            sp.wait_ge(sc_add, n_items * 4)
            sp.dma_start(out.rearrange("o (t p) d -> p (o t) d", p=P), X[:, :, :]).then_inc(out_dma, 16)
            sp.wait_ge(out_dma, 16)

        @block.gpsimd
        def _(pool):
            pool.wait_ge(unit_used, 4)
            pool.dma_start(bg[:, :], a["b_gate"][0:1, :].to_broadcast([P, 3 * D])).then_inc(bcast_in, 16)
            pool.dma_start(gffn[:, :], a["g_ffn"][0:1, :].to_broadcast([P, D])).then_inc(bcast_in, 16)
            pool.dma_start(brt[:, :], a["b_router"][0:1, :].to_broadcast([P, NE])).then_inc(bcast_in, 16)
            pool.dma_start(wr[:, :, :], a["w_router"][0].rearrange("(k p) e -> p k e", p=P)).then_inc(bcast_in, 16)
            pool.wait_ge(pair_sem("gate5"), GI["gate5"] // 2 + 1)
            for t in range(TT):
                pool.wait_ge(task_done, TASKS[("oT", "moba", t)] + 1)
            pool.dma_start(b2s, a["b_mlp2"][0]).then_inc(b2_in, 16)
            pool.dma_start(bsel[:, 0:NE], a["misc"][0:64, 4 * P + 64:4 * P + 64 + NE]).then_inc(b2_in, 16)
            pool.memset(b1s[64:P, :].bitcast(F32), 0.0).then_inc(zeroed, 1)
            pool.wait_ge(silu_done, 2)
            pool.wait_ge(y_done, 4)
            pool.wait_ge(b1l, 1)
            pool.wait_ge(zeroed, 1)
            pool.memset(BL[:, :].bitcast(F32), 0.0).then_inc(zeroed, 1)
            for t in range(TT):
                pool.wait_ge(xh_done, t + 1)
                if t:
                    pool.wait_ge(xl_done, t)
                pool.tensor_tensor(xtl[:, t, :], hx[:, t, :], xth[:, t, :].bitcast(F32), ALU.subtract).then_inc(xl_done, 1)

        @block.scalar
        def _(act):
            act.dma_start(misc[:, :], a["misc"]).then_inc(const_in, 16)
            act.dma_start(gains[:, :], a["gains"]).then_inc(const_in, 16)
            def roots(name, count, n):
                i = NORMS.index(name)
                act.wait_ge(sq_done, sum(SQUARES[:i + 1]))
                if SUMS[i]:
                    act.wait_ge(ss_done, sum(SUMS[:i + 1]))
                act.activation(stat[:, 1, 16 * i:16 * i + count], stat[:, 0, 16 * i:16 * i + count], ACT.Sqrt,
                               bias=eps, scale=1.0 / n).then_inc(sd_done, 1)

            def row_squares(name, src):
                i = NORMS.index(name)
                for t in range(TT):
                    if sum(SQUARES[:i]) + t:
                        act.wait_ge(sq_done, sum(SQUARES[:i]) + t)
                    act.activation(sq, src[:, t, :], ACT.Square,
                                   accum_out=stat[:, 0, 16 * i + t:16 * i + t + 1]).then_inc(sq_done, 1)
                roots(name, TT, D)

            def load_table(func, column):
                act.activation(spare[:, column:column + 1], spare[:, 0:1], func)

            def high(j, u):
                if native(j, u):
                    return
                slot, uses = raw_at(j, u)
                act.wait_ge(raw_in[slot], uses * 16)
                if not (isinstance(j, int) and split_count(j, u) <= HL):
                    act.wait_ge(hl_used, split_count(j, u) - HL)
                act.activation(hi[hl_slot(j, u)][:, :], raw[slot][:, :], ACT.Copy).then_inc(hi_done, 1)

            act.wait_ge(warm, 1)
            load_table(ACT.Sqrt, 1)
            for t in range(TT):
                act.wait_ge(x_half[t], 16)
                if t:
                    act.wait_ge(sq_done, t)
                act.activation(sq, X[:, t, :], ACT.Square, accum_out=stat[:, 0, t:t + 1]).then_inc(sq_done, 1)
            act.wait_ge(const_in, 16 * N_CONST)
            roots("x", TT, D)
            act.wait_ge(mem_in, 16)
            row_squares("mem", mem)
            act.dma_start(decay, a["decay"]).then_inc(table_in, 16)
            act.dma_start(alibi[:, :], a["alibi"]).then_inc(table_in, 16)

            for step in STEPS:
                if step[0] == "group":
                    g = step[1]
                    P2 = pair[GI[g] % 2]
                    if g in ("mq", "mk", "cq", "ck"):
                        act.wait_ge(unit_used, UNITS_DONE[GI[g]])
                        act.wait_ge(sq_done, sum(SQUARES[:NORMS.index(g)]))
                        act.activation(sq.rearrange("p (t n) -> p t n", t=TT), P2, ACT.Square).then_inc(sq_done, 1)
                        heads = TT * (MOBA_H if g[0] == "m" else MEM_H)
                        roots(g, heads, MOBA_HD if g[0] == "m" else MEM_HD)
                    elif g in V:
                        act.wait_ge(unit_used, UNITS_DONE[GI[g]])
                        act.activation(V[g][:, :, :], P2, ACT.Copy).then_inc(pair_sem(g), 1)
                    elif g == "gate3":
                        act.wait_ge(pair_sem("rg"), GI["rg"] // 2 + 1)
                        act.activation(rgs, V["rg"][:, :, :], ACT.Sigmoid).then_inc(sig_done, 1)
                        for i in range(4):
                            sigmoid_gate(act, i)
                    elif g in ("gate4", "gate5"):
                        sigmoid_gate(act, int(g[-1]))
                else:
                    key = step[1:]
                    kind, b = key[0], bank(key)
                    if kind == "ret_o":
                        hp = key[1]
                        act.wait_ge(task_done, TASKS[key] + 1)
                        act.wait_ge(sq_done, sum(SQUARES[:NORMS.index(f"ret{hp}")]))
                        act.activation(sq[:, 0:512], b, ACT.Square).then_inc(sq_done, 1)
                        roots(f"ret{hp}", 2 * TT, RET_DV)
                    elif kind == "sc":
                        h = key[1]
                        act.wait_ge(max_done, 2 * h + 2)
                        pr = probs[h % 4]
                        if HEADS[h][0] == "mem" and h >= 4:
                            act.wait_ge(task_done, TASKS[("pT", h - 4)] + 1)
                        for it in range(TT):
                            cols = slice(it * S, (it + 1) * S)
                            act.activation(pr[:, cols], (pr if HEADS[h][0] == "moba" else b)[:, cols], ACT.Exp,
                                           bias=smx[:, 1, 2 * h + it:2 * h + it + 1],
                                           accum_out=smx[:, 2, 2 * h + it:2 * h + it + 1]).then_inc(exp_done, 1)
                    elif kind == "pT":
                        h = key[1]
                        n = 384 if HEADS[h][0] == "moba" else 512
                        act.wait_ge(task_done, TASKS[key] + 1)
                        if h >= 4:
                            act.wait_ge(task_done, TASKS[("pv", h - 4)] + 1)
                        act.activation(PT[h % 4][:, 0:n], b[:, 0:n], ACT.Copy).then_inc(read_sem(key), 1)
                    elif kind == "oT" and key[1] != "ret":
                        act.wait_ge(task_done, TASKS[key] + 1)
                        act.activation(oT[key[1]][:, :, key[2] * P:(key[2] + 1) * P], b.rearrange("p (c s) -> p c s", s=P),
                                       ACT.Copy).then_inc(read_sem(key), 1)
                    elif kind == "yT":
                        n, t = key[1:]
                        act.wait_ge(task_done, TASKS[key] + 1)
                        act.activation(mT[:, 4 * n:4 * n + 4, t * P:(t + 1) * P], b.rearrange("p (c s) -> p c s", s=P),
                                       ACT.Copy).then_inc(read_sem(key), 1)
                    elif kind == "xT":
                        t, kk = key[1:]
                        act.wait_ge(task_done, TASKS[key] + 1)
                        if t == 0:
                            for c in range(4):
                                ins = act.activation(hT[:, 4 * kk + c, t * P:(t + 1) * P], b[:, c * P:(c + 1) * P], ACT.Copy,
                                                     scale=fcol[:, 4 * kk + c:4 * kk + c + 1])
                            ins.then_inc(read_sem(key), 1)
                        if (t, kk) == (1, 1):
                            act.wait_ge(ss_done, sum(SUMS))
                            roots("x2", TT, D)
                            load_table(ACT.Exp, 2)
                            for i in range(TT):
                                act.wait_ge(xt_done, i + 1)
                                act.activation(xth[:, i, :], hx[:, i, :], ACT.Copy).then_inc(xh_done, 1)
                            high(0, 1)
                    elif kind == "pos":
                        act.wait_ge(rout, RI["nv"])
                        for t in range(TT):
                            act.activation(e4[:, t, :], v8[:, t, 0:4], ACT.Exp, bias=nv[:, t:t + 1],
                                           accum_out=se[:, t:t + 1]).then_inc(rexp, 1)
                        load_table(ACT.Sigmoid, 3)
                        high(0, 2)
                if step == ("group", "br_moba0"):
                    for half in range(2):
                        act.dma_start(b1raw[32 * half:32 * half + 32, :], a["b_mlp1"][0]).then_inc(b1_in, 16)
                if step == ("group", "br_mem1"):
                    load_table(ACT.Sqrt, 1)
                    act.wait_ge(b1_in, 32)
                    act.activation(b1s[0:64, :], b1raw, ACT.Copy).then_inc(b1h, 1)
                if step in (("group", "out0"), ("group", "out1")):
                    n = int(step[1][-1])
                    for t in range(TT):
                        act.wait_ge(x2_done, TT * n + t + 1)
                        act.wait_ge(sq_done, sum(SQUARES[:-1]) + TT * n + t)
                        act.activation(y[:, t, 512 * n:512 * n + 512], X[:, t, 512 * n:512 * n + 512], ACT.Square,
                                       accum_out=stat[:, 1, 8 + TT * n + t:9 + TT * n + t]).then_inc(sq_done, 1)
                    if n == 0:
                        act.wait_ge(y_done, 4)
                        high(0, 0)

            def gathered(i):
                act.wait_ge(ga_pe, i * 2 + 1)
                act.activation(XG[:, :, 0:SL], banks[6].rearrange("p (k s) -> p k s", s=SL), ACT.Copy).then_inc(xgh, 1)

            def output_high(i):
                act.activation(YH[:, :], PS[:, 2048:3072], ACT.Copy).then_inc(yh, 1)

            def scatter_matrix(i):
                act.activation(ST[:, :], banks[7][:, 0:S], ACT.Copy).then_inc(st_act, 1)

            def body(j):
                later = not isinstance(j, int)
                for u in range(W1U):
                    if later or j or u >= HL:
                        high(j, u)
                    if u == 0 and (later or j >= 1):
                        act.wait_ge(tr_pe, j)
                        act.activation(AT[:, :, 0, :].rearrange("p (h c) s -> p h c s", h=2),
                                       banks[6].rearrange("p (c h s) -> p h c s", h=2, s=SL), ACT.Copy).then_inc(ath, 1)
                    if u == 1 and later:
                        unit_done(act, j - 1, IU - 1)
                        output_high(j - 2)
                    if u == 3:
                        act.wait_ge(st_pe, j + 1)
                        if later:
                            scatter_matrix(j - 2)
                        if later or j >= 1:
                            act.wait_ge(swi, 6 * j)
                        act.activation(slotw[:, :], banks[7][:, S:S + 1], ACT.Copy).then_inc(slw, 1)
                if later or j >= 1:
                    for u in range(W1U, IU):
                        high(j, u)
                unit_done(act, j, W1U - 1)
                act.activation(HB[0:64, :], PS[64:P, 0:1024], ACT.Copy).then_inc(hb_act, 1)
                act.activation(HB[64:P, :], PS[0:64, 1024:2048], ACT.Copy).then_inc(hb_act, 1)
                gathered(j + 1)
                act.wait_ge(swi, 6 * j + 3)
                act.activation(sig, glu, ACT.Sigmoid, scale=ALPHA).then_inc(sgm, 1)

            gathered(0)
            body(0)
            body(1)
            n_items = number_of_items(act)
            with act.Fori(2, n_items) as j:
                body(j)
            j = n_items
            act.wait_ge(tr_pe, j)
            act.activation(AT[:, :, 0, :].rearrange("p (h c) s -> p h c s", h=2),
                           banks[6].rearrange("p (c h s) -> p h c s", h=2, s=SL), ACT.Copy).then_inc(ath, 1)
            unit_done(act, j - 1, IU - 1)
            output_high(j - 2)
            act.wait_ge(st_pe, j + 1)
            scatter_matrix(j - 2)
            act.wait_ge(nat_used, native_count(j - 1, IU - 1) + W2U)
            act.wait_ge(sc_pe, 4 * (j - 1))
            output_high(j - 1)
            act.wait_ge(st_pe, j + 2)
            scatter_matrix(j - 1)

        @block.vector
        def _(dve):
            def linked(ins, s, value):
                ins.then_inc(s, 1)
                dve.wait_ge(s, value)

            def reciprocal_roots(name, count):
                i = NORMS.index(name)
                dve.wait_ge(sd_done, i + 1)
                linked(dve.reciprocal(stat[:, 2, 16 * i:16 * i + count], stat[:, 1, 16 * i:16 * i + count]), rs_done, i + 1)
                return stat[:, 2, 16 * i:16 * i + count]

            def row_norm(i, src, dst):
                r = reciprocal_roots(NORMS[i], TT)
                for t in range(TT):
                    dve.tensor_scalar(dst[:, t, :], src[:, t, :], r[:, t:t + 1], None, ALU.mult).then_inc(hx_done, 1)

            def low(j, u):
                if native(j, u):
                    return
                slot, _ = raw_at(j, u)
                dve.wait_ge(hi_done, split_count(j, u))
                dve.tensor_tensor(lo[hl_slot(j, u)][:, :], raw[slot][:, :], hi[hl_slot(j, u)][:, :].bitcast(F32), ALU.subtract)\
                    .then_inc(lo_done, 1)

            dve.memset(spare[:, :], 1.0).then_inc(warm, 1)
            row_norm(0, X, hx)
            dve.wait_ge(const_in, 16 * N_CONST)
            for step in STEPS:
                if step[0] == "group":
                    g = step[1]
                    P2 = pair[GI[g] % 2]
                    free = pair_sem(g)
                    if g == "rqk":
                        row_norm(1, mem, mem)
                        dve.wait_ge(unit_used, UNITS_DONE[GI[g]])
                        dve.tensor_copy(tq[0][:, :, :], P2).then_inc(free, 1)
                    elif g in ("mq", "mk", "cq", "ck"):
                        i, hd = NORMS.index(g), (MOBA_HD if g[0] == "m" else MEM_HD)
                        heads = 512 // hd
                        dve.wait_ge(sq_done, sum(SQUARES[:i + 1]))
                        dve.tensor_reduce(stat[:, 0, 16 * i:16 * i + TT * heads], sq.rearrange("p (g d) -> p g d", d=hd),
                                          AX.X, ALU.add).then_inc(ss_done, 1)
                        r = reciprocal_roots(g, TT * heads)
                        q = Q_GROUPS.index(g)
                        if q >= 2:
                            dve.wait_ge(task_done, TASKS[("qT", Q_GROUPS[q - 2], 1)] + 1)
                        dve.tensor_tensor(tq[q % 2][:, :, :].rearrange("p t (h d) -> p (t h) d", d=hd),
                                          P2.rearrange("p t (h d) -> p (t h) d", d=hd),
                                          r.rearrange("p (g o) -> p g o", o=1).to_broadcast([P, TT * heads, hd]),
                                          ALU.mult).then_inc(free, 1)
                    elif g.startswith("gate"):
                        i = int(g[-1])
                        dve.wait_ge(bcast_in, 16 * N_BCAST)
                        dve.wait_ge(unit_used, UNITS_DONE[GI[g]])
                        for t in range(TT):
                            ins = dve.tensor_tensor(gates[:, t, 512 * i:512 * i + 512], P2[:, t, :], bg[:, 512 * i:512 * i + 512], ALU.add)
                            if t:
                                ins.then_inc(free, 1)
                        if g == "gate4":
                            dve.wait_ge(sig_done, 1)
                            linked(dve.tensor_tensor(V["rg"][:, :, :], V["rg"][:, :, :], rgs, ALU.mult), silu_done, 1)
                            dve.tensor_tensor(o["ret"][:, :, :], o["ret"][:, :, :], V["rg"][:, :, :], ALU.mult).then_inc(silu_done, 1)
                    elif g.startswith("br_"):
                        n, br = int(g[-1]), g[3:-1]
                        gate = 2 * {"ret": 0, "moba": 1, "mem": 2}[br] + n
                        col = 512 * gate
                        half = slice(512 * n, 512 * n + 512)
                        dve.wait_ge(unit_used, UNITS_DONE[GI[g]])
                        dve.wait_ge(sig_done, gate + 2)
                        if br == BRANCH_ORDER[0][1]:
                            dve.tensor_tensor(y[:, :, half], P2, gates[:, :, col:col + 512], ALU.mult).then_inc(free, 1)
                        else:
                            linked(dve.tensor_tensor(tmp[:, :, :], P2, gates[:, :, col:col + 512], ALU.mult), free, GI[g] // 2 + 1)
                            k = 2 * n + (br == "ret") + 1
                            if k % 2:
                                first = f"br_{BRANCH_ORDER[0][1]}{n}"
                                dve.wait_ge(pair_sem(first), GI[first] // 2 + 1)
                            linked(dve.tensor_tensor(y[:, :, half], y[:, :, half], tmp[:, :, :], ALU.add), y_done, k)
                    elif g.startswith("out"):
                        n = int(g[-1])
                        half = slice(512 * n, 512 * n + 512)
                        for t in range(TT):
                            if n == 1 and t == 0:
                                dve.wait_ge(row0_done, 1)
                            else:
                                dve.wait_ge(unit_used, UNITS_DONE[GI[g]])
                            dve.tensor_tensor(X[:, t, half], X[:, t, half], P2[:, t, :], ALU.add).then_inc(x2_done, 1)
                        if n == 0:
                            dve.wait_ge(b1h, 1)
                            dve.tensor_tensor(b1s[32:64, :], b1raw[32:64, :], b1s[32:64, :].bitcast(F32), ALU.subtract)\
                                .then_inc(b1l, 1)
                            low(0, 0)
                    continue
                key = step[1:]
                kind, b = key[0], bank(key)
                done = read_sem(key)
                blocks = b.rearrange("p (c s) -> p c s", s=P)
                if kind == "hT":
                    src, t, kk = key[1:]
                    dve.wait_ge(task_done, TASKS[key] + 1)
                    c = src * KC + 4 * kk
                    dve.tensor_tensor((hT, mT)[src][:, 4 * kk:4 * kk + 4, t * P:(t + 1) * P], blocks,
                                      gcol[:, c:c + 4].rearrange("p (c o) -> p c o", o=1).to_broadcast([P, 4, P]),
                                      ALU.mult).then_inc(done, 1)
                elif kind == "qT":
                    g, t = key[1:]
                    dst = qT[g][:, :, t * P:(t + 1) * P]
                    dve.wait_ge(task_done, TASKS[key] + 1)
                    if g == "rqk":
                        dve.tensor_copy(dst, blocks).then_inc(done, 1)
                    else:
                        c = ("mq", "mk", "cq", "ck").index(g)
                        scale = {"mq": MOBA_HD ** -0.5, "cq": MEM_HD ** -0.5}.get(g, 1.0)
                        dve.tensor_scalar(dst, blocks, qgain[:, c:c + 1], scale, ALU.mult, ALU.mult).then_inc(done, 1)
                elif kind == "ret_s":
                    h = key[1]
                    dve.wait_ge(task_done, TASKS[key] + 1)
                    if h == 0:
                        dve.wait_ge(table_in, 16 * N_TABLE)
                    if h >= 2:
                        dve.wait_ge(task_done, TASKS[("ret_o", h // 2 - 1)] + 1)
                    dve.tensor_tensor(retS[h % 2], b[:, 0:384], decay[:, 384 * h:384 * h + 384], ALU.mult).then_inc(done, 1)
                elif kind == "ret_o":
                    hp = key[1]
                    i = NORMS.index(f"ret{hp}")
                    dve.wait_ge(sq_done, sum(SQUARES[:i + 1]))
                    dve.tensor_reduce(stat[:, 0, 16 * i:16 * i + 4], sq[:, 0:512].rearrange("p (g d) -> p g d", d=RET_DV),
                                      AX.X, ALU.add).then_inc(ss_done, 1)
                    r = reciprocal_roots(f"ret{hp}", 4)
                    dve.tensor_tensor(o["ret"][:, :, 256 * hp:256 * hp + 256].rearrange("p t (h d) -> p t h d", d=RET_DV),
                                      b.rearrange("p (t h d) -> p t h d", t=TT, d=RET_DV),
                                      r.rearrange("p (t h o) -> p t h o", t=TT, o=1).to_broadcast([P, TT, 2, RET_DV]),
                                      ALU.mult).then_inc(done, 1)
                elif kind == "sc":
                    h = key[1]
                    hh, moba = HEADS[h][1], HEADS[h][0] == "moba"
                    cols = slice(2 * h, 2 * h + 2)
                    dve.wait_ge(task_done, TASKS[key] + 1)
                    src = b
                    if moba:
                        if h >= 4:
                            dve.wait_ge(task_done, TASKS[("pT", h - 4)] + 1)
                        src = probs[h % 4]
                        dve.scalar_tensor_tensor(src, alibi[:, :], 2.0 ** (-8.0 * (hh + 1) / MOBA_H), b, ALU.mult, ALU.add)\
                            .then_inc(done, 1)
                        in_sbuf(dve, key)
                    linked(dve.tensor_reduce(smx[:, 0, cols], src.rearrange("p (t s) -> p t s", s=S), AX.X, ALU.max),
                           max_done, 2 * h + 1)
                    dve.tensor_scalar(smx[:, 1, cols], smx[:, 0, cols], -1.0, None, ALU.mult).then_inc(max_done, 1)
                    dve.wait_ge(exp_done, 2 * h + 2)
                    dve.reciprocal(smx[:, 3, cols], smx[:, 2, cols]).then_inc(rcp_done if moba else done, 1)
                elif kind == "pv":
                    h = key[1]
                    br, hh = HEADS[h]
                    hd = MOBA_HD if br == "moba" else MEM_HD
                    dve.wait_ge(task_done, TASKS[key] + 1)
                    if br == "moba":
                        dve.wait_ge(rcp_done, h + 1)
                    else:
                        in_sbuf(dve, ("sc", h))
                    dve.tensor_tensor(o[br][:, :, hh * hd:(hh + 1) * hd],
                                      b[:, 0:TT * hd].rearrange("p (t d) -> p t d", d=hd),
                                      smx[:, 3, 2 * h:2 * h + 2].rearrange("p (t o) -> p t o", o=1).to_broadcast([P, TT, hd]),
                                      ALU.mult).then_inc(done, 1)
                elif kind == "oT" and key[1] == "ret":
                    t = key[2]
                    dve.wait_ge(task_done, TASKS[key] + 1)
                    dve.tensor_scalar(oT["ret"][:, :, t * P:(t + 1) * P], blocks, qgain[:, 4:5], None, ALU.mult).then_inc(done, 1)
                elif kind == "xT":
                    t, kk = key[1:]
                    if t == 1:
                        dve.wait_ge(task_done, TASKS[key] + 1)
                        dve.tensor_tensor(hT[:, 4 * kk:4 * kk + 4, P:S], blocks,
                                          fcol[:, 4 * kk:4 * kk + 4].rearrange("p (c o) -> p c o", o=1).to_broadcast([P, 4, P]),
                                          ALU.mult).then_inc(done, 1)
                    if (t, kk) == (1, 1):
                        dve.wait_ge(sq_done, sum(SQUARES))
                        i = NORMS.index("x2")
                        dve.tensor_tensor(stat[:, 0, 16 * i:16 * i + TT], stat[:, 1, 8:8 + TT], stat[:, 1, 10:10 + TT], ALU.add)\
                            .then_inc(ss_done, 1)
                        r = reciprocal_roots("x2", TT)
                        for i in range(TT):
                            dve.scalar_tensor_tensor(hx[:, i, :], X[:, i, :], r[:, i:i + 1], gffn[:, :], ALU.mult, ALU.mult)\
                                .then_inc(xt_done, 1)
                elif kind == "pos":
                    r = stat[:, 2, 16 * NORMS.index("x2"):]
                    for t in range(TT):
                        dve.wait_ge(logits_done, t + 1)
                        dve.scalar_tensor_tensor(lg[:, t, :], pair[GI["out0"] % 2][:, t, 0:NE], r[:, t:t + 1], brt[:, :],
                                                 ALU.mult, ALU.add).then_inc(rout, 1)
                    dve.wait_ge(rout, RI["lg1"])
                    for t in range(TT):
                        dve.max(v8[:, t, :], lg[:, t, :]).then_inc(rout, 1)
                    dve.wait_ge(rout, RI["max1"])
                    for t in range(TT):
                        dve.max_index(i8[:, t, :], v8[:, t, :], lg[:, t, :]).then_inc(rout, 1)
                    dve.tensor_scalar(nv[:, :], v8[:, :, 0], -1.0, None, ALU.mult).then_inc(rout, 1)
                    dve.wait_ge(rout, RI["mi1"])
                    linked(dve.tensor_copy(i8f[:, :, :], i8[:, :, :]), rout, RI["if"])
                    for t in range(TT):
                        dve.tensor_tensor(oh[:, t, :, :], iota32.rearrange("p (o e) -> p o e", o=1).to_broadcast([P, 4, NE]),
                                          i8f[:, t, 0:4].rearrange("p (k o) -> p k o", o=1).to_broadcast([P, 4, NE]),
                                          ALU.is_equal).then_inc(rout, 1)
                    dve.wait_ge(rout, RI["oh1"])
                    for t in range(TT):
                        dve.tensor_reduce(MG[:, t, :], oh[:, t, :, :].rearrange("p k e -> p e k"), AX.X, ALU.add).then_inc(rout, 1)
                    dve.wait_ge(rexp, TT)
                    linked(dve.reciprocal(se[:, TT:2 * TT], se[:, 0:TT]), rout, RI["rse"])
                    linked(dve.tensor_tensor(e4[:, :, :], e4[:, :, :],
                                             se[:, TT:2 * TT].rearrange("p (t o) -> p t o", o=1).to_broadcast([P, TT, 4]), ALU.mult),
                           rout, RI["w4"])
                    for t in range(TT):
                        dve.tensor_tensor(ohw[:, t, :, :], oh[:, t, :, :],
                                          e4[:, t, :].rearrange("p (k o) -> p k o", o=1).to_broadcast([P, 4, NE]),
                                          ALU.mult).then_inc(rout, 1)
                    dve.wait_ge(rout, RI["ow1"])
                    for t in range(TT):
                        dve.tensor_reduce(G[:, t, :], ohw[:, t, :, :].rearrange("p k e -> p e k"), AX.X, ALU.add).then_inc(rout, 1)
                    dve.wait_ge(task_done, TASKS[key] + 1)
                    dve.scalar_tensor_tensor(posm, b[:, 0:TT * NE].rearrange("p (t e) -> p t e", t=TT), 1.0,
                                             MG[:, :, :], ALU.add, ALU.mult).then_inc(done, 1)
                    in_sbuf(dve, key)
                    dve.tensor_scalar(posm, posm, -1.0, None, ALU.add).then_inc(rout, 1)

            def gather_matrix(i):
                for t in range(TT):
                    dve.tensor_scalar(SG[:, t, :], slotn, posi[:, t, bass.ds(i, 1)], None, ALU.is_equal).then_inc(sg_done, 1)
                dve.tensor_scalar(BL[0:64, 0:SL], ones[0:64, 0:SL], bsel[:, bass.ds(i, 1)], None, ALU.mult).then_inc(sg_done, 1)

            def scatter_matrix(i):
                for t in range(TT):
                    dve.tensor_scalar(SS[:, t, :], slotn, posi[:, t, bass.ds(i, 1)], None, ALU.is_equal).then_inc(ss_mat, 1)

            def gathered(i):
                dve.wait_ge(ga_pe, i * 2 + 2)
                dve.tensor_copy(XG[:, :, SL:2 * SL], banks[7].rearrange("p (k s) -> p k s", s=SL)).then_inc(xgl, 1)

            def activations_low(j):
                dve.wait_ge(ath, j)
                dve.tensor_tensor(AT[:, :, 1, :].rearrange("p (h c) s -> p h c s", h=2),
                                  banks[6].rearrange("p (c h s) -> p h c s", h=2, s=SL),
                                  AT[:, :, 0, :].bitcast(F32).rearrange("p (h c) s -> p h c s", h=2), ALU.subtract).then_inc(atl, 1)

            def output_low(i):
                dve.wait_ge(yh, i + 1)
                dve.tensor_tensor(YL[:, :], PS[:, 2048:3072], YH[:, :].bitcast(F32), ALU.subtract).then_inc(yl, 1)

            def add(i, q):
                t, n = q // 2, q % 2
                dve.wait_ge(sc_pe, 4 * i + (q + 1))
                dve.tensor_tensor(X[:, t, 512 * n:512 * n + 512], X[:, t, 512 * n:512 * n + 512], banks[6 + q % 2], ALU.add)\
                    .then_inc(sc_add, 1)

            def late_task(key):
                kind, b, done = key[0], late_bank(key), late_read[LATE.index(key) % 2]
                if kind == "cnt":
                    dve.wait_ge(late_done, LATE.index(key) + 1)
                    dve.tensor_copy(rt[:, 0:1], b[0:NE, 0:1]).then_inc(done, 1)
                    late_in_sbuf(dve, key)
                    dve.wait_ge(rout, RI["posm"])
                    linked(dve.tensor_scalar(rt[:, 1:4], thresholds[0:NE, :], rt[:, 0:1], None, ALU.is_lt), rout, RI["g3"])
                    linked(dve.tensor_reduce(rt[:, 4:5], rt[:, 1:4], AX.X, ALU.add), rout, RI["n"])
                elif kind == "tabT":
                    dve.wait_ge(late_done, LATE.index(key) + 1)
                    dve.tensor_copy(tabT[:, :, :], b[0:NE, :].rearrange("p (a s) -> p a s", a=2)).then_inc(done, 1)
                elif kind == "off":
                    dve.wait_ge(late_done, LATE.index(key) + 1)
                    linked(dve.tensor_copy(rt[:, 5:6], b[0:NE, 0:1]), rout, RI["off"])
                    dve.tensor_copy(items[0:1, MAX_ITEMS:MAX_ITEMS + 1], b[0:1, 2:3]).then_inc(done, 1)
                    linked(dve.tensor_scalar(rt[:, 6:9], iota32[0:NE, 0:3], rt[:, 5:6], None, ALU.add), rout, RI["offr"])
                    sel = [rt[:, 16 + 16 * r:32 + 16 * r] for r in range(3)]
                    for r in range(3):
                        dve.tensor_scalar(sel[r], iota32[0:NE, 0:16], rt[:, 6 + r:7 + r], rt[:, 1 + r:2 + r], ALU.is_equal, ALU.mult)\
                            .then_inc(rout, 1)
                    dve.wait_ge(rout, RI["s3"])
                    linked(dve.tensor_tensor(selw[:, 0, NE:], sel[0], sel[1], ALU.add), rout, RI["t1"])
                    linked(dve.tensor_tensor(selw[:, 0, NE:], selw[:, 0, NE:], sel[2], ALU.add), rout, RI["t2"])
                    linked(dve.scalar_tensor_tensor(selw[:, 1, NE:], sel[1], 2.0, sel[0], ALU.mult, ALU.add), rout, RI["u1"])
                    linked(dve.scalar_tensor_tensor(selw[:, 1, NE:], sel[2], 3.0, selw[:, 1, NE:], ALU.mult, ALU.add), rout, RI["u2"])
                    dve.tensor_scalar(selw[:, 1, NE:], selw[:, 1, NE:], -float(SL), None, ALU.mult).then_inc(rout, 1)
                    dve.tensor_copy(selw[:, 0, 0:NE], ident[0:NE, 0:NE]).then_inc(rout, 1)
                    dve.memset(selw[:, 1, 0:NE], 0.0).then_inc(rout, 1)
                elif kind == "tab":
                    dve.wait_ge(late_done, LATE.index(key) + 1)
                    m = MAX_ITEMS - NE
                    dve.tensor_copy(posi[:, :, NE:], b[:, 0:2 * m].rearrange("p (t j) -> p t j", t=TT)).then_inc(rout, 1)
                    dve.tensor_copy(gi[:, :, NE:], b[:, 2 * m:4 * m].rearrange("p (t j) -> p t j", t=TT)).then_inc(rout, 1)
                    dve.tensor_copy(bsel[:, NE:], b[0:64, 4 * m:5 * m]).then_inc(rout, 1)
                    dve.tensor_copy(items[0:1, 0:NE], iota32[0:1, :]).then_inc(rout, 1)
                    dve.tensor_copy(items[0:1, NE:MAX_ITEMS], b[0:1, 5 * m:6 * m]).then_inc(done, 1)
                elif kind == "b2":
                    t, n = key[1:]
                    dve.wait_ge(late_done, LATE.index(key) + 1)
                    dve.tensor_tensor(X[:, t, 512 * n:512 * n + 512], X[:, t, 512 * n:512 * n + 512], b, ALU.add).then_inc(done, 1)

            def body(j):
                later = not isinstance(j, int)
                for u in range(W1U):
                    if later or j or u >= HL:
                        low(j, u)
                    if isinstance(j, int) and j == 0:
                        for key in LATE_DVE.get(u, []):
                            late_task(key)
                    if u == 0 and (later or j >= 1):
                        activations_low(j)
                    if u == 1 and later:
                        output_low(j - 2)
                        dve.wait_ge(st_pe, j)
                        scatter_matrix(j - 2)
                    if later and u in (5, 7):
                        for q in ((0, 1) if u == 5 else (2, 3)):
                            add(j - 2, q)
                dve.wait_ge(st_pe, j + 1)
                gather_matrix(j + 1)
                if later or j >= 1:
                    for u in range(W1U, IU):
                        low(j, u)
                dve.wait_ge(hb_act, 2 * j + 1)
                dve.tensor_tensor(HS[0:64, :], PS[0:64, 0:1024], HB[0:64, :], ALU.add).then_inc(swi, 1)
                dve.wait_ge(hb_act, 2 * j + 2)
                dve.tensor_tensor(HS[64:P, :], PS[64:P, 1024:2048], HB[64:P, :], ALU.add).then_inc(swi, 1)
                dve.wait_ge(swi, 6 * j + 2)
                dve.tensor_scalar(glu, HS[:, 0:1024:2], LIMIT, None, ALU.min).then_inc(swi, 1)
                dve.tensor_scalar(lin, HS[:, 1:1024:2], LIMIT, -LIMIT, ALU.min, ALU.max).then_inc(swi, 1)
                gathered(j + 1)
                dve.wait_ge(swi, 6 * j + 4)
                dve.scalar_tensor_tensor(lin, lin, 1.0, glu, ALU.add, ALU.mult).then_inc(swi, 1)
                dve.wait_ge(swi, 6 * j + 5)
                dve.wait_ge(sgm, j + 1)
                dve.wait_ge(slw, j + 1)
                dve.scalar_tensor_tensor(act_t, lin, slotw[:, 0:1], sig, ALU.mult, ALU.mult).then_inc(swi, 1)

            dve.wait_ge(rout, RI["posm"])
            dve.wait_ge(zeroed, 2)
            dve.wait_ge(b2_in, 32)
            gather_matrix(0)
            late_task(("cnt",))
            low(0, 1)
            low(0, 2)
            gathered(0)
            late_task(("off",))
            late_task(("tabT",))
            body(0)
            dve.wait_ge(rout, RI["bsel"])
            body(1)
            n_items = number_of_items(dve)
            with dve.Fori(2, n_items) as j:
                body(j)
            j = n_items
            activations_low(j)
            output_low(j - 2)
            dve.wait_ge(st_pe, j)
            scatter_matrix(j - 2)
            for q in range(4):
                add(j - 2, q)
            dve.wait_ge(st_pe, j + 1)
            scatter_matrix(j - 1)
            output_low(j - 1)
            for q in range(4):
                add(j - 1, q)

        @block.tensor
        def _(pe):
            unit = 0
            for step in STEPS:
                if step[0] == "group":
                    g = step[1]
                    gi_, kc = GI[g], dict(GROUPS)[g]
                    if g == "rqk":
                        src = hT
                        for t in range(TT):
                            for kk in range(2):
                                in_sbuf(pe, ("hT", 0, t, kk))
                    if g == "ck":
                        for t in range(TT):
                            for kk in range(2):
                                in_sbuf(pe, ("hT", 1, t, kk))
                    if g.startswith("br_"):
                        for t in range(TT):
                            in_sbuf(pe, ("oT", g[3:-1], t))
                    if g == "out0":
                        for n in range(2):
                            for t in range(TT):
                                in_sbuf(pe, ("yT", n, t))
                    src = mT if g in ("ck", "cv") or g.startswith("out") else oT[g[3:-1]] if g.startswith("br_") else hT
                    if gi_ >= 2:
                        pe.wait_ge(pair_free[gi_ % 2], gi_ // 2)
                    if g == "out1":
                        for t in range(TT):
                            for hk in range(2):
                                if t == 0:
                                    pe.wait_ge(raw_in[(unit + hk) % RING], 16 * ((unit + hk) // RING + 1))
                                w = raw[(unit + hk) % RING][:, :].rearrange("p (k n) -> p k n", k=4)
                                for kk in range(4):
                                    k = 4 * hk + kk
                                    mm = pe.matmul(pair[gi_ % 2][:, t, :], src[:, k, t * P:(t + 1) * P], w[:, kk, :],
                                                   start=(k == 0), stop=(k == kc - 1))
                                if t == 1:
                                    mm.then_inc(unit_used, 1)
                                elif hk == 1:
                                    mm.then_inc(row0_done, 1)
                        continue
                    for hk in range(kc // 4):
                        pe.wait_ge(raw_in[unit % RING], 16 * (unit // RING + 1))
                        w = raw[unit % RING][:, :].rearrange("p (k n) -> p k n", k=4)
                        for t in range(TT):
                            for kk in range(4):
                                k = 4 * hk + kk
                                mm = pe.matmul(pair[gi_ % 2][:, t, :], src[:, k, t * P:(t + 1) * P], w[:, kk, :],
                                               start=(k == 0), stop=(k == kc - 1))
                        mm.then_inc(unit_used, 1)
                        unit += 1
                    continue
                key = step[1:]
                kind, b, n = key[0], bank(key), TASKS[key]
                if n >= 4:
                    pe.wait_ge(bank_read[n % 4], n // 4)

                def transposes(src, rows=P, blocks=4):
                    for c in range(blocks):
                        mm = pe.transpose(b[0:P, c * P:(c + 1) * P], src(c), ident)
                    return mm

                if kind == "hT":
                    s, t, kk = key[1:]
                    pe.wait_ge(const_in, 16 * N_CONST)
                    pe.wait_ge(hx_done, 2 * s + t + 1)
                    mm = transposes(lambda c: (hx, mem)[s][:, t, (4 * kk + c) * P:(4 * kk + c + 1) * P])
                elif kind == "qT":
                    g, t = key[1:]
                    pe.wait_ge(pair_sem(g), GI[g] // 2 + 1)
                    mm = transposes(lambda c: tq[Q_GROUPS.index(g) % 2][:, t, c * P:(c + 1) * P])
                elif kind == "ret_s":
                    h = key[1]
                    po, c = 64 * (h % 2), h // 2
                    q, k = qT["rqk"][po:po + 64, c, :], qT["rqk"][po:po + 64, 2 + c, :]
                    for t in range(TT):
                        in_sbuf(pe, ("qT", "rqk", t))
                    pe.matmul(b[:, 0:S], k[:, 0:P], q, start=True, stop=True)
                    mm = pe.matmul(b[:, S:384], k[:, P:S], q[:, P:S], start=True, stop=True)
                elif kind == "ret_o":
                    hp = key[1]
                    pe.wait_ge(pair_sem("rv"), GI["rv"] // 2 + 1)
                    for hh in range(2):
                        h = 2 * hp + hh
                        in_sbuf(pe, ("ret_s", h))
                        v = V["rv"][:, :, h * RET_DV:(h + 1) * RET_DV]
                        sc = retS[h % 2]
                        pe.matmul(b[:, hh * P:(hh + 1) * P], sc[:, 0:P], v[:, 0, :], start=True, stop=True)
                        ob = b[:, S + hh * P:S + (hh + 1) * P]
                        pe.matmul(ob, sc[:, P:S], v[:, 0, :], start=True, stop=False)
                        mm = pe.matmul(ob, sc[:, S:384], v[:, 1, :], start=False, stop=True)
                elif kind == "sc":
                    br, h = HEADS[key[1]]
                    gq, gk = ("mq", "mk") if br == "moba" else ("cq", "ck")
                    for t in range(TT):
                        in_sbuf(pe, ("qT", gq, t))
                        in_sbuf(pe, ("qT", gk, t))
                    rows, c = (slice(64 * (h % 2), 64 * (h % 2) + 64), h // 2) if br == "moba" else (slice(0, P), h)
                    for it in range(TT):
                        mm = pe.matmul(b[:, it * S:(it + 1) * S], qT[gq][rows, c, it * P:(it + 1) * P], qT[gk][rows, c, :],
                                       start=True, stop=True)
                elif kind == "pT":
                    h = key[1]
                    pe.wait_ge(exp_done, 2 * h + 2)
                    order = [(0, 0), (1, 0), (1, 1)] if HEADS[h][0] == "moba" else [(0, 0), (0, 1), (1, 0), (1, 1)]
                    mm = transposes(lambda c: probs[h % 4][:, order[c][0] * S + order[c][1] * P:order[c][0] * S + (order[c][1] + 1) * P],
                                    blocks=len(order))
                elif kind == "pv":
                    h = key[1]
                    br, hh = HEADS[h]
                    hd, vg = (MOBA_HD, "mv") if br == "moba" else (MEM_HD, "cv")
                    in_sbuf(pe, ("pT", h))
                    pe.wait_ge(pair_sem(vg), GI[vg] // 2 + 1)
                    order = [(0, 0), (1, 0), (1, 1)] if br == "moba" else [(0, 0), (0, 1), (1, 0), (1, 1)]
                    for c, (it, jt) in enumerate(order):
                        last = c + 1 == len(order) or order[c + 1][0] != it
                        mm = pe.matmul(b[:, it * hd:(it + 1) * hd], PT[h % 4][:, c * P:(c + 1) * P], V[vg][:, jt, hh * hd:(hh + 1) * hd],
                                       start=(jt == 0), stop=last)
                elif kind == "oT":
                    br, t = key[1:]
                    if br == "ret":
                        pe.wait_ge(silu_done, 2)
                    else:
                        for h in range(NH):
                            if HEADS[h][0] == br:
                                in_sbuf(pe, ("pv", h))
                    mm = transposes(lambda c: o[br][:, t, c * P:(c + 1) * P])
                elif kind == "yT":
                    nn, t = key[1:]
                    pe.wait_ge(y_done, 2 * nn + 2)
                    mm = transposes(lambda c: y[:, t, nn * 512 + c * P:nn * 512 + (c + 1) * P])
                elif kind == "xT":
                    t, kk = key[1:]
                    pe.wait_ge(x2_done, TT * kk + t + 1)
                    mm = transposes(lambda c: X[:, t, (4 * kk + c) * P:(4 * kk + c + 1) * P])
                elif kind == "pos":
                    pe.wait_ge(rout, RI["m1"])
                    pe.matmul(b[:, 0:NE], before, MG[:, 0, :], start=True, stop=True)
                    pe.matmul(b[:, NE:2 * NE], ones, MG[:, 0, :], start=True, stop=False)
                    mm = pe.matmul(b[:, NE:2 * NE], before, MG[:, 1, :], start=False, stop=True)
                mm.then_inc(task_done, 1)
                if kind == "xT" and key[1] == TT - 1:
                    for t in range(TT):
                        in_sbuf(pe, ("xT", t, kk))
                        if kk == 0 and t == 0:
                            pe.wait_ge(bcast_in, 16 * N_BCAST)
                            pe.wait_ge(x2_done, TT)
                        for k in range(4 * kk, 4 * kk + 4):
                            lm = pe.matmul(pair[GI["out0"] % 2][:, t, 0:NE], hT[:, k, t * P:(t + 1) * P], wr[:, k, :],
                                           start=(k == 0), stop=(k == KC - 1))
                        if kk == 1:
                            lm.then_inc(logits_done, 1)

            def late_task(key):
                kind, b, n = key[0], late_bank(key), LATE.index(key)
                if n >= 2:
                    pe.wait_ge(late_read[n % 2], n // 2)
                if kind == "cnt":
                    for t in range(TT):
                        mm = pe.matmul(b[0:NE, 0:1], MG[:, t, :], ones[:, 0:1], start=(t == 0), stop=(t == 1))
                elif kind == "tabT":
                    pe.wait_ge(rout, RI["posm"])
                    for t in range(TT):
                        pe.transpose(b[0:NE, t * P:(t + 1) * P], posm[:, t, :], ident)
                        mm = pe.transpose(b[0:NE, S + t * P:S + (t + 1) * P], G[:, t, :], ident)
                elif kind == "off":
                    pe.wait_ge(rout, RI["n"])
                    pe.matmul(b[0:NE, 0:1], before[0:NE, 0:NE], rt[:, 4:5], start=True, stop=True)
                    mm = pe.matmul(b[0:1, 2:3], ones[0:NE, 0:1], rt[:, 4:5], start=True, stop=True)
                elif kind == "tab":
                    pe.wait_ge(rout, RI["sz"])
                    late_in_sbuf(pe, ("tabT",))
                    m = MAX_ITEMS - NE
                    for t in range(TT):
                        rows = slice(t * P, (t + 1) * P)
                        pe.matmul(b[:, t * m:(t + 1) * m], tabT[:, 0, rows], selw[:, 0, NE:], start=True, stop=False)
                        pe.matmul(b[:, t * m:(t + 1) * m], ones[0:NE, :], selw[:, 1, NE:], start=False, stop=True)
                        pe.matmul(b[:, (2 + t) * m:(3 + t) * m], tabT[:, 1, rows], selw[:, 0, NE:], start=True, stop=True)
                    pe.matmul(b[0:64, 4 * m:5 * m], twice, selw[:, 0, NE:], start=True, stop=True)
                    mm = pe.matmul(b[0:1, 5 * m:6 * m], iotap[0:NE, :], selw[:, 0, NE:], start=True, stop=True)
                elif kind == "b2":
                    t, nn = key[1:]
                    pe.wait_ge(b2_in, 32)
                    mm = pe.matmul(b, tabT[:, 1, t * P:(t + 1) * P], b2s[:, nn * 512:nn * 512 + 512], start=True, stop=True)
                mm.then_inc(late_done, 1)

            def gather(i):
                pe.wait_ge(sg_done, 3 * (i + 1))
                for part, xt in enumerate((xth, xtl)):
                    if part and isinstance(i, int) and i == 0:
                        pe.wait_ge(xl_done, TT)
                    for k in range(KC):
                        for t in range(TT):
                            mm = pe.matmul(banks[6 + part][:, k * SL:(k + 1) * SL], xt[:, t, k * P:(k + 1) * P], SG[:, t, 0:SL],
                                           start=(t == 0), stop=(t == 1))
                    mm.then_inc(ga_pe, 1)

            def products(j, u, first, chunks, lhs, width, out0, last_chunk, use_native):
                slot, uses = raw_at(j, u)
                if use_native:
                    pe.wait_ge(raw_in[slot], uses * 16)
                    parts = [raw[slot][:, :]]
                else:
                    pe.wait_ge(hi_done, split_count(j, u))
                    pe.wait_ge(lo_done, split_count(j, u))
                    parts = [hi[hl_slot(j, u)][:, :], lo[hl_slot(j, u)][:, :]]
                for c in range(chunks):
                    for p, w in enumerate(parts):
                        for n in range(width // 512):
                            mm = pe.matmul(PS[:, out0 + n * 512:out0 + (n + 1) * 512],
                                           lhs(c).bitcast(F32) if use_native else lhs(c),
                                           w[:, c * width + n * 512:c * width + (n + 1) * 512],
                                           start=(first and c == 0 and p == 0),
                                           stop=(last_chunk and c == chunks - 1 and p == len(parts) - 1))
                mm.then_inc(nat_used if use_native else hl_used, 1)

            def up(j, u):
                products(j, u, False, 1, lambda c: XG[:, u, :], FF2, 0, u == W1U - 1, native(j, u))

            def down(j, u, v, use_native):
                products(j, u, v == 0, 2, lambda c: AT[:, 2 * v + c, :, :].rearrange("p a s -> p (a s)"), D, 2048, v == W2U - 1, use_native)

            def scatter_transposes(i):
                pe.wait_ge(ss_mat, 2 * (i + 1))
                for t in range(TT):
                    mm = pe.transpose(banks[7][:, t * P:(t + 1) * P], SS[:, t, :].bitcast(F32), ident)
                return mm

            def scatter(i, q):
                t, n = q // 2, q % 2
                for p, part in enumerate((YH, YL)):
                    mm = pe.matmul(banks[6 + q % 2], ST[:, t * P:(t + 1) * P], part[:, n * 512:(n + 1) * 512], start=(p == 0), stop=(p == 1))
                mm.then_inc(sc_pe, 1)

            def body(j):
                later = not isinstance(j, int)
                pe.wait_ge(xgh, j + 1)
                pe.wait_ge(xgl, j + 1)
                if later or j >= 1:
                    pe.wait_ge(swi, 6 * j - 4)
                for n in range(4):
                    pe.matmul(banks[n], BL[:, :], b1s[:, n * 512:(n + 1) * 512], start=True, stop=False)
                for u in range(W1U):
                    up(j, u)
                    if isinstance(j, int) and j == 0:
                        for key in LATE_PE.get(u, []):
                            late_task(key)
                    if u == 2:
                        if later:
                            scatter_transposes(j - 2)
                        for t in range(TT):
                            mm = pe.matmul(banks[7][:, S:S + 1], SG[:, t, :].bitcast(F32), gi[:, t, bass.ds(j, 1)],
                                           start=(t == 0), stop=(t == 1))
                        mm.then_inc(st_pe, 1)
                    if later and u == 4:
                        pe.wait_ge(atl, j)
                        pe.wait_ge(yh, j - 1)
                        pe.wait_ge(yl, j - 1)
                        pe.wait_ge(st_act, j - 1)
                        scatter(j - 2, 0)
                        pe.wait_ge(slw, j + 1)
                        scatter(j - 2, 1)
                    if later and u == 6:
                        for q in (2, 3):
                            pe.wait_ge(sc_add, 4 * (j - 2) + (q - 1))
                            scatter(j - 2, q)
                if later:
                    pe.wait_ge(sc_add, 4 * (j - 1))
                else:
                    pe.wait_ge(slw, j + 1)
                    if j == 1:
                        pe.wait_ge(atl, j)
                gather(j + 1)
                if later or j >= 1:
                    pe.wait_ge(ath, j)
                    pe.wait_ge(atl, j)
                    if later:
                        pe.wait_ge(yl, j - 1)
                    for v in range(W2U):
                        down(j, W1U + v, v, W1U + v in NATIVE)
                pe.wait_ge(swi, 6 * (j + 1))
                pe.wait_ge(xgh, j + 2)
                for c in range(4):
                    mm = pe.transpose(banks[6][:, c * P:(c + 1) * P], act_t[:, c * P:(c + 1) * P], ident)
                mm.then_inc(tr_pe, 1)

            pe.wait_ge(xh_done, TT)
            for n in range(N_TASKS - 4, N_TASKS):
                pe.wait_ge(bank_read[n % 4], n // 4 + 1)
            late_task(("cnt",))
            gather(0)
            late_task(("off",))
            late_task(("tabT",))
            pe.wait_ge(b1h, 1)
            pe.wait_ge(b1l, 1)
            pe.wait_ge(zeroed, 2)
            body(0)
            body(1)
            n_items = number_of_items(pe)
            with pe.Fori(2, n_items) as j:
                body(j)
            j = n_items
            pe.wait_ge(xgl, j + 1)
            scatter_transposes(j - 2).then_inc(st_pe, 1)
            pe.wait_ge(ath, j)
            pe.wait_ge(atl, j)
            pe.wait_ge(yl, j - 1)
            for v in range(W2U):
                down(j, v, v, True)
            pe.wait_ge(yh, j - 1)
            pe.wait_ge(st_act, j - 1)
            for q in range(4):
                if q >= 2:
                    pe.wait_ge(sc_add, 4 * (j - 2) + (q - 1))
                scatter(j - 2, q)
            pe.wait_ge(sc_add, 4 * (j - 1))
            scatter_transposes(j - 1).then_inc(st_pe, 1)
            pe.wait_ge(yh, j)
            pe.wait_ge(yl, j)
            pe.wait_ge(st_act, j)
            for q in range(4):
                if q >= 2:
                    pe.wait_ge(sc_add, 4 * (j - 1) + (q - 1))
                scatter(j - 1, q)


NAMES = ["x", "mem", "g_mix", "w_in", "b_gate", "g_ret_out", "g_moba_q", "g_moba_k", "g_mem", "w_mem_kv", "g_mem_q", "g_mem_k",
         "w_br_ret", "w_br_moba", "w_br_mem", "w_out", "g_ffn", "w_router", "b_router", "w_mlp1", "b_mlp1", "w_mlp2", "b_mlp2"]


def kernel(x, mem, g_mix, w_in, b_gate, g_ret_out, g_moba_q, g_moba_k, g_mem, w_mem_kv, g_mem_q, g_mem_k, w_br_ret, w_br_moba,
           w_br_mem, w_out, g_ffn, w_router, b_router, w_mlp1, b_mlp1, w_mlp2, b_mlp2):
    import numpy as np
    import concourse.bacc as bacc
    from concourse.bass_utils import run_bass_kernel_spmd

    given = dict(zip(NAMES, (x, mem, g_mix, w_in, b_gate, g_ret_out, g_moba_q, g_moba_k, g_mem, w_mem_kv, g_mem_q, g_mem_k,
                             w_br_ret, w_br_moba, w_br_mem, w_out, g_ffn, w_router, b_router, w_mlp1, b_mlp1, w_mlp2, b_mlp2)))
    arrays = {n: np.ascontiguousarray(v) for n, v in given.items()}
    cols = [arrays[n][0].reshape(KC, P).T for n in ("g_mix", "g_mem", "g_ffn")]
    cols += [np.tile(arrays[n][0], P // arrays[n].shape[1])[:, None] for n in ("g_moba_q", "g_moba_k", "g_mem_q", "g_mem_k", "g_ret_out")]
    arrays["gains"] = np.ascontiguousarray(np.concatenate(cols, 1))
    for n in ("g_mix", "g_mem", "g_moba_q", "g_moba_k", "g_mem_q", "g_mem_k", "g_ret_out"):
        del arrays[n]
    arrays["decay"], arrays["alibi"], arrays["misc"] = host_constants()
    nc = bacc.Bacc("TRN2", target_bir_lowering=False, num_devices=1)
    aps = {n: nc.dram_tensor(f"in_{n}", v.shape, mybir.dt.from_np(v.dtype), kind="ExternalInput").ap() for n, v in arrays.items()}
    out = nc.dram_tensor("out", (1, S, D), F32, kind="ExternalOutput").ap()
    build(nc, aps, out)
    r = run_bass_kernel_spmd(nc, [{f"in_{n}": v for n, v in arrays.items()}], core_ids=[0])
    return r.results[0]["out"]
```

```python
import concourse.bass as bass
from concourse import mybir
from contextlib import ExitStack

F32 = mybir.dt.float32
F32R = mybir.dt.float32r
I32 = mybir.dt.int32
U32 = mybir.dt.uint32
ALU = mybir.AluOpType
ACT = mybir.ActivationFunctionType
AX = mybir.AxisListType

P = 128
S = 256
TT = S // P
D = 1024
KC = D // P
EPS = 1e-5
RET_H, RET_DK, RET_DV = 4, 64, 128
MOBA_H, MOBA_HD = 8, 64
MEM_H, MEM_HD = 4, 128
NE = 32
TOPK = 4
FF2 = 2 * D
LIMIT, ALPHA = 7.0, 1.702
SL = 64
MISC = 4 * P + 128
MAX_ITEMS = NE + (S * TOPK) // SL
G_COLS = 512

GROUPS = [("rqk", KC), ("mq", KC), ("mk", KC), ("cq", KC), ("ck", KC), ("cv", KC), ("rv", KC), ("mv", KC), ("rg", KC)]
GROUPS += [(f"gate{i}", KC) for i in range(6)]
BRANCH_ORDER = [(n, br) for n in range(2) for br in ("moba", "ret", "mem")]
GROUPS += [(f"br_{br}{n}", 4) for n, br in BRANCH_ORDER]
GROUPS += [(f"out{n}", KC) for n in range(2)]
GI = {name: i for i, (name, _) in enumerate(GROUPS)}
W_IN_COL = {"rqk": 0, "rv": 512, "rg": 1024, "mq": 1536, "mk": 2048, "mv": 2560, "cq": 3072,
            **{f"gate{i}": 3584 + 512 * i for i in range(6)}}
UNITS = [(g, hk) for g, (_, kc) in enumerate(GROUPS) for hk in range(kc // 4)]
N_MIX = len(UNITS)
UNITS_DONE = [sum(1 for (gg, _) in UNITS if gg <= g) for g in range(len(GROUPS))]

RING = 6
MIX_RING = 4
NATIVE_GROUPS = ("rqk",)
SPLIT_UNITS = [m for m, (g, _) in enumerate(UNITS) if GROUPS[g][0] not in NATIVE_GROUPS]
MIX_HL = 2
SPLIT_3 = SPLIT_UNITS.index(UNITS_DONE[GI["gate5"]])
HI_SLOT = [k % MIX_HL if k < SPLIT_3 else (k - SPLIT_3 + MIX_HL) % (MIX_HL + 1) for k in range(len(SPLIT_UNITS))]
HI_LAST = [max([i for i in range(k) if HI_SLOT[i] == HI_SLOT[k]], default=None) for k in range(len(SPLIT_UNITS))]
assert N_MIX % MIX_RING == 0 and HI_SLOT[SPLIT_3 - 1] == MIX_HL - 1
W1U, W2U = 8, 4
IU = W1U + W2U
NATIVE = {1, 4, 10}
NATIVE_0 = {3, 7}
HL = 3
SPLIT = [u for u in range(IU) if u not in NATIVE]
SPLIT_0 = [u for u in range(W1U) if u not in NATIVE_0]
W2_SPLIT = [u for u in SPLIT if u >= W1U]
W2_NATIVE = [u for u in NATIVE if u >= W1U]
assert len(SPLIT) % HL == 0 and IU % RING == 0 and len(SPLIT_0) == len(SPLIT) - len(W2_SPLIT) and SPLIT_0[:HL] == list(range(HL))

Q_GROUPS = ["rqk", "mq", "mk", "cq", "ck"]
HEADS = [("moba", h) for h in range(MOBA_H)] + [("mem", h) for h in range(MEM_H)]
NH = len(HEADS)
SLOTS = ["mv", "rg"] + [f"gate{i}" for i in range(6)]


def schedule():
    def splits(g, which=(0, 1)):
        units = [m for m in SPLIT_UNITS if UNITS[m][0] == g]
        return [("split", m) for i, m in enumerate(units) if i in which]

    def tasks(*keys):
        return [("task",) + key for key in keys]

    tiles = range(TT)
    between = {"rqk": tasks(*[("hT", 1, t, kk) for t in tiles for kk in range(2)]),
               "mq": tasks(*[("qT", "rqk", t) for t in tiles]),
               "mk": tasks(*[("qT", "mq", t) for t in tiles], ("ret_s", 0), ("ret_s", 1)),
               "cq": tasks(*[("qT", "mk", t) for t in tiles]),
               "ck": tasks(*[("qT", "cq", t) for t in tiles]),
               "cv": tasks(*[("qT", "ck", t) for t in tiles]),
               "rv": tasks(("ret_o", 0), ("ret_s", 2), ("ret_s", 3))}
    steps = tasks(*[("hT", 0, t, kk) for t in tiles for kk in range(2)])
    for g in ("rqk", "mq", "mk", "cq", "ck", "cv", "rv"):
        if g == "rv":
            steps += splits(GI[g] + 1, (0,)) + [("group", g)] + between[g] + splits(GI[g] + 1, (1,))
        else:
            steps += splits(GI[g] + 1) + [("group", g)] + between[g]
    for s, g in enumerate(SLOTS):
        last = g == SLOTS[-1]
        steps += splits(GI[g] + 1) + splits(GI[g] + 2) if last else splits(GI[g] + 1, (0,))
        steps += [("group", g)]
        if g == "mv":
            steps += tasks(("ret_o", 1))
        if g == "gate4":
            steps += tasks(*[("oT", "moba", t) for t in tiles])
        steps += tasks(*[("pv", a) for a in (2 * s - 4, 2 * s - 3) if 0 <= a < NH])
        steps += tasks(*[("pT", a) for a in (2 * s - 2, 2 * s - 1) if 0 <= a < NH])
        if not last:
            steps += splits(GI[g] + 1, (1,))
        steps += tasks(*[("sc", a) for a in (2 * s, 2 * s + 1) if a < NH])
        if g == "gate5":
            steps += tasks(*[("oT", "ret", t) for t in tiles])
    rest = SPLIT_UNITS[SPLIT_3 + 2:]
    for i, (n, br) in enumerate(BRANCH_ORDER):
        steps += [("split", rest.pop(0)), ("group", f"br_{br}{n}")]
        if i == 0:
            steps += tasks(*[("oT", "mem", t) for t in tiles])
        if i == 4:
            steps += tasks(*[("yT", 0, t) for t in tiles])
    steps += [("split", rest.pop(0)), ("group", "out0")] + tasks(*[("yT", 1, t) for t in tiles])
    steps += [("split", rest.pop(0)), ("half", "out0")]
    steps += [("group", "out1")] + tasks(*[("xT", t, 0) for t in tiles])
    steps += [("half", "out1")] + tasks(*[("xT", t, 1) for t in tiles]) + tasks(("pos",))
    assert not rest and sorted(s[1] for s in steps if s[0] == "split") == SPLIT_UNITS
    return steps


LATE = [("cnt",), ("off",), ("tabT",), ("tab",)] + [("b2", t, n) for t in range(TT) for n in range(2)]
END = IU
LATE_PE = {(0, 2): [("tab",)], (0, END): LATE[4:6], (1, 0): [LATE[6]], (1, 1): [LATE[7]]}
LATE_DVE = {(0, 4): [("tab",)], (0, END): LATE[4:6], (1, 0): [LATE[6]], (1, 2): [LATE[7]]}


NORMS = ["x", "mem", "mq", "mk", "cq", "ck", "ret0", "ret1", "x2"]
SQUARES = [2, 2, 1, 1, 1, 1, 1, 1, 4]
SUMS = [0, 0, 1, 1, 1, 1, 1, 1, 1]
ROUTE = ["lg0", "lg1", "max0", "max1", "mi0", "mi1", "nv", "if", "oh0", "oh1", "m0", "m1", "posm", "rse", "w4", "ow0", "ow1",
         "g0", "g1", "g3", "n", "off", "offr", "s1", "s2", "s3", "t1", "t2", "u1", "u2", "u3", "si", "sz",
         "posi", "gi", "bsel", "it"]
PARTS = [s[1:] for s in schedule() if s[0] == "task" and (s[1] in ("oT", "yT"))]
RI = {n: i + 1 for i, n in enumerate(ROUTE)}
STEPS = schedule()
TASKS = {s[1:]: n for n, s in enumerate([s for s in STEPS if s[0] == "task"])}
N_TASKS = len(TASKS)


def host_constants():
    import numpy as np
    i = np.arange(P, dtype=np.float64)[:, None]
    t = np.arange(S, dtype=np.float64)[None, :]
    diff = t - i
    decay = np.zeros((P, RET_H, 384))
    for h in range(RET_H):
        lg = np.log1p(-np.exp2(-5.0 - h))
        d = np.where(diff >= 0, np.exp(np.maximum(diff, 0) * lg), 0.0) * RET_DK ** -0.5
        decay[:, h, 0:S] = d
        decay[:, h, S:384] = d[:, 0:P]
    alibi = np.zeros((P, TT, S))
    for tt in range(TT):
        dist = (i + P * tt) - t
        alibi[:, tt, :] = np.where(dist >= 0, -dist, -1e33)
    misc = np.zeros((P, MISC))
    misc[:, 0:P] = np.eye(P)
    misc[:, P:2 * P] = (i < i.T)
    misc[:, 2 * P:3 * P] = 1.0
    misc[:, 3 * P:4 * P] = np.arange(P)[None, :] % SL
    misc[:, 4 * P:4 * P + 32] = np.arange(32)[None, :]
    misc[:, 4 * P + 32] = i[:, 0]
    misc[:, 4 * P + 33:4 * P + 36] = [SL, 2 * SL, 3 * SL]
    misc[:, 4 * P + 36] = EPS
    misc[0:NE, 4 * P + 64:4 * P + 128] = np.concatenate([np.eye(NE), np.eye(NE)], 1)
    misc[NE:2 * NE, 4 * P + 64:4 * P + 96] = np.eye(NE)
    f = np.float32
    return decay.reshape(P, -1).astype(f), alibi.reshape(P, -1).astype(f), misc.astype(f)


def build(nc, a, out):
    ctx = ExitStack()
    with ctx:
        def sem(name):
            return ctx.enter_context(nc.semaphore(name))

        def sb(name, shape, dt=F32, scope=ctx):
            return scope.enter_context(nc.sbuf_tensor(name, shape, dt))

        first = ExitStack()
        rest = [sb(f"rest{i}", [P, 2048], F32R, scope=first) for i in range(MIX_RING)]
        first.close()
        raw = [sb(f"raw{i}", [P, 2048]) for i in range(MIX_RING)]
        mix_hi = [sb(f"mix_hi{i}", [P, 2048], F32R) for i in range(MIX_HL)]
        X = sb("X", [P, TT, D])
        first = ExitStack()
        hTh = sb("hTh", [P, KC, S], F32R, scope=first)
        first.close()
        hT = sb("hT", [P, KC, S])
        first = ExitStack()
        mTl = sb("mTl", [P, KC, S], F32R, scope=first)
        first.close()
        hx = sb("hx", [P, TT, D])
        first = ExitStack()
        mTh = sb("mTh", [P, KC, S], F32R, scope=first)
        first.close()
        mT = sb("mT", [P, KC, S])
        misc = sb("misc", [P, MISC])
        ident, before, ones, slotn = (misc[:, i * P:(i + 1) * P] for i in range(4))
        iota32 = misc[:, 4 * P:4 * P + 32]
        iotap = misc[:, 4 * P + 32:4 * P + 33]
        thresholds = misc[:, 4 * P + 33:4 * P + 36]
        eps = misc[:, 4 * P + 36:4 * P + 37]
        twice = misc[0:NE, 4 * P + 64:4 * P + 128]
        gffn = sb("gffn", [P, D])
        wr = sb("wr", [P, KC, NE])
        brt = sb("brt", [P, NE])
        gains = sb("gains", [P, 3 * KC + 5])
        gcol = gains[:, 0:2 * KC]
        fcol = gains[:, 2 * KC:3 * KC]
        qgain = gains[:, 3 * KC:]
        stat = sb("stat", [P, 3, 16 * len(NORMS)])
        smx = sb("smx", [P, 4, 2 * NH])
        spare = sb("spare", [1, 4])
        lg = sb("lg", [P, TT, NE])
        v8 = sb("v8", [P, TT, 8])
        i8 = sb("i8", [P, TT, 8], U32)
        i8f = sb("i8f", [P, TT, 8])
        nv = sb("nv", [P, TT])
        e4 = sb("e4", [P, TT, 4])
        se = sb("se", [P, 2 * TT])
        oh = sb("oh", [P, TT, 4, NE])
        ohw = sb("ohw", [P, TT, 4, NE])
        MG = sb("MG", [P, TT, NE])
        rt = sb("rt", [NE, 96])
        selw = sb("selw", [NE, 2, MAX_ITEMS])
        tabT = sb("tabT", [NE, 2, S])
        PG = sb("PG", [P, 2, TT, MAX_ITEMS])
        posi, gi = PG[:, 0, :, :], PG[:, 1, :, :]
        posm, G = posi[:, :, 0:NE], gi[:, :, 0:NE]
        bsel = sb("bsel", [64, MAX_ITEMS])
        items = sb("items", [1, MAX_ITEMS + 2], I32)

        mix = ExitStack()
        qTs = {g: sb(f"qT_{g}", [P, 4, S], scope=mix) for g in Q_GROUPS}
        bg = sb("bg", [P, 2, 512], scope=mix)
        mix.close()
        mix = ExitStack()
        oTp = {br: [sb(f"oT_{br}{p}", [P, 4, S], F32R, scope=mix) for p in range(2)] for br in ("moba", "ret", "mem")}
        mem = sb("mem", [P, TT, D], scope=mix)
        V = {g: sb(f"V_{g}", [P, TT, 512], scope=mix) for g in ("rv", "cv", "mv", "rg")}
        gates = sb("gates", [P, TT, 3 * D], scope=mix)
        tq = [sb(f"tq{i}", [P, TT, 512], scope=mix) for i in range(2)]
        PTs = sb("PTs", [P, 2048], scope=mix)
        PT = [PTs[:, i * 512:(i + 1) * 512] for i in range(4)]
        o = {br: sb(f"o_{br}", [P, TT, 512], scope=mix) for br in ("ret", "mem", "moba")}
        alibi = sb("alibi", [P, TT * S], scope=mix)
        hTl = sb("hTl", [P, KC, S], F32R, scope=mix)
        mix.close()
        probs = [hx[:, i // 2, (i % 2) * 512:(i % 2) * 512 + 512] for i in range(4)]
        decay = gates[:, 1, 3 * D - RET_H * 384:3 * D]
        retS = [PT[i][:, 0:384] for i in range(2)]
        sq = gates[:, 0, 0:D]
        rgs = mem[:, 1, :].rearrange("p (t n) -> p t n", t=TT)
        tmp = V["rv"]
        hTf = PTs[:, :].rearrange("p (k s) -> p k s", s=S)
        y = hx
        b2s = o["moba"][0:NE, :, :].rearrange("p t n -> p (t n)")
        b1raw = PTs[0:64, :]

        raw += [sb(f"raw{i}", [P, 2048]) for i in range(MIX_RING, RING)]
        hi = [sb("hi", [P, 2048], F32R)] + mix_hi
        lo = [sb(f"lo{i}", [P, 2048], F32R) for i in range(HL)]
        XG = sb("XG", [P, KC, 2 * SL], F32R)
        AT = sb("AT", [P, KC, 2, SL], F32R)
        YH = sb("YH", [P, D], F32R)
        YL = sb("YL", [P, D], F32R)
        xth = sb("xth", [P, TT, D], F32R)
        b1s = sb("b1s", [P, FF2], F32R)
        xtl = sb("xtl", [P, TT, D], F32R)
        SG = sb("SG", [P, TT, 2 * SL], F32R)
        SS = sb("SS", [P, TT, 2 * SL], F32R)
        ST = sb("ST", [P, S], F32R)
        SS2 = sb("SS2", [P, TT, 2 * SL], F32R)
        STL = sb("STL", [P, 2 * S], F32R)
        BL = sb("BL", [P, 2 * SL], F32R)
        slotw = sb("slotw", [P, 1])
        YH2, YL2 = xth[:, 0, :], xtl[:, 0, :]
        HB = mT[:, 0:4, :].rearrange("p k s -> p (k s)")
        HS = mT[:, 4:8, :].rearrange("p k s -> p (k s)")
        hview = hT[:, :, :].rearrange("p k s -> p (k s)")
        glu, lin, sig, act_t = (hview[:, i * 512:(i + 1) * 512] for i in range(4))

        PS = ctx.enter_context(nc.psum_tensor("PS", [P, 4096], F32))
        banks = [PS[:, i * 512:(i + 1) * 512] for i in range(8)]
        pair = [PS[:, i * 1024:(i + 1) * 1024].rearrange("p (t n) -> p t n", t=TT) for i in range(2)]

        def bank(key):
            return banks[4 + TASKS[key] % 4]

        raw_in = [sem(f"raw_in{i}") for i in range(RING)]
        x_half = [sem(f"x_half{t}") for t in range(TT)]
        mem_in, const_in, table_in, bcast_in, b1_in, b2_in = (sem(n) for n in ("mem_in", "const_in", "table_in", "bcast_in", "b1_in", "b2_in"))
        unit_used = sem("unit_used")
        task_done = sem("task_done")
        pair_free = [sem(f"pair_free{i}") for i in range(2)]
        bank_read = [sem(f"bank_read{i}") for i in range(4)]
        sq_done, sd_done = sem("sq_done"), sem("sd_done")
        rs_done = sem("rs_done")
        ss_done = sem("ss_done")
        hx_done = sem("hx_done")
        max_done = sem("max_done")
        exp_done = sem("exp_done")
        rcp_done = sem("rcp_done")
        sig_done = sem("sig_done")
        y_done = sem("y_done")
        x2_done = sem("x2_done")
        silu_done = sem("silu_done")
        xt_done = sem("xt_done")
        row0_done, logits_done = sem("row0_done"), sem("logits_done")
        late_done = sem("late_done")
        late_read = [sem(f"late_read{i}") for i in range(2)]
        warm = sem("warm")
        xh_done, xl_done = sem("xh_done"), sem("xl_done")
        wh_done, wl_done = sem("wh_done"), sem("wl_done")
        hTh_done, hTl_done = sem("hTh_done"), sem("hTl_done")
        part_high = sem("part_high")
        bias_in = [sem(f"bias_in{i}") for i in range(2)]
        rout = sem("rout")
        rexp = sem("rexp")
        b1h, b1l = sem("b1h"), sem("b1l")
        zeroed = sem("zeroed")
        hi_done, lo_done = sem("hi_done"), sem("lo_done")
        hl_used = sem("hl_used")
        nat_used = sem("nat_used")
        sg_done = sem("sg_done")
        ss_mat = sem("ss_mat")
        st_pe, st_act, slw = sem("st_pe"), sem("st_act"), sem("slw")
        ga_pe, xgh, xgl = sem("ga_pe"), sem("xgh"), sem("xgl")
        hb_act = sem("hb_act")
        swi = sem("swi")
        sgm = sem("sgm")
        tr_pe, ath, atl = sem("tr_pe"), sem("ath"), sem("atl")
        yh, yl = sem("yh"), sem("yl")
        sc_pe, sc_add = sem("sc_pe"), sem("sc_add")
        out_dma = sem("out_dma")

        N_CONST, N_TABLE, N_BCAST = 2, 2, 3

        def sigmoid_gate(act, i):
            act.wait_ge(pair_sem(f"gate{i}"), GI[f"gate{i}"] // 2 + 1)
            act.activation(gates[:, :, 512 * i:512 * i + 512], gates[:, :, 512 * i:512 * i + 512], ACT.Sigmoid).then_inc(sig_done, 1)

        def raw_at(j, u):
            if isinstance(j, int) and j == 0:
                slot, uses = (MIX_RING + u) % RING, u // RING + 1
            else:
                slot, uses = u % RING, j * (IU // RING) + ((u - MIX_RING) // RING + 1)
            return slot, uses + (N_MIX // MIX_RING if slot < MIX_RING else 0)

        def mix_high_part(m):
            return (mix_hi + [lo[HL - 1]])[HI_SLOT[SPLIT_UNITS.index(m)]]

        def split_count(j, u):
            if isinstance(j, int) and j == 0:
                return sum(1 for x in SPLIT_0 if x <= u)
            return j * len(SPLIT) + (sum(1 for x in SPLIT if x <= u) - len(W2_SPLIT))

        def native_count(j, u):
            if isinstance(j, int) and j == 0:
                return sum(1 for x in NATIVE_0 if x <= u)
            return j * len(NATIVE) + (sum(1 for x in NATIVE if x <= u) - len(W2_NATIVE))

        def hl_slot(j, u):
            if isinstance(j, int) and j == 0:
                return SPLIT_0.index(u) % HL
            return (SPLIT.index(u) - len(W2_SPLIT)) % HL

        def native(j, u):
            return u in (NATIVE_0 if isinstance(j, int) and j == 0 else NATIVE)

        def unit_done(eng, j, u):
            if native(j, u):
                eng.wait_ge(nat_used, native_count(j, u))
            else:
                eng.wait_ge(hl_used, split_count(j, u))

        def in_sbuf(eng, key):
            n = TASKS[key]
            eng.wait_ge(bank_read[n % 4], n // 4 + 1)

        def late_in_sbuf(eng, key):
            n = LATE.index(key)
            eng.wait_ge(late_read[n % 2], n // 2 + 1)

        def late_bank(key):
            return banks[4 + LATE.index(key) % 2]

        def read_sem(key):
            return bank_read[TASKS[key] % 4]

        def pair_sem(g):
            return pair_free[GI[g] % 2]

        def number_of_items(eng):
            late_in_sbuf(eng, ("off",))
            return eng.value_load(items[0:1, MAX_ITEMS:MAX_ITEMS + 1], min_val=0, max_val=MAX_ITEMS - NE - 1) + NE

        block = ctx.enter_context(nc.Block())

        @block.sync
        def _(sp):
            for t in range(TT):
                sp.dma_start(X[:, t, :], a["x"][0, t * P:(t + 1) * P, :]).then_inc(x_half[t], 16)

            def mixer_source(g, hk):
                name = GROUPS[g][0]
                if name in W_IN_COL:
                    w, c = a["w_in"][0], W_IN_COL[name]
                elif name in ("ck", "cv"):
                    w, c = a["w_mem_kv"][0], 512 * (name == "cv")
                elif name.startswith("br_"):
                    w, c = a[{"ret": "w_br_ret", "moba": "w_br_moba", "mem": "w_br_mem"}[name[3:-1]]][0], 512 * int(name[-1])
                else:
                    w, c = a["w_out"][0], 512 * int(name[-1])
                return w[512 * hk:512 * hk + 512, c:c + 512].rearrange("(k p) n -> p k n", p=P)

            for m, (g, hk) in enumerate(UNITS):
                if m >= MIX_RING:
                    sp.wait_ge(unit_used, m - MIX_RING + 1)
                sp.dma_start(raw[m % MIX_RING][:, :].rearrange("p (k n) -> p k n", k=4),
                             mixer_source(g, hk)).then_inc(raw_in[m % MIX_RING], 16)
                if m == 1:
                    sp.dma_start(mem[:, :, :], a["mem"].rearrange("o (t p) d -> p (o t) d", p=P)).then_inc(mem_in, 16)

            def slot_free(j, u):
                if isinstance(j, int) and j == 0 and u < RING:
                    slot, _ = raw_at(j, u)
                    sp.wait_ge(unit_used, N_MIX - MIX_RING + slot + 1 if slot < MIX_RING else UNITS_DONE[GI["out0"] - 1])
                    return
                if isinstance(j, int) and j == 1 and u < RING:
                    pj, pu = 0, W1U - RING + u
                elif u >= RING:
                    pj, pu = j, u - RING
                else:
                    pj, pu = j - 1, u + IU - RING
                if native(pj, pu):
                    sp.wait_ge(nat_used, native_count(pj, pu))
                else:
                    sp.wait_ge(hi_done, split_count(pj, pu))
                    sp.wait_ge(lo_done, split_count(pj, pu))

            w1, w2 = a["w_mlp1"][0], a["w_mlp2"][0]

            def load_w1(j, e):
                for u in range(W1U):
                    slot_free(j, u)
                    slot, _ = raw_at(j, u)
                    sp.dma_start(raw[slot][:, :], w1[e, u * P:(u + 1) * P, :].rearrange("e p n -> p (e n)"))\
                        .then_inc(raw_in[slot], 16)

            def load_w2(j, e, first):
                for v in range(W2U):
                    slot_free(j, first + v)
                    slot, _ = raw_at(j, first + v)
                    sp.dma_start(raw[slot][:, :].rearrange("p (k n) -> p k n", k=2),
                                 w2[e, 2 * v * P:(2 * v + 2) * P, :].rearrange("e (k p) n -> p (e k) n", p=P))\
                        .then_inc(raw_in[slot], 16)

            load_w1(0, slice(0, 1))
            def expert(j):
                return bass.ds(sp.value_load(items[0:1, bass.ds(j, 1)], min_val=0, max_val=NE - 1), 1)

            load_w1(1, slice(1, 2))
            load_w2(1, slice(0, 1), W1U)
            late_in_sbuf(sp, ("tab",))
            n_items = number_of_items(sp)
            with sp.Fori(2, n_items) as j:
                load_w1(j, expert(j))
                load_w2(j, expert(j - 1), W1U)
            load_w2(n_items, expert(n_items - 1), 0)
            for i, (n, t) in enumerate([(n, t) for n in range(2) for t in range(TT)]):
                sp.wait_ge(sc_add, 4 * (n_items - 2) + (i + 1))
                sp.dma_start(out[0, t * P:(t + 1) * P, 512 * n:512 * n + 512], X[:, t, 512 * n:512 * n + 512]).then_inc(out_dma, 16)
            sp.wait_ge(out_dma, 16 * 4)

        @block.gpsimd
        def _(pool):
            def load_router(pool):
                pool.dma_start(gffn[:, :], a["g_ffn"][0:1, :].to_broadcast([P, D])).then_inc(bcast_in, 16)
                pool.dma_start(brt[:, :], a["b_router"][0:1, :].to_broadcast([P, NE])).then_inc(bcast_in, 16)
                pool.dma_start(wr[:, :, :], a["w_router"][0].rearrange("(k p) e -> p k e", p=P)).then_inc(bcast_in, 16)

            pool.wait_ge(unit_used, 4)
            for i in range(6):
                if i == 2:
                    load_router(pool)
                if i >= 2:
                    pool.wait_ge(pair_sem(f"gate{i - 2}"), GI[f"gate{i - 2}"] // 2 + 1)
                pool.dma_start(bg[:, i % 2, :], a["b_gate"][0:1, 512 * i:512 * i + 512].to_broadcast([P, 512])).then_inc(bias_in[i % 2], 16)
            pool.wait_ge(pair_sem("gate5"), GI["gate5"] // 2 + 1)
            for t in range(TT):
                pool.wait_ge(task_done, TASKS[("oT", "moba", t)] + 1)
            pool.dma_start(b2s, a["b_mlp2"][0]).then_inc(b2_in, 16)
            pool.dma_start(bsel[:, 0:NE], a["misc"][0:64, 4 * P + 64:4 * P + 64 + NE]).then_inc(b2_in, 16)
            pool.memset(b1s[64:P, :].bitcast(F32), 0.0).then_inc(zeroed, 1)
            pool.wait_ge(silu_done, 2)
            pool.wait_ge(y_done, 4)
            pool.wait_ge(b1l, 1)
            pool.wait_ge(zeroed, 1)
            pool.memset(BL[:, :].bitcast(F32), 0.0).then_inc(zeroed, 1)
            for t in range(TT):
                pool.wait_ge(xh_done, t + 1)
                if t:
                    pool.wait_ge(xl_done, t)
                pool.tensor_tensor(xtl[:, t, :], hx[:, t, :], xth[:, t, :].bitcast(F32), ALU.subtract).then_inc(xl_done, 1)

        @block.scalar
        def _(act):
            act.dma_start(misc[:, :], a["misc"]).then_inc(const_in, 16)
            act.dma_start(gains[:, :], a["gains"]).then_inc(const_in, 16)
            def roots(name, count, n):
                i = NORMS.index(name)
                act.wait_ge(sq_done, sum(SQUARES[:i + 1]))
                if SUMS[i]:
                    act.wait_ge(ss_done, sum(SUMS[:i + 1]))
                act.activation(stat[:, 1, 16 * i:16 * i + count], stat[:, 0, 16 * i:16 * i + count], ACT.Sqrt,
                               bias=eps, scale=1.0 / n).then_inc(sd_done, 1)

            def row_squares(name, src):
                i = NORMS.index(name)
                for t in range(TT):
                    if sum(SQUARES[:i]) + t:
                        act.wait_ge(sq_done, sum(SQUARES[:i]) + t)
                    act.activation(sq, src[:, t, :], ACT.Square,
                                   accum_out=stat[:, 0, 16 * i + t:16 * i + t + 1]).then_inc(sq_done, 1)
                roots(name, TT, D)

            def load_table(func, column):
                act.activation(spare[:, column:column + 1], spare[:, 0:1], func)

            def high(j, u):
                if native(j, u):
                    return
                slot, uses = raw_at(j, u)
                act.wait_ge(raw_in[slot], uses * 16)
                if not (isinstance(j, int) and split_count(j, u) <= HL):
                    act.wait_ge(hl_used, split_count(j, u) - HL)
                act.activation(hi[hl_slot(j, u)][:, :], raw[slot][:, :], ACT.Copy).then_inc(hi_done, 1)

            def mix_high(m):
                k = SPLIT_UNITS.index(m)
                act.wait_ge(raw_in[m % MIX_RING], 16 * (m // MIX_RING + 1))
                if HI_LAST[k] is not None:
                    act.wait_ge(unit_used, SPLIT_UNITS[HI_LAST[k]] + 1)
                elif k >= SPLIT_3:
                    act.wait_ge(silu_done, 2)
                    act.wait_ge(task_done, TASKS[("pv", MOBA_H - 1)] + 1)
                act.activation(mix_high_part(m)[:, :], raw[m % MIX_RING][:, :], ACT.Copy).then_inc(wh_done, 1)

            act.wait_ge(warm, 1)
            load_table(ACT.Sqrt, 1)
            for t in range(TT):
                act.wait_ge(x_half[t], 16)
                if t:
                    act.wait_ge(sq_done, t)
                act.activation(sq, X[:, t, :], ACT.Square, accum_out=stat[:, 0, t:t + 1]).then_inc(sq_done, 1)
            act.wait_ge(const_in, 16 * N_CONST)
            roots("x", TT, D)
            act.wait_ge(mem_in, 16)
            row_squares("mem", mem)
            act.dma_start(decay, a["decay"]).then_inc(table_in, 16)
            act.dma_start(alibi[:, :], a["alibi"]).then_inc(table_in, 16)

            for step in STEPS:
                if step[0] == "split":
                    mix_high(step[1])
                elif step[0] == "half":
                    pass
                elif step[0] == "group":
                    g = step[1]
                    P2 = pair[GI[g] % 2]
                    if g in ("rqk", "mq"):
                        src = int(g == "mq")
                        for t in range(TT):
                            for kk in range(2):
                                in_sbuf(act, ("hT", src, t, kk))
                        act.activation((hTh, mTh)[src][:, :, :], hTf, ACT.Copy).then_inc(hTh_done, 1)
                    if g in ("mq", "mk", "cq", "ck"):
                        act.wait_ge(unit_used, UNITS_DONE[GI[g]])
                        act.wait_ge(sq_done, sum(SQUARES[:NORMS.index(g)]))
                        act.activation(sq.rearrange("p (t n) -> p t n", t=TT), P2, ACT.Square).then_inc(sq_done, 1)
                        heads = TT * (MOBA_H if g[0] == "m" else MEM_H)
                        roots(g, heads, MOBA_HD if g[0] == "m" else MEM_HD)
                    elif g in V:
                        act.wait_ge(unit_used, UNITS_DONE[GI[g]])
                        act.activation(V[g][:, :, :], P2, ACT.Copy).then_inc(pair_sem(g), 1)
                    elif g == "gate4":
                        act.wait_ge(pair_sem("rg"), GI["rg"] // 2 + 1)
                        act.activation(rgs, V["rg"][:, :, :], ACT.Sigmoid).then_inc(sig_done, 1)
                        for i in range(3):
                            sigmoid_gate(act, i)
                    elif g == "gate5":
                        for i in range(3, 6):
                            sigmoid_gate(act, i)
                else:
                    key = step[1:]
                    kind, b = key[0], bank(key)
                    if kind == "ret_o":
                        hp = key[1]
                        act.wait_ge(task_done, TASKS[key] + 1)
                        act.wait_ge(sq_done, sum(SQUARES[:NORMS.index(f"ret{hp}")]))
                        act.activation(sq[:, 0:512], b, ACT.Square).then_inc(sq_done, 1)
                        roots(f"ret{hp}", 2 * TT, RET_DV)
                    elif kind == "sc":
                        h = key[1]
                        act.wait_ge(max_done, 2 * h + 2)
                        pr = probs[h % 4]
                        if HEADS[h][0] == "mem" and h >= 4:
                            act.wait_ge(task_done, TASKS[("pT", h - 4)] + 1)
                        for it in range(TT):
                            cols = slice(it * S, (it + 1) * S)
                            act.activation(pr[:, cols], (pr if HEADS[h][0] == "moba" else b)[:, cols], ACT.Exp,
                                           bias=smx[:, 1, 2 * h + it:2 * h + it + 1],
                                           accum_out=smx[:, 2, 2 * h + it:2 * h + it + 1]).then_inc(exp_done, 1)
                    elif kind == "pT":
                        h = key[1]
                        n = 384 if HEADS[h][0] == "moba" else 512
                        act.wait_ge(task_done, TASKS[key] + 1)
                        if h >= 4:
                            act.wait_ge(task_done, TASKS[("pv", h - 4)] + 1)
                        act.activation(PT[h % 4][:, 0:n], b[:, 0:n], ACT.Copy).then_inc(read_sem(key), 1)
                    elif kind == "oT":
                        br, t = key[1:]
                        act.wait_ge(task_done, TASKS[key] + 1)
                        act.activation(oTp[br][0][:, :, t * P:(t + 1) * P], b.rearrange("p (c s) -> p c s", s=P), ACT.Copy,
                                       scale=qgain[:, 4:5] if br == "ret" else 1.0).then_inc(part_high, 1)
                    elif kind == "yT":
                        n, t = key[1:]
                        act.wait_ge(task_done, TASKS[key] + 1)
                        act.activation(hTh[:, 4 * n:4 * n + 4, t * P:(t + 1) * P], b.rearrange("p (c s) -> p c s", s=P),
                                       ACT.Copy).then_inc(part_high, 1)
                    elif kind == "xT":
                        t, kk = key[1:]
                        act.wait_ge(task_done, TASKS[key] + 1)
                        if t == 0:
                            for c in range(4):
                                ins = act.activation(mT[:, 4 * kk + c, t * P:(t + 1) * P], b[:, c * P:(c + 1) * P], ACT.Copy,
                                                     scale=fcol[:, 4 * kk + c:4 * kk + c + 1])
                            ins.then_inc(read_sem(key), 1)
                        if (t, kk) == (1, 1):
                            act.wait_ge(ss_done, sum(SUMS))
                            roots("x2", TT, D)
                            load_table(ACT.Exp, 2)
                            for i in range(TT):
                                act.wait_ge(xt_done, i + 1)
                                act.activation(xth[:, i, :], hx[:, i, :], ACT.Copy).then_inc(xh_done, 1)
                            high(0, 1)
                    elif kind == "pos":
                        act.wait_ge(rout, RI["nv"])
                        for t in range(TT):
                            act.activation(e4[:, t, :], v8[:, t, 0:4], ACT.Exp, bias=nv[:, t:t + 1],
                                           accum_out=se[:, t:t + 1]).then_inc(rexp, 1)
                        load_table(ACT.Sigmoid, 3)
                        high(0, 2)
                if step == ("group", "br_moba0"):
                    act.wait_ge(task_done, TASKS[("pv", NH - 1)] + 1)
                    for half in range(2):
                        act.dma_start(b1raw[32 * half:32 * half + 32, :], a["b_mlp1"][0]).then_inc(b1_in, 16)
                if step == ("group", "br_mem1"):
                    load_table(ACT.Sqrt, 1)
                    act.wait_ge(b1_in, 32)
                    act.activation(b1s[0:64, :], b1raw, ACT.Copy).then_inc(b1h, 1)
                for n, t in {("half", "out0"): [(0, 0), (0, 1)], ("group", "out1"): [(1, 0)], ("half", "out1"): [(1, 1)]}.get(step, []):
                    act.wait_ge(x2_done, TT * n + t + 1)
                    act.wait_ge(sq_done, sum(SQUARES[:-1]) + TT * n + t)
                    act.activation(y[:, t, 512 * n:512 * n + 512], X[:, t, 512 * n:512 * n + 512], ACT.Square,
                                   accum_out=stat[:, 1, 8 + TT * n + t:9 + TT * n + t]).then_inc(sq_done, 1)
                    if (n, t) == (0, 1):
                        act.wait_ge(y_done, 4)
                        high(0, 0)

            def gathered(i):
                act.wait_ge(ga_pe, i * 2 + 1)
                act.activation(XG[:, :, 0:SL], banks[6].rearrange("p (k s) -> p k s", s=SL), ACT.Copy).then_inc(xgh, 1)

            def output_high(i):
                act.activation(YH[:, :], PS[:, 2048:3072], ACT.Copy).then_inc(yh, 1)

            def scatter_matrix(i):
                act.activation(ST[:, :], banks[7][:, 0:S], ACT.Copy).then_inc(st_act, 1)

            def body(j):
                later = not isinstance(j, int)
                for u in range(W1U):
                    if later or j or u >= HL:
                        high(j, u)
                    if u == 0 and (later or j >= 1):
                        act.wait_ge(tr_pe, j)
                        act.activation(AT[:, :, 0, :].rearrange("p (h c) s -> p h c s", h=2),
                                       banks[6].rearrange("p (c h s) -> p h c s", h=2, s=SL), ACT.Copy).then_inc(ath, 1)
                    if u == 1 and later:
                        unit_done(act, j - 1, IU - 1)
                        output_high(j - 2)
                    if u == (5 if not later and j == 0 else 3):
                        act.wait_ge(st_pe, j + 1)
                        if later:
                            scatter_matrix(j - 2)
                        if later or j >= 1:
                            act.wait_ge(swi, 6 * j)
                        act.activation(slotw[:, :], banks[7][:, S:S + 1], ACT.Copy).then_inc(slw, 1)
                if later or j >= 1:
                    for u in range(W1U, IU):
                        high(j, u)
                unit_done(act, j, W1U - 1)
                act.activation(HB[0:64, :], PS[64:P, 0:1024], ACT.Copy).then_inc(hb_act, 1)
                act.activation(HB[64:P, :], PS[0:64, 1024:2048], ACT.Copy).then_inc(hb_act, 1)
                gathered(j + 1)
                act.wait_ge(swi, 6 * j + 3)
                act.activation(sig, glu, ACT.Sigmoid, scale=ALPHA).then_inc(sgm, 1)

            gathered(0)
            body(0)
            body(1)
            n_items = number_of_items(act)
            with act.Fori(2, n_items) as j:
                body(j)
            j = n_items
            high(j, 0)
            act.wait_ge(tr_pe, j)
            act.activation(AT[:, :, 0, :].rearrange("p (h c) s -> p h c s", h=2),
                           banks[6].rearrange("p (c h s) -> p h c s", h=2, s=SL), ACT.Copy).then_inc(ath, 1)
            unit_done(act, j - 1, IU - 1)
            output_high(j - 2)
            high(j, 2)
            high(j, 3)
            act.wait_ge(st_pe, j + 1)
            act.activation(STL[:, :], banks[7], ACT.Copy).then_inc(st_act, 1)
            unit_done(act, j, W2U - 1)
            for n in range(2):
                act.activation(YH2[:, n * 512:n * 512 + 512], banks[n], ACT.Copy).then_inc(yh, 1)

        @block.vector
        def _(dve):
            def linked(ins, s, value):
                ins.then_inc(s, 1)
                dve.wait_ge(s, value)

            def reciprocal_roots(name, count):
                i = NORMS.index(name)
                dve.wait_ge(sd_done, i + 1)
                linked(dve.reciprocal(stat[:, 2, 16 * i:16 * i + count], stat[:, 1, 16 * i:16 * i + count]), rs_done, i + 1)
                return stat[:, 2, 16 * i:16 * i + count]

            def row_norm(i, src, dst):
                r = reciprocal_roots(NORMS[i], TT)
                for t in range(TT):
                    dve.tensor_scalar(dst[:, t, :], src[:, t, :], r[:, t:t + 1], None, ALU.mult).then_inc(hx_done, 1)

            def low(j, u):
                if native(j, u):
                    return
                slot, _ = raw_at(j, u)
                dve.wait_ge(hi_done, split_count(j, u))
                dve.tensor_tensor(lo[hl_slot(j, u)][:, :], raw[slot][:, :], hi[hl_slot(j, u)][:, :].bitcast(F32), ALU.subtract)\
                    .then_inc(lo_done, 1)

            def gather_matrix(i):
                for t in range(TT):
                    dve.tensor_scalar(SG[:, t, :], slotn, posi[:, t, bass.ds(i, 1)], None, ALU.is_equal).then_inc(sg_done, 1)
                dve.tensor_scalar(BL[0:64, 0:SL], ones[0:64, 0:SL], bsel[:, bass.ds(i, 1)], None, ALU.mult).then_inc(sg_done, 1)

            def mix_low(m):
                k = SPLIT_UNITS.index(m)
                dve.wait_ge(wh_done, k + 1)
                dve.tensor_tensor(rest[m % MIX_RING][:, :], raw[m % MIX_RING][:, :], mix_high_part(m)[:, :].bitcast(F32), ALU.subtract)\
                    .then_inc(wl_done, 1)

            dve.memset(spare[:, :], 1.0).then_inc(warm, 1)
            row_norm(0, X, hx)
            dve.wait_ge(const_in, 16 * N_CONST)
            for step in STEPS:
                if step[0] == "split":
                    mix_low(step[1])
                    continue
                if step[0] in ("group", "half"):
                    g = step[1]
                    P2 = pair[GI[g] % 2]
                    free = pair_sem(g)
                    if g == "rqk":
                        row_norm(1, mem, mem)
                    if g in ("rqk", "mq"):
                        src = int(g == "mq")
                        dve.wait_ge(hTh_done, src + 1)
                        dve.tensor_tensor((hTl, mTl)[src][:, :, :], hTf, (hTh, mTh)[src][:, :, :].bitcast(F32), ALU.subtract)\
                            .then_inc(hTl_done, 1)
                    if g == "rqk":
                        dve.wait_ge(unit_used, UNITS_DONE[GI[g]])
                        dve.tensor_copy(tq[0][:, :, :], P2).then_inc(free, 1)
                    elif g in ("mq", "mk", "cq", "ck"):
                        i, hd = NORMS.index(g), (MOBA_HD if g[0] == "m" else MEM_HD)
                        heads = 512 // hd
                        dve.wait_ge(sq_done, sum(SQUARES[:i + 1]))
                        dve.tensor_reduce(stat[:, 0, 16 * i:16 * i + TT * heads], sq.rearrange("p (g d) -> p g d", d=hd),
                                          AX.X, ALU.add).then_inc(ss_done, 1)
                        r = reciprocal_roots(g, TT * heads)
                        q = Q_GROUPS.index(g)
                        if q >= 2:
                            dve.wait_ge(task_done, TASKS[("qT", Q_GROUPS[q - 2], 1)] + 1)
                        dve.tensor_tensor(tq[q % 2][:, :, :].rearrange("p t (h d) -> p (t h) d", d=hd),
                                          P2.rearrange("p t (h d) -> p (t h) d", d=hd),
                                          r.rearrange("p (g o) -> p g o", o=1).to_broadcast([P, TT * heads, hd]),
                                          ALU.mult).then_inc(free, 1)
                    elif g.startswith("gate"):
                        i = int(g[-1])
                        dve.wait_ge(bias_in[i % 2], 16 * (i // 2 + 1))
                        dve.wait_ge(unit_used, UNITS_DONE[GI[g]])
                        for t in range(TT):
                            ins = dve.tensor_tensor(gates[:, t, 512 * i:512 * i + 512], P2[:, t, :], bg[:, i % 2, :], ALU.add)
                            if t:
                                ins.then_inc(free, 1)
                        if g == "gate4":
                            dve.wait_ge(sig_done, 1)
                            linked(dve.tensor_tensor(V["rg"][:, :, :], V["rg"][:, :, :], rgs, ALU.mult), silu_done, 1)
                            dve.tensor_tensor(o["ret"][:, :, :], o["ret"][:, :, :], V["rg"][:, :, :], ALU.mult).then_inc(silu_done, 1)
                    elif g.startswith("br_"):
                        n, br = int(g[-1]), g[3:-1]
                        gate = 2 * {"ret": 0, "moba": 1, "mem": 2}[br] + n
                        col = 512 * gate
                        half = slice(512 * n, 512 * n + 512)
                        dve.wait_ge(unit_used, UNITS_DONE[GI[g]])
                        dve.wait_ge(sig_done, gate + 2)
                        if br == BRANCH_ORDER[0][1]:
                            dve.tensor_tensor(y[:, :, half], P2, gates[:, :, col:col + 512], ALU.mult).then_inc(free, 1)
                        else:
                            linked(dve.tensor_tensor(tmp[:, :, :], P2, gates[:, :, col:col + 512], ALU.mult), free, GI[g] // 2 + 1)
                            k = 2 * n + (br == BRANCH_ORDER[-1][1]) + 1
                            if k % 2:
                                first = f"br_{BRANCH_ORDER[0][1]}{n}"
                                dve.wait_ge(pair_sem(first), GI[first] // 2 + 1)
                            linked(dve.tensor_tensor(y[:, :, half], y[:, :, half], tmp[:, :, :], ALU.add), y_done, k)
                    elif g.startswith("out"):
                        n = int(g[-1])
                        half = slice(512 * n, 512 * n + 512)
                        rows = {("half", "out0"): [0, 1], ("group", "out1"): [0], ("half", "out1"): [1]}.get(step, [])
                        for t in rows:
                            if n == 1 and t == 0:
                                dve.wait_ge(row0_done, 1)
                            else:
                                dve.wait_ge(unit_used, UNITS_DONE[GI[g]])
                            dve.tensor_tensor(X[:, t, half], X[:, t, half], P2[:, t, :], ALU.add).then_inc(x2_done, 1)
                        if step == ("half", "out0"):
                            dve.wait_ge(b1h, 1)
                            dve.tensor_tensor(b1s[32:64, :], b1raw[32:64, :], b1s[32:64, :].bitcast(F32), ALU.subtract)\
                                .then_inc(b1l, 1)
                            low(0, 0)
                    continue
                key = step[1:]
                kind, b = key[0], bank(key)
                done = read_sem(key)
                blocks = b.rearrange("p (c s) -> p c s", s=P)
                if kind == "hT":
                    src, t, kk = key[1:]
                    dve.wait_ge(task_done, TASKS[key] + 1)
                    if src:
                        dve.wait_ge(hTl_done, 1)
                    c = src * KC + 4 * kk
                    dve.tensor_tensor(hTf[:, 4 * kk:4 * kk + 4, t * P:(t + 1) * P], blocks,
                                      gcol[:, c:c + 4].rearrange("p (c o) -> p c o", o=1).to_broadcast([P, 4, P]),
                                      ALU.mult).then_inc(done, 1)
                elif kind == "qT":
                    g, t = key[1:]
                    dst = qTs[g][:, :, t * P:(t + 1) * P]
                    dve.wait_ge(task_done, TASKS[key] + 1)
                    if g == "rqk":
                        dve.tensor_copy(dst, blocks).then_inc(done, 1)
                    else:
                        c = ("mq", "mk", "cq", "ck").index(g)
                        scale = {"mq": MOBA_HD ** -0.5, "cq": MEM_HD ** -0.5}.get(g, 1.0)
                        dve.tensor_scalar(dst, blocks, qgain[:, c:c + 1], scale, ALU.mult, ALU.mult).then_inc(done, 1)
                elif kind == "ret_s":
                    h = key[1]
                    dve.wait_ge(task_done, TASKS[key] + 1)
                    if h == 0:
                        dve.wait_ge(table_in, 16 * N_TABLE)
                    if h >= 2:
                        dve.wait_ge(task_done, TASKS[("ret_o", h // 2 - 1)] + 1)
                    dve.tensor_tensor(retS[h % 2], b[:, 0:384], decay[:, 384 * h:384 * h + 384], ALU.mult).then_inc(done, 1)
                elif kind == "ret_o":
                    hp = key[1]
                    i = NORMS.index(f"ret{hp}")
                    dve.wait_ge(sq_done, sum(SQUARES[:i + 1]))
                    dve.tensor_reduce(stat[:, 0, 16 * i:16 * i + 4], sq[:, 0:512].rearrange("p (g d) -> p g d", d=RET_DV),
                                      AX.X, ALU.add).then_inc(ss_done, 1)
                    r = reciprocal_roots(f"ret{hp}", 4)
                    dve.tensor_tensor(o["ret"][:, :, 256 * hp:256 * hp + 256].rearrange("p t (h d) -> p t h d", d=RET_DV),
                                      b.rearrange("p (t h d) -> p t h d", t=TT, d=RET_DV),
                                      r.rearrange("p (t h o) -> p t h o", t=TT, o=1).to_broadcast([P, TT, 2, RET_DV]),
                                      ALU.mult).then_inc(done, 1)
                elif kind == "sc":
                    h = key[1]
                    hh, moba = HEADS[h][1], HEADS[h][0] == "moba"
                    cols = slice(2 * h, 2 * h + 2)
                    dve.wait_ge(task_done, TASKS[key] + 1)
                    src = b
                    if moba:
                        if h >= 4:
                            dve.wait_ge(task_done, TASKS[("pT", h - 4)] + 1)
                        src = probs[h % 4]
                        dve.scalar_tensor_tensor(src, alibi[:, :], 2.0 ** (-8.0 * (hh + 1) / MOBA_H), b, ALU.mult, ALU.add)\
                            .then_inc(done, 1)
                        in_sbuf(dve, key)
                    linked(dve.tensor_reduce(smx[:, 0, cols], src.rearrange("p (t s) -> p t s", s=S), AX.X, ALU.max),
                           max_done, 2 * h + 1)
                    dve.tensor_scalar(smx[:, 1, cols], smx[:, 0, cols], -1.0, None, ALU.mult).then_inc(max_done, 1)
                    dve.wait_ge(exp_done, 2 * h + 2)
                    dve.reciprocal(smx[:, 3, cols], smx[:, 2, cols]).then_inc(rcp_done if moba else done, 1)
                elif kind == "pv":
                    h = key[1]
                    br, hh = HEADS[h]
                    hd = MOBA_HD if br == "moba" else MEM_HD
                    dve.wait_ge(task_done, TASKS[key] + 1)
                    if br == "moba":
                        dve.wait_ge(rcp_done, h + 1)
                    else:
                        in_sbuf(dve, ("sc", h))
                    dve.tensor_tensor(o[br][:, :, hh * hd:(hh + 1) * hd],
                                      b[:, 0:TT * hd].rearrange("p (t d) -> p t d", d=hd),
                                      smx[:, 3, 2 * h:2 * h + 2].rearrange("p (t o) -> p t o", o=1).to_broadcast([P, TT, hd]),
                                      ALU.mult).then_inc(done, 1)
                elif kind in ("oT", "yT"):
                    t = key[2]
                    dve.wait_ge(part_high, PARTS.index(key) + 1)
                    if kind == "yT":
                        n = key[1]
                        high_part, low_part = (p[:, 4 * n:4 * n + 4, t * P:(t + 1) * P] for p in (hTh, hTl))
                    else:
                        high_part, low_part = (p[:, :, t * P:(t + 1) * P] for p in oTp[key[1]])
                    if key[1] == "ret":
                        dve.scalar_tensor_tensor(low_part, blocks, qgain[:, 4:5], high_part.bitcast(F32), ALU.mult, ALU.subtract)\
                            .then_inc(done, 1)
                    else:
                        dve.tensor_tensor(low_part, blocks, high_part.bitcast(F32), ALU.subtract).then_inc(done, 1)
                elif kind == "xT":
                    t, kk = key[1:]
                    if t == 1:
                        dve.wait_ge(task_done, TASKS[key] + 1)
                        dve.tensor_tensor(mT[:, 4 * kk:4 * kk + 4, P:S], blocks,
                                          fcol[:, 4 * kk:4 * kk + 4].rearrange("p (c o) -> p c o", o=1).to_broadcast([P, 4, P]),
                                          ALU.mult).then_inc(done, 1)
                    if (t, kk) == (1, 1):
                        dve.wait_ge(sq_done, sum(SQUARES))
                        i = NORMS.index("x2")
                        dve.tensor_tensor(stat[:, 0, 16 * i:16 * i + TT], stat[:, 1, 8:8 + TT], stat[:, 1, 10:10 + TT], ALU.add)\
                            .then_inc(ss_done, 1)
                        r = reciprocal_roots("x2", TT)
                        for i in range(TT):
                            dve.scalar_tensor_tensor(hx[:, i, :], X[:, i, :], r[:, i:i + 1], gffn[:, :], ALU.mult, ALU.mult)\
                                .then_inc(xt_done, 1)
                elif kind == "pos":
                    r = stat[:, 2, 16 * NORMS.index("x2"):]
                    for t in range(TT):
                        dve.wait_ge(logits_done, t + 1)
                        dve.scalar_tensor_tensor(lg[:, t, :], pair[GI["out0"] % 2][:, t, 0:NE], r[:, t:t + 1], brt[:, :],
                                                 ALU.mult, ALU.add).then_inc(rout, 1)
                    dve.wait_ge(rout, RI["lg1"])
                    for t in range(TT):
                        dve.max(v8[:, t, :], lg[:, t, :]).then_inc(rout, 1)
                    dve.wait_ge(rout, RI["max1"])
                    for t in range(TT):
                        dve.max_index(i8[:, t, :], v8[:, t, :], lg[:, t, :]).then_inc(rout, 1)
                    dve.tensor_scalar(nv[:, :], v8[:, :, 0], -1.0, None, ALU.mult).then_inc(rout, 1)
                    dve.wait_ge(rout, RI["mi1"])
                    linked(dve.tensor_copy(i8f[:, :, :], i8[:, :, :]), rout, RI["if"])
                    for t in range(TT):
                        dve.tensor_tensor(oh[:, t, :, :], iota32.rearrange("p (o e) -> p o e", o=1).to_broadcast([P, 4, NE]),
                                          i8f[:, t, 0:4].rearrange("p (k o) -> p k o", o=1).to_broadcast([P, 4, NE]),
                                          ALU.is_equal).then_inc(rout, 1)
                    dve.wait_ge(rout, RI["oh1"])
                    for t in range(TT):
                        dve.tensor_reduce(MG[:, t, :], oh[:, t, :, :].rearrange("p k e -> p e k"), AX.X, ALU.add).then_inc(rout, 1)
                    dve.wait_ge(task_done, TASKS[key] + 1)
                    dve.scalar_tensor_tensor(posm, b[:, 0:TT * NE].rearrange("p (t e) -> p t e", t=TT), 1.0,
                                             MG[:, :, :], ALU.add, ALU.mult).then_inc(done, 1)
                    in_sbuf(dve, key)
                    dve.tensor_scalar(posm, posm, -1.0, None, ALU.add).then_inc(rout, 1)
                    dve.wait_ge(rout, RI["posm"])
                    dve.wait_ge(zeroed, 2)
                    dve.wait_ge(b2_in, 32)
                    gather_matrix(0)
                    dve.wait_ge(rexp, TT)
                    linked(dve.reciprocal(se[:, TT:2 * TT], se[:, 0:TT]), rout, RI["rse"])
                    linked(dve.tensor_tensor(e4[:, :, :], e4[:, :, :],
                                             se[:, TT:2 * TT].rearrange("p (t o) -> p t o", o=1).to_broadcast([P, TT, 4]), ALU.mult),
                           rout, RI["w4"])
                    for t in range(TT):
                        dve.tensor_tensor(ohw[:, t, :, :], oh[:, t, :, :],
                                          e4[:, t, :].rearrange("p (k o) -> p k o", o=1).to_broadcast([P, 4, NE]),
                                          ALU.mult).then_inc(rout, 1)
                    dve.wait_ge(rout, RI["ow1"])
                    for t in range(TT):
                        dve.tensor_reduce(G[:, t, :], ohw[:, t, :, :].rearrange("p k e -> p e k"), AX.X, ALU.add).then_inc(rout, 1)

            def scatter_matrix(i):
                for t in range(TT):
                    dve.tensor_scalar(SS[:, t, :], slotn, posi[:, t, bass.ds(i, 1)], None, ALU.is_equal).then_inc(ss_mat, 1)

            def gathered(i):
                dve.wait_ge(ga_pe, i * 2 + 2)
                dve.tensor_copy(XG[:, :, SL:2 * SL], banks[7].rearrange("p (k s) -> p k s", s=SL)).then_inc(xgl, 1)

            def activations_low(j):
                dve.wait_ge(ath, j)
                dve.tensor_tensor(AT[:, :, 1, :].rearrange("p (h c) s -> p h c s", h=2),
                                  banks[6].rearrange("p (c h s) -> p h c s", h=2, s=SL),
                                  AT[:, :, 0, :].bitcast(F32).rearrange("p (h c) s -> p h c s", h=2), ALU.subtract).then_inc(atl, 1)

            def output_low(i):
                dve.wait_ge(yh, i + 1)
                dve.tensor_tensor(YL[:, :], PS[:, 2048:3072], YH[:, :].bitcast(F32), ALU.subtract).then_inc(yl, 1)

            def add(i, q):
                t, n = q // 2, q % 2
                dve.wait_ge(sc_pe, 4 * i + (q + 1))
                dve.tensor_tensor(X[:, t, 512 * n:512 * n + 512], X[:, t, 512 * n:512 * n + 512], banks[6 + q % 2], ALU.add)\
                    .then_inc(sc_add, 1)

            def late_task(key):
                kind, b, done = key[0], late_bank(key), late_read[LATE.index(key) % 2]
                if kind == "cnt":
                    dve.wait_ge(late_done, LATE.index(key) + 1)
                    dve.tensor_copy(rt[:, 0:1], b[0:NE, 0:1]).then_inc(done, 1)
                    late_in_sbuf(dve, key)
                    dve.wait_ge(rout, RI["g1"])
                    linked(dve.tensor_scalar(rt[:, 1:4], thresholds[0:NE, :], rt[:, 0:1], None, ALU.is_lt), rout, RI["g3"])
                    linked(dve.tensor_reduce(rt[:, 4:5], rt[:, 1:4], AX.X, ALU.add), rout, RI["n"])
                elif kind == "tabT":
                    dve.wait_ge(late_done, LATE.index(key) + 1)
                    dve.tensor_copy(tabT[:, :, :], b[0:NE, :].rearrange("p (a s) -> p a s", a=2)).then_inc(done, 1)
                elif kind == "off":
                    dve.wait_ge(late_done, LATE.index(key) + 1)
                    linked(dve.tensor_copy(rt[:, 5:6], b[0:NE, 0:1]), rout, RI["off"])
                    dve.tensor_copy(items[0:1, MAX_ITEMS:MAX_ITEMS + 1], b[0:1, 2:3]).then_inc(done, 1)
                    linked(dve.tensor_scalar(rt[:, 6:9], iota32[0:NE, 0:3], rt[:, 5:6], None, ALU.add), rout, RI["offr"])
                    sel = [rt[:, 16 + 16 * r:32 + 16 * r] for r in range(3)]
                    for r in range(3):
                        dve.tensor_scalar(sel[r], iota32[0:NE, 0:16], rt[:, 6 + r:7 + r], rt[:, 1 + r:2 + r], ALU.is_equal, ALU.mult)\
                            .then_inc(rout, 1)
                    dve.wait_ge(rout, RI["s3"])
                    linked(dve.tensor_tensor(selw[:, 0, NE:], sel[0], sel[1], ALU.add), rout, RI["t1"])
                    linked(dve.tensor_tensor(selw[:, 0, NE:], selw[:, 0, NE:], sel[2], ALU.add), rout, RI["t2"])
                    linked(dve.scalar_tensor_tensor(selw[:, 1, NE:], sel[1], 2.0, sel[0], ALU.mult, ALU.add), rout, RI["u1"])
                    linked(dve.scalar_tensor_tensor(selw[:, 1, NE:], sel[2], 3.0, selw[:, 1, NE:], ALU.mult, ALU.add), rout, RI["u2"])
                    dve.tensor_scalar(selw[:, 1, NE:], selw[:, 1, NE:], -float(SL), None, ALU.mult).then_inc(rout, 1)
                    dve.tensor_copy(selw[:, 0, 0:NE], ident[0:NE, 0:NE]).then_inc(rout, 1)
                    dve.memset(selw[:, 1, 0:NE], 0.0).then_inc(rout, 1)
                elif kind == "tab":
                    dve.wait_ge(late_done, LATE.index(key) + 1)
                    m = MAX_ITEMS - NE
                    dve.tensor_copy(posi[:, :, NE:], b[:, 0:2 * m].rearrange("p (t j) -> p t j", t=TT)).then_inc(rout, 1)
                    dve.tensor_copy(gi[:, :, NE:], b[:, 2 * m:4 * m].rearrange("p (t j) -> p t j", t=TT)).then_inc(rout, 1)
                    dve.tensor_copy(bsel[:, NE:], b[0:64, 4 * m:5 * m]).then_inc(rout, 1)
                    dve.tensor_copy(items[0:1, 0:NE], iota32[0:1, :]).then_inc(rout, 1)
                    dve.tensor_copy(items[0:1, NE:MAX_ITEMS], b[0:1, 5 * m:6 * m]).then_inc(done, 1)
                elif kind == "b2":
                    t, n = key[1:]
                    dve.wait_ge(late_done, LATE.index(key) + 1)
                    dve.tensor_tensor(X[:, t, 512 * n:512 * n + 512], X[:, t, 512 * n:512 * n + 512], b, ALU.add).then_inc(done, 1)

            def body(j):
                later = not isinstance(j, int)
                for u in range(W1U):
                    if later or j or u >= HL:
                        low(j, u)
                    if u == 0 and (later or j >= 1):
                        activations_low(j)
                    for key in [] if later else LATE_DVE.get((j, u), []):
                        late_task(key)
                    if u == 1 and later:
                        output_low(j - 2)
                        dve.wait_ge(st_pe, j)
                        scatter_matrix(j - 2)
                    if later and u in (5, 7):
                        for q in ((0, 1) if u == 5 else (2, 3)):
                            add(j - 2, q)
                dve.wait_ge(st_pe, j + 1)
                gather_matrix(j + 1)
                if later or j >= 1:
                    for u in range(W1U, IU):
                        low(j, u)
                dve.wait_ge(hb_act, 2 * j + 1)
                dve.tensor_tensor(HS[0:64, :], PS[0:64, 0:1024], HB[0:64, :], ALU.add).then_inc(swi, 1)
                dve.wait_ge(hb_act, 2 * j + 2)
                dve.tensor_tensor(HS[64:P, :], PS[64:P, 1024:2048], HB[64:P, :], ALU.add).then_inc(swi, 1)
                dve.wait_ge(swi, 6 * j + 2)
                dve.tensor_scalar(glu, HS[:, 0:1024:2], LIMIT, None, ALU.min).then_inc(swi, 1)
                dve.tensor_scalar(lin, HS[:, 1:1024:2], LIMIT, -LIMIT, ALU.min, ALU.max).then_inc(swi, 1)
                gathered(j + 1)
                dve.wait_ge(swi, 6 * j + 4)
                dve.scalar_tensor_tensor(lin, lin, 1.0, glu, ALU.add, ALU.mult).then_inc(swi, 1)
                dve.wait_ge(swi, 6 * j + 5)
                dve.wait_ge(sgm, j + 1)
                dve.wait_ge(slw, j + 1)
                dve.scalar_tensor_tensor(act_t, lin, slotw[:, 0:1], sig, ALU.mult, ALU.mult).then_inc(swi, 1)
                for key in [] if later else LATE_DVE.get((j, END), []):
                    late_task(key)

            late_task(("cnt",))
            low(0, 1)
            gathered(0)
            low(0, 2)
            late_task(("off",))
            late_task(("tabT",))
            body(0)
            dve.wait_ge(rout, RI["bsel"])
            body(1)
            n_items = number_of_items(dve)
            with dve.Fori(2, n_items) as j:
                body(j)
            j = n_items
            low(j, 0)
            dve.wait_ge(st_pe, j)
            scatter_matrix(j - 2)
            for t in range(TT):
                dve.tensor_scalar(SS2[:, t, :], slotn, posi[:, t, bass.ds(j - 1, 1)], None, ALU.is_equal).then_inc(ss_mat, 1)
            activations_low(j)
            output_low(j - 2)
            low(j, 2)
            low(j, 3)
            for n in range(2):
                dve.wait_ge(yh, j + n)
                dve.tensor_tensor(YL2[:, n * 512:n * 512 + 512], banks[n], YH2[:, n * 512:n * 512 + 512].bitcast(F32), ALU.subtract)\
                    .then_inc(yl, 1)
            for i, (n, t) in enumerate([(n, t) for n in range(2) for t in range(TT)]):
                dve.wait_ge(sc_pe, 4 * (j - 2) + (i + 1))
                dve.tensor_tensor(X[:, t, 512 * n:512 * n + 512], X[:, t, 512 * n:512 * n + 512], banks[4 + i], ALU.add)\
                    .then_inc(sc_add, 1)

        @block.tensor
        def _(pe):
            def keep_warm(count):
                for _ in range(count):
                    pe.transpose(pair[GI["out1"] % 2][:, 0, 0:P], ident, ident)

            unit = 0
            for step in STEPS:
                if step[0] == "split":
                    continue
                if step[0] in ("group", "half"):
                    g = step[1]
                    gi_, kc = GI[g], dict(GROUPS)[g]
                    if g == "rqk":
                        for t in range(TT):
                            for kk in range(2):
                                in_sbuf(pe, ("hT", 0, t, kk))
                    if g == "mq":
                        pe.wait_ge(hTl_done, 1)
                    if g == "ck":
                        pe.wait_ge(hTl_done, 2)
                    if g.startswith("br_"):
                        for t in range(TT):
                            in_sbuf(pe, ("oT", g[3:-1], t))
                    if g == "out0":
                        for t in range(TT):
                            in_sbuf(pe, ("yT", int(step[0] == "half"), t))
                    if gi_ >= 2 and step[0] == "group":
                        pe.wait_ge(pair_free[gi_ % 2], gi_ // 2)
                    src = hTf
                    parts = oTp[g[3:-1]] if g.startswith("br_") else (mTh, mTl) if g in ("ck", "cv") else (hTh, hTl)
                    units = list(range(kc // 4))
                    order = [(t, hk) for hk in units for t in range(TT)]
                    if g == "out0":
                        order = [(t, int(step[0] == "half")) for t in range(TT)]
                    if g == "out1":
                        order = [(int(step[0] == "half"), hk) for hk in units]
                    for t, hk in order:
                        m = unit + hk
                        w = raw[m % MIX_RING][:, :].rearrange("p (k n) -> p k n", k=4)
                        if t == 0 and g in NATIVE_GROUPS:
                            pe.wait_ge(raw_in[m % MIX_RING], 16 * (m // MIX_RING + 1))
                        elif t == 0:
                            pe.wait_ge(wl_done, SPLIT_UNITS.index(m) + 1)
                        for kk in range(4):
                            k = 4 * hk + kk
                            rows = slice(t * P, (t + 1) * P)
                            if g in NATIVE_GROUPS:
                                mm = pe.matmul(pair[gi_ % 2][:, t, :], src[:, k, rows], w[:, kk, :], start=(k == 0), stop=(k == kc - 1))
                            else:
                                wh = mix_high_part(m)[:, :].rearrange("p (k n) -> p k n", k=4)[:, kk, :]
                                wl = rest[m % MIX_RING][:, :].rearrange("p (k n) -> p k n", k=4)[:, kk, :]
                                pe.matmul(pair[gi_ % 2][:, t, :], parts[0][:, k, rows], wh, start=(k == 0), stop=False)
                                pe.matmul(pair[gi_ % 2][:, t, :], parts[0][:, k, rows], wl, start=False, stop=False)
                                mm = pe.matmul(pair[gi_ % 2][:, t, :], parts[1][:, k, rows], wh, start=False, stop=(k == kc - 1))
                        if t == 1:
                            mm.then_inc(unit_used, 1)
                        elif g == "out1" and hk == units[-1]:
                            mm.then_inc(row0_done, 1)
                    if step[0] == "half" or g not in ("out0", "out1"):
                        unit += kc // 4
                    continue
                key = step[1:]
                kind, b, n = key[0], bank(key), TASKS[key]
                if n >= 4:
                    pe.wait_ge(bank_read[n % 4], n // 4)

                def transposes(src, rows=P, blocks=4):
                    for c in range(blocks):
                        mm = pe.transpose(b[0:P, c * P:(c + 1) * P], src(c), ident)
                    return mm

                if kind == "hT":
                    s, t, kk = key[1:]
                    pe.wait_ge(const_in, 16 * N_CONST)
                    pe.wait_ge(hx_done, 2 * s + t + 1)
                    mm = transposes(lambda c: (hx, mem)[s][:, t, (4 * kk + c) * P:(4 * kk + c + 1) * P])
                elif kind == "qT":
                    g, t = key[1:]
                    pe.wait_ge(pair_sem(g), GI[g] // 2 + 1)
                    mm = transposes(lambda c: tq[Q_GROUPS.index(g) % 2][:, t, c * P:(c + 1) * P])
                elif kind == "ret_s":
                    h = key[1]
                    po, c = 64 * (h % 2), h // 2
                    q, k = qTs["rqk"][po:po + 64, c, :], qTs["rqk"][po:po + 64, 2 + c, :]
                    for t in range(TT):
                        in_sbuf(pe, ("qT", "rqk", t))
                    pe.matmul(b[:, 0:S], k[:, 0:P], q, start=True, stop=True)
                    mm = pe.matmul(b[:, S:384], k[:, P:S], q[:, P:S], start=True, stop=True)
                elif kind == "ret_o":
                    hp = key[1]
                    pe.wait_ge(pair_sem("rv"), GI["rv"] // 2 + 1)
                    for hh in range(2):
                        h = 2 * hp + hh
                        in_sbuf(pe, ("ret_s", h))
                        v = V["rv"][:, :, h * RET_DV:(h + 1) * RET_DV]
                        sc = retS[h % 2]
                        pe.matmul(b[:, hh * P:(hh + 1) * P], sc[:, 0:P], v[:, 0, :], start=True, stop=True)
                        ob = b[:, S + hh * P:S + (hh + 1) * P]
                        pe.matmul(ob, sc[:, P:S], v[:, 0, :], start=True, stop=False)
                        mm = pe.matmul(ob, sc[:, S:384], v[:, 1, :], start=False, stop=True)
                elif kind == "sc":
                    br, h = HEADS[key[1]]
                    gq, gk = ("mq", "mk") if br == "moba" else ("cq", "ck")
                    for t in range(TT):
                        in_sbuf(pe, ("qT", gq, t))
                        in_sbuf(pe, ("qT", gk, t))
                    rows, c = (slice(64 * (h % 2), 64 * (h % 2) + 64), h // 2) if br == "moba" else (slice(0, P), h)
                    for it in range(TT):
                        mm = pe.matmul(b[:, it * S:(it + 1) * S], qTs[gq][rows, c, it * P:(it + 1) * P], qTs[gk][rows, c, :],
                                       start=True, stop=True)
                elif kind == "pT":
                    h = key[1]
                    pe.wait_ge(exp_done, 2 * h + 2)
                    order = [(0, 0), (1, 0), (1, 1)] if HEADS[h][0] == "moba" else [(0, 0), (0, 1), (1, 0), (1, 1)]
                    mm = transposes(lambda c: probs[h % 4][:, order[c][0] * S + order[c][1] * P:order[c][0] * S + (order[c][1] + 1) * P],
                                    blocks=len(order))
                elif kind == "pv":
                    h = key[1]
                    br, hh = HEADS[h]
                    hd, vg = (MOBA_HD, "mv") if br == "moba" else (MEM_HD, "cv")
                    in_sbuf(pe, ("pT", h))
                    pe.wait_ge(pair_sem(vg), GI[vg] // 2 + 1)
                    order = [(0, 0), (1, 0), (1, 1)] if br == "moba" else [(0, 0), (0, 1), (1, 0), (1, 1)]
                    for c, (it, jt) in enumerate(order):
                        last = c + 1 == len(order) or order[c + 1][0] != it
                        mm = pe.matmul(b[:, it * hd:(it + 1) * hd], PT[h % 4][:, c * P:(c + 1) * P], V[vg][:, jt, hh * hd:(hh + 1) * hd],
                                       start=(jt == 0), stop=last)
                elif kind == "oT":
                    br, t = key[1:]
                    if br == "ret":
                        pe.wait_ge(silu_done, 2)
                    else:
                        for h in range(NH):
                            if HEADS[h][0] == br:
                                in_sbuf(pe, ("pv", h))
                    mm = transposes(lambda c: o[br][:, t, c * P:(c + 1) * P])
                elif kind == "yT":
                    nn, t = key[1:]
                    pe.wait_ge(y_done, 2 * nn + 2)
                    mm = transposes(lambda c: y[:, t, nn * 512 + c * P:nn * 512 + (c + 1) * P])
                elif kind == "xT":
                    t, kk = key[1:]
                    pe.wait_ge(x2_done, TT * kk + t + 1)
                    mm = transposes(lambda c: X[:, t, (4 * kk + c) * P:(4 * kk + c + 1) * P])
                elif kind == "pos":
                    pe.wait_ge(rout, RI["m1"])
                    pe.matmul(b[:, 0:NE], before, MG[:, 0, :], start=True, stop=True)
                    pe.matmul(b[:, NE:2 * NE], ones, MG[:, 0, :], start=True, stop=False)
                    mm = pe.matmul(b[:, NE:2 * NE], before, MG[:, 1, :], start=False, stop=True)
                mm.then_inc(task_done, 1)
                if key == ("xT", TT - 1, 1):
                    for kk in range(2):
                        for t in range(TT):
                            in_sbuf(pe, ("xT", t, kk))
                            if kk == 0 and t == 0:
                                pe.wait_ge(bcast_in, 16 * N_BCAST)
                                pe.wait_ge(x2_done, TT)
                            for k in range(4 * kk, 4 * kk + 4):
                                lm = pe.matmul(pair[GI["out0"] % 2][:, t, 0:NE], mT[:, k, t * P:(t + 1) * P], wr[:, k, :],
                                               start=(k == 0), stop=(k == KC - 1))
                            if kk == 1:
                                lm.then_inc(logits_done, 1)
                    keep_warm(28)

            def late_task(key):
                kind, b, n = key[0], late_bank(key), LATE.index(key)
                if n >= 2:
                    pe.wait_ge(late_read[n % 2], n // 2)
                if kind == "cnt":
                    for t in range(TT):
                        mm = pe.matmul(b[0:NE, 0:1], MG[:, t, :], ones[:, 0:1], start=(t == 0), stop=(t == 1))
                elif kind == "tabT":
                    pe.wait_ge(rout, RI["g1"])
                    for t in range(TT):
                        pe.transpose(b[0:NE, t * P:(t + 1) * P], posm[:, t, :], ident)
                        mm = pe.transpose(b[0:NE, S + t * P:S + (t + 1) * P], G[:, t, :], ident)
                elif kind == "off":
                    pe.wait_ge(rout, RI["n"])
                    pe.matmul(b[0:NE, 0:1], before[0:NE, 0:NE], rt[:, 4:5], start=True, stop=True)
                    mm = pe.matmul(b[0:1, 2:3], ones[0:NE, 0:1], rt[:, 4:5], start=True, stop=True)
                elif kind == "tab":
                    pe.wait_ge(rout, RI["sz"])
                    late_in_sbuf(pe, ("tabT",))
                    m = MAX_ITEMS - NE
                    for t in range(TT):
                        rows = slice(t * P, (t + 1) * P)
                        pe.matmul(b[:, t * m:(t + 1) * m], tabT[:, 0, rows], selw[:, 0, NE:], start=True, stop=False)
                        pe.matmul(b[:, t * m:(t + 1) * m], ones[0:NE, :], selw[:, 1, NE:], start=False, stop=True)
                        pe.matmul(b[:, (2 + t) * m:(3 + t) * m], tabT[:, 1, rows], selw[:, 0, NE:], start=True, stop=True)
                    pe.matmul(b[0:64, 4 * m:5 * m], twice, selw[:, 0, NE:], start=True, stop=True)
                    mm = pe.matmul(b[0:1, 5 * m:6 * m], iotap[0:NE, :], selw[:, 0, NE:], start=True, stop=True)
                elif kind == "b2":
                    t, nn = key[1:]
                    pe.wait_ge(b2_in, 32)
                    mm = pe.matmul(b, tabT[:, 1, t * P:(t + 1) * P], b2s[:, nn * 512:nn * 512 + 512], start=True, stop=True)
                mm.then_inc(late_done, 1)

            def gather(i):
                pe.wait_ge(sg_done, 3 * (i + 1))
                for part, xt in enumerate((xth, xtl)):
                    if part and isinstance(i, int) and i == 0:
                        pe.wait_ge(xl_done, TT)
                    for k in range(KC):
                        for t in range(TT):
                            mm = pe.matmul(banks[6 + part][:, k * SL:(k + 1) * SL], xt[:, t, k * P:(k + 1) * P], SG[:, t, 0:SL],
                                           start=(t == 0), stop=(t == 1))
                    mm.then_inc(ga_pe, 1)

            def products(j, u, first, chunks, lhs, width, out0, last_chunk, use_native):
                slot, uses = raw_at(j, u)
                if use_native:
                    pe.wait_ge(raw_in[slot], uses * 16)
                    parts = [raw[slot][:, :]]
                else:
                    pe.wait_ge(hi_done, split_count(j, u))
                    pe.wait_ge(lo_done, split_count(j, u))
                    parts = [hi[hl_slot(j, u)][:, :], lo[hl_slot(j, u)][:, :]]
                for c in range(chunks):
                    for p, w in enumerate(parts):
                        for n in range(width // 512):
                            mm = pe.matmul(PS[:, out0 + n * 512:out0 + (n + 1) * 512],
                                           lhs(c).bitcast(F32) if use_native else lhs(c),
                                           w[:, c * width + n * 512:c * width + (n + 1) * 512],
                                           start=(first and c == 0 and p == 0),
                                           stop=(last_chunk and c == chunks - 1 and p == len(parts) - 1))
                mm.then_inc(nat_used if use_native else hl_used, 1)

            def up(j, u):
                products(j, u, False, 1, lambda c: XG[:, u, :], FF2, 0, u == W1U - 1, native(j, u))

            def down(j, u, v, out0=2048):
                products(j, u, v == 0, 2, lambda c: AT[:, 2 * v + c, :, :].rearrange("p a s -> p (a s)"), D, out0, v == W2U - 1,
                         native(j, u))

            def scatter_transposes(i):
                pe.wait_ge(ss_mat, 2 * (i + 1))
                for t in range(TT):
                    mm = pe.transpose(banks[7][:, t * P:(t + 1) * P], SS[:, t, :].bitcast(F32), ident)
                return mm

            def scatter(i, q):
                t, n = q // 2, q % 2
                for p, part in enumerate((YH, YL)):
                    mm = pe.matmul(banks[6 + q % 2], ST[:, t * P:(t + 1) * P], part[:, n * 512:(n + 1) * 512], start=(p == 0), stop=(p == 1))
                mm.then_inc(sc_pe, 1)

            def body(j):
                later = not isinstance(j, int)
                pe.wait_ge(xgh, j + 1)
                pe.wait_ge(xgl, j + 1)
                if later or j >= 1:
                    pe.wait_ge(swi, 6 * j - 4)
                for n in range(4):
                    pe.matmul(banks[n], BL[:, :], b1s[:, n * 512:(n + 1) * 512], start=True, stop=False)
                for u in range(W1U):
                    up(j, u)
                    for key in [] if later else LATE_PE.get((j, u), []):
                        late_task(key)
                    if u == 2:
                        if later:
                            scatter_transposes(j - 2)
                        for t in range(TT):
                            mm = pe.matmul(banks[7][:, S:S + 1], SG[:, t, :].bitcast(F32), gi[:, t, bass.ds(j, 1)],
                                           start=(t == 0), stop=(t == 1))
                        mm.then_inc(st_pe, 1)
                    if later and u == 4:
                        pe.wait_ge(atl, j)
                        pe.wait_ge(yh, j - 1)
                        pe.wait_ge(yl, j - 1)
                        pe.wait_ge(st_act, j - 1)
                        scatter(j - 2, 0)
                        pe.wait_ge(slw, j + 1)
                        scatter(j - 2, 1)
                    if later and u == 6:
                        for q in (2, 3):
                            pe.wait_ge(sc_add, 4 * (j - 2) + (q - 1))
                            scatter(j - 2, q)
                if later:
                    pe.wait_ge(sc_add, 4 * (j - 1))
                else:
                    pe.wait_ge(slw, j + 1)
                    if j == 1:
                        pe.wait_ge(atl, j)
                gather(j + 1)
                if not later:
                    for key in LATE_PE.get((j, END), []):
                        late_task(key)
                    if j == 1:
                        for key in LATE[-2:]:
                            late_in_sbuf(pe, key)
                if later or j >= 1:
                    pe.wait_ge(ath, j)
                    pe.wait_ge(atl, j)
                    if later:
                        pe.wait_ge(yl, j - 1)
                    for v in range(W2U):
                        down(j, W1U + v, v)
                pe.wait_ge(swi, 6 * (j + 1))
                pe.wait_ge(xgh, j + 2)
                for c in range(4):
                    mm = pe.transpose(banks[6][:, c * P:(c + 1) * P], act_t[:, c * P:(c + 1) * P], ident)
                mm.then_inc(tr_pe, 1)

            pe.wait_ge(xh_done, TT)
            for n in range(N_TASKS - 4, N_TASKS):
                pe.wait_ge(bank_read[n % 4], n // 4 + 1)
            late_task(("cnt",))
            keep_warm(6)
            gather(0)
            late_task(("off",))
            late_task(("tabT",))
            pe.wait_ge(b1h, 1)
            pe.wait_ge(b1l, 1)
            pe.wait_ge(zeroed, 2)
            body(0)
            body(1)
            n_items = number_of_items(pe)
            with pe.Fori(2, n_items) as j:
                body(j)
            j = n_items
            pe.wait_ge(xgl, j + 1)
            pe.wait_ge(ss_mat, 2 * j)
            for i, matrix in enumerate((SS, SS2)):
                for t in range(TT):
                    mm = pe.transpose(banks[7][:, i * S + t * P:i * S + (t + 1) * P], matrix[:, t, :].bitcast(F32), ident)
            mm.then_inc(st_pe, 1)
            pe.wait_ge(ath, j)
            pe.wait_ge(atl, j)
            for v in range(W2U):
                down(j, v, v, 0)
            pe.wait_ge(yh, j - 1)
            pe.wait_ge(yl, j - 1)
            pe.wait_ge(st_act, j - 1)
            quarters = [(n, t) for n in range(2) for t in range(TT)]
            for i, (n, t) in enumerate(quarters):
                for p, part in enumerate((YH, YL)):
                    pe.matmul(banks[4 + i], STL[:, t * P:(t + 1) * P], part[:, n * 512:(n + 1) * 512], start=(p == 0), stop=False)
            for i, (n, t) in enumerate(quarters):
                pe.wait_ge(yh, j + n)
                pe.wait_ge(yl, j + n)
                for p, part in enumerate((YH2, YL2)):
                    mm = pe.matmul(banks[4 + i], STL[:, S + t * P:S + (t + 1) * P], part[:, n * 512:(n + 1) * 512], start=False, stop=(p == 1))
                mm.then_inc(sc_pe, 1)


NAMES = ["x", "mem", "g_mix", "w_in", "b_gate", "g_ret_out", "g_moba_q", "g_moba_k", "g_mem", "w_mem_kv", "g_mem_q", "g_mem_k",
         "w_br_ret", "w_br_moba", "w_br_mem", "w_out", "g_ffn", "w_router", "b_router", "w_mlp1", "b_mlp1", "w_mlp2", "b_mlp2"]


def kernel(x, mem, g_mix, w_in, b_gate, g_ret_out, g_moba_q, g_moba_k, g_mem, w_mem_kv, g_mem_q, g_mem_k, w_br_ret, w_br_moba,
           w_br_mem, w_out, g_ffn, w_router, b_router, w_mlp1, b_mlp1, w_mlp2, b_mlp2):
    import numpy as np
    import concourse.bacc as bacc
    from concourse.bass_utils import run_bass_kernel_spmd

    given = dict(zip(NAMES, (x, mem, g_mix, w_in, b_gate, g_ret_out, g_moba_q, g_moba_k, g_mem, w_mem_kv, g_mem_q, g_mem_k,
                             w_br_ret, w_br_moba, w_br_mem, w_out, g_ffn, w_router, b_router, w_mlp1, b_mlp1, w_mlp2, b_mlp2)))
    arrays = {n: np.ascontiguousarray(v) for n, v in given.items()}
    cols = [arrays[n][0].reshape(KC, P).T for n in ("g_mix", "g_mem", "g_ffn")]
    cols += [np.tile(arrays[n][0], P // arrays[n].shape[1])[:, None] for n in ("g_moba_q", "g_moba_k", "g_mem_q", "g_mem_k", "g_ret_out")]
    arrays["gains"] = np.ascontiguousarray(np.concatenate(cols, 1))
    for n in ("g_mix", "g_mem", "g_moba_q", "g_moba_k", "g_mem_q", "g_mem_k", "g_ret_out"):
        del arrays[n]
    arrays["decay"], arrays["alibi"], arrays["misc"] = host_constants()
    nc = bacc.Bacc("TRN2", target_bir_lowering=False, num_devices=1)
    aps = {n: nc.dram_tensor(f"in_{n}", v.shape, mybir.dt.from_np(v.dtype), kind="ExternalInput").ap() for n, v in arrays.items()}
    out = nc.dram_tensor("out", (1, S, D), F32, kind="ExternalOutput").ap()
    build(nc, aps, out)
    r = run_bass_kernel_spmd(nc, [{f"in_{n}": v for n, v in arrays.items()}], core_ids=[0])
    return r.results[0]["out"]
```
